# Optimizing a Trainium2 kernel written in Bass

```python
import math
import jax
import jax.numpy as jnp
from jax import lax
import numpy as np

D_MODEL = 1024
BATCH = 1
SEQ = 512
DEPTH = 2
DEC_BATCH = 8
DEC_SEQ = 1
PAST_LEN = 256
PAGE_SIZE = 128

HEAD_DIM = 64
D_PLE = 256
A_HEADS = 8
A_BRANCHES = ((128, 1), (512, 4), (2048, 16))
A_WIN_MAX = max(w for w, _ in A_BRANCHES)
B_HEADS = 4
B_DK = 64
B_DV = 128
B_GATE_RANK = 16
B_GATE_TAU = 16.0
B_CHUNK = 64
C_HEADS = 16
C_KV_HEADS = 4
C_IDX_HEADS = 8
C_IDX_DIM = 64
C_TOPK_MAX = 256
D_FF = ((8 * D_MODEL + 3 * 256 - 1) // (3 * 256)) * 256
N_BUCKETS = 32
REL_MAX_DIST = A_WIN_MAX
BIAS_HEADS = max(A_HEADS, C_HEADS)
Q_BLOCK = 128
NORM_EPS = 1e-6
N_AB = (DEPTH + 1) // 2
N_C = DEPTH // 2
AB_SPLITS = (A_HEADS * HEAD_DIM, A_HEADS * HEAD_DIM, A_HEADS * HEAD_DIM,
             B_HEADS * B_DK, B_HEADS * B_DK, B_HEADS * B_DV, B_GATE_RANK, B_HEADS * B_DV)
C_SPLITS = (C_HEADS * HEAD_DIM, C_KV_HEADS * HEAD_DIM, C_KV_HEADS * HEAD_DIM,
            C_IDX_HEADS * C_IDX_DIM, C_IDX_DIM, C_IDX_HEADS)

kernel_name = 'hybrid_dilated_gla_dsa_decoder_step'

def rmsnorm(x, g):
    xf = x.astype(jnp.float32)
    y = xf * lax.rsqrt(jnp.mean(xf * xf, axis=-1, keepdims=True) + NORM_EPS)
    return (y * g.astype(jnp.float32)).astype(x.dtype)

def split_cols(y, sizes):
    bounds = [int(b) for b in np.cumsum(sizes)[:-1]]
    return jnp.split(y, bounds, axis=-1)

def rel_bucket(dist):
    n = jnp.maximum(dist, 0)
    exact = N_BUCKETS // 2
    nf = jnp.maximum(n, exact).astype(jnp.float32)
    large = exact + (jnp.log(nf / exact) / math.log(REL_MAX_DIST / exact)
                     * (N_BUCKETS - exact)).astype(jnp.int32)
    return jnp.where(n < exact, n, jnp.minimum(large, N_BUCKETS - 1))

def rel_bias_for(rel_bias, dist, n_heads):
    return rel_bias[rel_bucket(dist)][..., :n_heads].astype(jnp.float32)

def take_rows(a, idx):
    return jax.vmap(lambda a_b, i_b: a_b[i_b])(a, idx)

def gathered_attention(q, kg, vg, bias, valid):
    bx, t, h, d = q.shape
    k, n_kv = kg.shape[2], kg.shape[3]
    grp = h // n_kv
    qg = q.reshape(bx, t, n_kv, grp, d)
    s = jnp.einsum('btngd,btknd->btkng', qg, kg).reshape(bx, t, k, h).astype(jnp.float32) + bias
    s = jnp.where(valid[..., None], s, -jnp.inf)
    lse = jax.nn.logsumexp(s, axis=2)
    p = jnp.exp(s - lse[:, :, None, :]).reshape(bx, t, k, n_kv, grp)
    o = jnp.einsum('btkng,btknd->btngd', p.astype(vg.dtype), vg).reshape(bx, t, h, d)
    return o, lse

def combine_branches(outs, lses):
    wts = jax.nn.softmax(jnp.stack(lses, 0), axis=0)
    return jnp.einsum('nbth,nbthd->bthd', wts.astype(outs[0].dtype), jnp.stack(outs, 0))

def branch_offsets(w, d):
    return jnp.arange(w // d + 1, dtype=jnp.int32) * d

def to_blocks(a):
    b, s = a.shape[:2]
    return a.reshape(b, s // Q_BLOCK, Q_BLOCK, *a.shape[2:]).swapaxes(0, 1)

def from_blocks(a):
    nb, b = a.shape[:2]
    return a.swapaxes(0, 1).reshape(b, nb * Q_BLOCK, *a.shape[3:])

def dilated_prompt(q, k, v, rel_bias):
    s_len, h = q.shape[1], q.shape[2]
    starts = jnp.arange(s_len // Q_BLOCK, dtype=jnp.int32) * Q_BLOCK

    def block(args):
        q_blk, t0 = args
        t = t0 + jnp.arange(Q_BLOCK, dtype=jnp.int32)
        outs, lses = [], []
        for w, d in A_BRANCHES:
            offs = branch_offsets(w, d)
            idx = t[:, None] - offs[None, :]
            idc = jnp.maximum(idx, 0)
            o, lse = gathered_attention(q_blk, jnp.take(k, idc, axis=1), jnp.take(v, idc, axis=1),
                                        rel_bias_for(rel_bias, offs, h), (idx >= 0)[None])
            outs.append(o)
            lses.append(lse)
        return combine_branches(outs, lses)

    return from_blocks(lax.map(block, (to_blocks(q), starts)))

def dilated_sample(q, k_new, v_new, k_buf, v_buf, rel_bias):
    t_len, h = q.shape[1], q.shape[2]
    wb = k_buf.shape[1]
    j = jnp.arange(t_len, dtype=jnp.int32)
    outs, lses = [], []
    for w, d in A_BRANCHES:
        offs = branch_offsets(w, d)
        idx = wb + j[:, None] - offs[None, :]
        in_buf = (idx < wb)[None, :, :, None, None]
        ib = jnp.clip(idx, 0, wb - 1)
        inew = jnp.clip(idx - wb, 0, t_len - 1)
        kg = jnp.where(in_buf, jnp.take(k_buf, ib, axis=1), jnp.take(k_new, inew, axis=1))
        vg = jnp.where(in_buf, jnp.take(v_buf, ib, axis=1), jnp.take(v_new, inew, axis=1))
        o, lse = gathered_attention(q, kg, vg, rel_bias_for(rel_bias, offs, h), (idx >= 0)[None])
        outs.append(o)
        lses.append(lse)
    return combine_branches(outs, lses)

def gla_chunked(q, k, v, g):
    b, s_len, h, dk = q.shape
    dv = v.shape[-1]
    nc = s_len // B_CHUNK
    causal = jnp.tril(jnp.ones((B_CHUNK, B_CHUNK), dtype=bool))

    def to_chunks(a):
        return a.reshape(b, nc, B_CHUNK, h, a.shape[-1]).transpose(1, 0, 3, 2, 4)

    def step(st, inp):
        qc, kc, vc, gc = inp
        cum = jnp.cumsum(gc.astype(jnp.float32), axis=2)
        o_inter = jnp.einsum('bhcd,bhde->bhce', qc * jnp.exp(cum).astype(qc.dtype), st)
        diff = cum[:, :, :, None, :] - cum[:, :, None, :, :]
        decay = jnp.exp(jnp.where(causal[None, None, :, :, None], diff, -jnp.inf))
        att = jnp.einsum('bhtd,bhsd,bhtsd->bhts', qc, kc, decay)
        o = o_inter + jnp.einsum('bhts,bhse->bhte', att, vc)
        last = cum[:, :, -1:, :]
        st_new = (jnp.exp(last[:, :, 0, :])[..., None] * st
                  + jnp.einsum('bhsd,bhse->bhde', kc * jnp.exp(last - cum), vc))
        return st_new, o

    s0 = jnp.zeros((b, h, dk, dv), jnp.float32)
    s_fin, o = lax.scan(step, s0, (to_chunks(q), to_chunks(k), to_chunks(v), to_chunks(g)))
    o = o.transpose(1, 0, 3, 2, 4).reshape(b, s_len, h, dv)
    return o.astype(v.dtype), s_fin

def gla_recurrent(q, k, v, g, s0):
    def step(st, inp):
        qt, kt, vt, gt = inp
        st = jnp.exp(gt.astype(jnp.float32))[..., None] * st + jnp.einsum('bhd,bhe->bhde', kt, vt)
        return st, jnp.einsum('bhd,bhde->bhe', qt, st)

    xs = tuple(a.transpose(1, 0, 2, 3) for a in (q, k, v, g))
    s_fin, o = lax.scan(step, s0.astype(jnp.float32), xs)
    return o.transpose(1, 0, 2, 3).astype(v.dtype), s_fin

def index_scores(iq, iw, ik):
    s = jnp.einsum('bthd,bsd->btsh', iq, ik).astype(jnp.float32)
    return jnp.einsum('btsh,bth->bts', jax.nn.relu(s), iw.astype(jnp.float32))

def dsa_prompt(q, k, v, iq, ik, iw, rel_bias):
    s_len, h = q.shape[1], q.shape[2]
    topk = min(C_TOPK_MAX, s_len // 4)
    key_pos = jnp.arange(s_len, dtype=jnp.int32)
    starts = jnp.arange(s_len // Q_BLOCK, dtype=jnp.int32) * Q_BLOCK

    def block(args):
        q_blk, iq_blk, iw_blk, t0 = args
        t = t0 + jnp.arange(Q_BLOCK, dtype=jnp.int32)
        score = index_scores(iq_blk, iw_blk, ik)
        score = jnp.where((key_pos[None, :] <= t[:, None])[None], score, -jnp.inf)
        _, idx = lax.top_k(score, topk)
        dist = t[None, :, None] - idx
        o, _ = gathered_attention(q_blk, take_rows(k, idx), take_rows(v, idx),
                                  rel_bias_for(rel_bias, dist, h), dist >= 0)
        return o

    return from_blocks(lax.map(block, (to_blocks(q), to_blocks(iq), to_blocks(iw), starts)))

def dsa_sample(q, k_new, v_new, iq, ik_new, iw, pool_k, pool_v, pool_ik, page_table, rel_bias):
    bx, t_len, h = q.shape[0], q.shape[1], q.shape[2]
    past = page_table.shape[1] * PAGE_SIZE
    n_keys = past + t_len
    topk = min(C_TOPK_MAX, n_keys // 4)
    ik_all = jnp.concatenate([pool_ik[page_table].reshape(bx, past, C_IDX_DIM), ik_new], axis=1)
    t = past + jnp.arange(t_len, dtype=jnp.int32)
    score = index_scores(iq, iw, ik_all)
    score = jnp.where((jnp.arange(n_keys, dtype=jnp.int32)[None, :] <= t[:, None])[None], score, -jnp.inf)
    _, idx = lax.top_k(score, topk)
    pidx = jnp.minimum(idx, past - 1)
    phys = take_rows(page_table, pidx // PAGE_SIZE)
    off = pidx % PAGE_SIZE
    nidx = jnp.clip(idx - past, 0, t_len - 1)
    in_past = (idx < past)[..., None, None]
    kg = jnp.where(in_past, pool_k[phys, off], take_rows(k_new, nidx))
    vg = jnp.where(in_past, pool_v[phys, off], take_rows(v_new, nidx))
    dist = t[None, :, None] - idx
    o, _ = gathered_attention(q, kg, vg, rel_bias_for(rel_bias, dist, h), dist >= 0)
    return o

def ab_inputs(hn, li, prm):
    lead = hn.shape[:-1]
    y = hn @ prm['w_in_ab'][li]
    aq, ak, av, bq, bk, bv, blr, bog = split_cols(y, AB_SPLITS)
    aq = rmsnorm(aq.reshape(*lead, A_HEADS, HEAD_DIM), prm['a_q_norm'][li]) * (HEAD_DIM ** -0.5)
    ak = rmsnorm(ak.reshape(*lead, A_HEADS, HEAD_DIM), prm['a_k_norm'][li])
    av = av.reshape(*lead, A_HEADS, HEAD_DIM)
    bq = bq.reshape(*lead, B_HEADS, B_DK) * (B_DK ** -0.5)
    bk = bk.reshape(*lead, B_HEADS, B_DK)
    bv = bv.reshape(*lead, B_HEADS, B_DV)
    z = (blr @ prm['b_gate_w2'][li] + prm['b_gate_b'][li]).astype(jnp.float32)
    bg = (jax.nn.log_sigmoid(z) / B_GATE_TAU).reshape(*lead, B_HEADS, B_DK)
    return aq, ak, av, bq, bk, bv, bg, bog

def ab_output(oa, ob, bog, li, prm):
    lead = oa.shape[:-2]
    gate = jax.nn.silu(bog).reshape(*lead, B_HEADS, B_DV)
    ob = rmsnorm(ob, prm['b_out_norm'][li]) * gate
    o = jnp.concatenate([oa.reshape(*lead, A_HEADS * HEAD_DIM), ob.reshape(*lead, B_HEADS * B_DV)], axis=-1)
    return o @ prm['w_out_ab'][li]

def c_inputs(hn, li, prm):
    lead = hn.shape[:-1]
    y = hn @ prm['w_in_c'][li]
    cq, ck, cv, iq, ik, iw = split_cols(y, C_SPLITS)
    cq = rmsnorm(cq.reshape(*lead, C_HEADS, HEAD_DIM), prm['c_q_norm'][li]) * (HEAD_DIM ** -0.5)
    ck = rmsnorm(ck.reshape(*lead, C_KV_HEADS, HEAD_DIM), prm['c_k_norm'][li])
    cv = cv.reshape(*lead, C_KV_HEADS, HEAD_DIM)
    iq = iq.reshape(*lead, C_IDX_HEADS, C_IDX_DIM)
    ik = rmsnorm(ik, prm['c_ik_norm'][li])
    iw = iw * ((C_IDX_HEADS ** -0.5) * (C_IDX_DIM ** -0.5))
    return cq, ck, cv, iq, ik, iw

def c_output(oc, li, prm):
    lead = oc.shape[:-2]
    return oc.reshape(*lead, C_HEADS * HEAD_DIM) @ prm['w_out_c'][li]

def ffn_ple(x, p_l, l, prm):
    hn = rmsnorm(x, prm['g_ffn'][l])
    x = x + (jax.nn.silu(hn @ prm['w_ff1'][l]) * (hn @ prm['w_ff3'][l])) @ prm['w_ff2'][l]
    u = rmsnorm(x, prm['g_ple'][l])
    return x + jax.nn.sigmoid(u @ prm['w_ple_gate'][l]) * (p_l @ prm['w_ple_proj'][l])

def prompt_forward(x, p, prm):
    s_len = x.shape[1]
    wp = min(A_WIN_MAX, s_len)
    a_k, a_v, b_s, c_k, c_v, c_ik = [], [], [], [], [], []
    for l in range(DEPTH):
        hn = rmsnorm(x, prm['g_mix'][l])
        li = l // 2
        if l % 2 == 0:
            aq, ak, av, bq, bk, bv, bg, bog = ab_inputs(hn, li, prm)
            oa = dilated_prompt(aq, ak, av, prm['rel_bias'])
            ob, s_fin = gla_chunked(bq, bk, bv, bg)
            x = x + ab_output(oa, ob, bog, li, prm)
            a_k.append(ak[:, s_len - wp:])
            a_v.append(av[:, s_len - wp:])
            b_s.append(s_fin)
        else:
            cq, ck, cv, iq, ik, iw = c_inputs(hn, li, prm)
            oc = dsa_prompt(cq, ck, cv, iq, ik, iw, prm['rel_bias'])
            x = x + c_output(oc, li, prm)
            c_k.append(ck)
            c_v.append(cv)
            c_ik.append(ik)
        x = ffn_ple(x, p[l], l, prm)
    return x, jnp.stack(a_k), jnp.stack(a_v), jnp.stack(b_s), jnp.stack(c_k), jnp.stack(c_v), jnp.stack(c_ik)

def sample_forward(x, p, cache_a_k, cache_a_v, state_b, cache_c_k, cache_c_v, cache_c_ik, page_table, prm):
    a_k, a_v, b_s, c_k, c_v, c_ik = [], [], [], [], [], []
    for l in range(DEPTH):
        hn = rmsnorm(x, prm['g_mix'][l])
        li = l // 2
        if l % 2 == 0:
            aq, ak, av, bq, bk, bv, bg, bog = ab_inputs(hn, li, prm)
            oa = dilated_sample(aq, ak, av, cache_a_k[li], cache_a_v[li], prm['rel_bias'])
            ob, s_fin = gla_recurrent(bq, bk, bv, bg, state_b[li])
            x = x + ab_output(oa, ob, bog, li, prm)
            a_k.append(ak)
            a_v.append(av)
            b_s.append(s_fin)
        else:
            cq, ck, cv, iq, ik, iw = c_inputs(hn, li, prm)
            oc = dsa_sample(cq, ck, cv, iq, ik, iw, cache_c_k[li], cache_c_v[li], cache_c_ik[li],
                            page_table, prm['rel_bias'])
            x = x + c_output(oc, li, prm)
            c_k.append(ck)
            c_v.append(cv)
            c_ik.append(ik)
        x = ffn_ple(x, p[l], l, prm)
    return x, jnp.stack(a_k), jnp.stack(a_v), jnp.stack(b_s), jnp.stack(c_k), jnp.stack(c_v), jnp.stack(c_ik)

def setup_inputs(seed: int = 0) -> dict:
    key = jax.random.key(seed)
    ks = jax.random.split(key, 32)

    def nrm(i, shape, scale=1.0):
        return jax.random.normal(ks[i], shape, jnp.float32) * scale

    def gain(i, shape):
        return 1.0 + nrm(i, shape, 0.05)

    n_pages = PAST_LEN // PAGE_SIZE
    n_used = DEC_BATCH * n_pages
    n_pool = n_used + n_used // 4
    wb = min(A_WIN_MAX, PAST_LEN)
    page_table = jax.random.permutation(ks[8], n_pool)[:n_used].reshape(DEC_BATCH, n_pages).astype(jnp.int32)
    d_ab_in = sum(AB_SPLITS)
    d_c_in = sum(C_SPLITS)
    d_ab_out = A_HEADS * HEAD_DIM + B_HEADS * B_DV
    d_c_out = C_HEADS * HEAD_DIM
    return {
        'x_prompt': nrm(0, (BATCH, SEQ, D_MODEL)),
        'x_sample': nrm(1, (DEC_BATCH, DEC_SEQ, D_MODEL)),
        'cache_a_k': nrm(2, (N_AB, DEC_BATCH, wb, A_HEADS, HEAD_DIM)),
        'cache_a_v': nrm(3, (N_AB, DEC_BATCH, wb, A_HEADS, HEAD_DIM)),
        'state_b': nrm(4, (N_AB, DEC_BATCH, B_HEADS, B_DK, B_DV)),
        'cache_c_k': nrm(5, (N_C, n_pool, PAGE_SIZE, C_KV_HEADS, HEAD_DIM)),
        'cache_c_v': nrm(6, (N_C, n_pool, PAGE_SIZE, C_KV_HEADS, HEAD_DIM)),
        'cache_c_ik': nrm(7, (N_C, n_pool, PAGE_SIZE, C_IDX_DIM)),
        'page_table': page_table,
        'p_prompt': nrm(9, (DEPTH, BATCH, SEQ, D_PLE)),
        'p_sample': nrm(10, (DEPTH, DEC_BATCH, DEC_SEQ, D_PLE)),
        'rel_bias': nrm(11, (N_BUCKETS, BIAS_HEADS), 0.5),
        'g_mix': gain(12, (DEPTH, D_MODEL)),
        'w_in_ab': nrm(13, (N_AB, D_MODEL, d_ab_in), D_MODEL ** -0.5),
        'a_q_norm': gain(14, (N_AB, HEAD_DIM)),
        'a_k_norm': gain(15, (N_AB, HEAD_DIM)),
        'b_gate_w2': nrm(16, (N_AB, B_GATE_RANK, B_HEADS * B_DK), B_GATE_RANK ** -0.5),
        'b_gate_b': nrm(17, (N_AB, B_HEADS * B_DK), 0.1),
        'b_out_norm': gain(18, (N_AB, B_DV)),
        'w_out_ab': nrm(19, (N_AB, d_ab_out, D_MODEL), d_ab_out ** -0.5),
        'w_in_c': nrm(20, (N_C, D_MODEL, d_c_in), D_MODEL ** -0.5),
        'c_q_norm': gain(21, (N_C, HEAD_DIM)),
        'c_k_norm': gain(22, (N_C, HEAD_DIM)),
        'c_ik_norm': gain(23, (N_C, C_IDX_DIM)),
        'w_out_c': nrm(24, (N_C, d_c_out, D_MODEL), d_c_out ** -0.5),
        'g_ffn': gain(25, (DEPTH, D_MODEL)),
        'w_ff1': nrm(26, (DEPTH, D_MODEL, D_FF), D_MODEL ** -0.5),
        'w_ff3': nrm(27, (DEPTH, D_MODEL, D_FF), D_MODEL ** -0.5),
        'w_ff2': nrm(28, (DEPTH, D_FF, D_MODEL), D_FF ** -0.5),
        'g_ple': gain(29, (DEPTH, D_MODEL)),
        'w_ple_gate': nrm(30, (DEPTH, D_MODEL, D_MODEL), D_MODEL ** -0.5),
        'w_ple_proj': nrm(31, (DEPTH, D_PLE, D_MODEL), D_PLE ** -0.5),
    }

def reference(x_prompt, x_sample, cache_a_k, cache_a_v, state_b, cache_c_k, cache_c_v, cache_c_ik,
              page_table, p_prompt, p_sample, rel_bias, g_mix, w_in_ab, a_q_norm, a_k_norm,
              b_gate_w2, b_gate_b, b_out_norm, w_out_ab, w_in_c, c_q_norm, c_k_norm, c_ik_norm,
              w_out_c, g_ffn, w_ff1, w_ff3, w_ff2, g_ple, w_ple_gate, w_ple_proj):
    prm = dict(rel_bias=rel_bias, g_mix=g_mix, w_in_ab=w_in_ab, a_q_norm=a_q_norm, a_k_norm=a_k_norm,
               b_gate_w2=b_gate_w2, b_gate_b=b_gate_b, b_out_norm=b_out_norm, w_out_ab=w_out_ab,
               w_in_c=w_in_c, c_q_norm=c_q_norm, c_k_norm=c_k_norm, c_ik_norm=c_ik_norm,
               w_out_c=w_out_c, g_ffn=g_ffn, w_ff1=w_ff1, w_ff3=w_ff3, w_ff2=w_ff2,
               g_ple=g_ple, w_ple_gate=w_ple_gate, w_ple_proj=w_ple_proj)
    y_prompt, pa_k, pa_v, pb_s, pc_k, pc_v, pc_ik = prompt_forward(x_prompt, p_prompt, prm)
    y_sample, sa_k, sa_v, sb_s, sc_k, sc_v, sc_ik = sample_forward(
        x_sample, p_sample, cache_a_k, cache_a_v, state_b, cache_c_k, cache_c_v, cache_c_ik, page_table, prm)
    return (y_prompt, y_sample, pa_k, pa_v, pb_s, pc_k, pc_v, pc_ik, sa_k, sa_v, sb_s, sc_k, sc_v, sc_ik)


_drawn_inputs = setup_inputs


def setup_inputs(seed=0):
    import zlib

    import numpy as np

    out = dict(_drawn_inputs(seed))
    spreads = {}
    factors = {'a_q_norm': 5.358, 'c_q_norm': 8.0, 'g_ple': 3.402}
    for name, (base, spread) in spreads.items():
        noise = np.random.default_rng([zlib.crc32(name.encode()), seed]).standard_normal(out[name].shape)
        drawn = base * np.exp(spread * noise) if base else spread * noise
        out[name] = jnp.asarray(drawn.astype(out[name].dtype))
    for name, factor in factors.items():
        out[name] = (out[name] * factor).astype(out[name].dtype)
    return out
```

```python
import math
from contextlib import ExitStack

import numpy as np
import concourse.bass as bass
from concourse import mybir
from concourse.alu_op_type import AluOpType as ALU

F32 = mybir.dt.float32
F32R = mybir.dt.float32r
I32 = mybir.dt.int32
ACT = mybir.ActivationFunctionType
AX = mybir.AxisListType

P = 128
DM, KC = 1024, 8
SEQ, NS = 512, 8
NT = SEQ + NS
HALF = NT // 2
DFF, FC = 2816, 22
DPLE = 256
HD = 64
NB = 32
PAST = 256
NK = PAST + 1
QB = SEQ // P
NEG = -1.0e30
GONE = -3.0e38
EPS = 1e-6
GC = 64
NCH = SEQ // GC
TOPK_P, TOPK_S = 128, 64
RW = 640

AB_BLOCKS = 25
C_BLOCKS = 18
B_AB = 0
B_OUT0 = B_AB + AB_BLOCKS
B_FF0 = B_OUT0 + KC
B_D0 = B_FF0 + 2 * FC
B_PR0 = B_D0 + 3 * KC
B_G0 = B_PR0 + 2
B_C = B_G0 + KC
B_OUT1 = B_C + C_BLOCKS
B_FF1 = B_OUT1 + KC
B_D1 = B_FF1 + 2 * FC
B_PR1 = B_D1 + 3 * KC
B_G1 = B_PR1 + 2
N_BLOCKS = B_G1 + KC

V_MIX, V_FFN, V_PLE, V_NG = 0, 16, 32, 48
N_NG = 19
V_BO, V_GB, V_EPS, V_ONE = 67, 68, 70, 71
NV = 72
K_ID, K_O2, K_ON, K_CA, K_FR, K_TR, K_RS = 0, 128, 256, 384, 896, 1408, 1472
NKC = 1480

R_A, R_C, R_SA, R_SC = 0, 8, 24, 88
O_A, O_C, O_SA, O_SC = 0, RW, 2 * RW, 2 * RW + NK
N_ONE = 2 * RW + 2 * NK


def build(nc, a):
    ctx = ExitStack()

    def sb(name, shape, dt=F32, scope=None):
        return (scope or ctx).enter_context(nc.sbuf_tensor(name, shape, dt))

    sems = {}

    def S(name):
        if name not in sems:
            sems[name] = ctx.enter_context(nc.semaphore(name))
        return sems[name]

    with ctx:
        x = sb("x", [P, KC, NT])
        act_hi = sb("act_hi", [P, KC, NT], F32R)
        act_lo = sb("act_lo", [P, KC, NT], F32R)
        w_raw = sb("w_raw", [P, 2, DM])
        w_hi = sb("w_hi", [P, 2, DM], F32R)
        w_lo = sb("w_lo", [P, 2, DM], F32R)
        vecs = sb("vecs", [P, NV])
        const = sb("const", [P, NKC])
        ident = const[:, K_ID:K_ID + P]
        ones2 = const[:, K_O2:K_O2 + P]
        ones = const[:, K_ON:K_ON + P]
        causal = const[:, K_CA:K_CA + SEQ]
        fresh = const[:, K_FR:K_FR + SEQ]
        tri = const[0:GC, K_TR:K_TR + GC]
        rowsel = const[:, K_RS:K_RS + NS]
        colsel = sb("colsel", [NS, P])
        sqsum = sb("sqsum", [P, NT])
        sq = sb("sq", [P, 2, NT])
        rs = sb("rs", [P, 2, NT])
        tmp = sb("tmp", [P, 2, NT])
        gains = sb("gains", [P, N_NG])

        sA = ExitStack()
        yA = sb("yA", [P, AB_BLOCKS - 1, NT], scope=sA)
        blr = sb("blr", [16, NT], scope=sA)
        gs = sb("gs", [P, 2, NS], scope=sA)
        gw2 = sb("gw2", [16, 256], scope=sA)
        sA0 = ExitStack()
        orow = sb("orow", [33, N_ONE], scope=sA0)
        brow = sb("brow", [33, 216], scope=sA0)
        rrow = sb("rrow", [16, 2, RW], scope=sA0)
        sA0.close()
        sA1 = ExitStack()
        vtokA = sb("vtokA", [P, QB, 512], scope=sA1)
        biasA = sb("biasA", [P, 2, 2, SEQ], scope=sA1)
        qstA = sb("qstA", [P, 2, SEQ], scope=sA1)
        kstA = sb("kstA", [P, 2, SEQ], scope=sA1)
        vstA = sb("vstA", [P, 2, QB, P], scope=sA1)
        xA = sb("xA", [P, 2, SEQ], scope=sA1)
        pA = sb("pA", [P, 2, SEQ], scope=sA1)
        ptA = sb("ptA", [P, 2, SEQ], scope=sA1)
        statA = sb("statA", [P, 2, 4], scope=sA1)
        sA1.close()
        sA2 = ExitStack()
        qzA = sb("qzA", [P, 32, 64], scope=sA2)
        kcA = sb("kcA", [P, 2, 4, NK], scope=sA2)
        vcA = sb("vcA", [P, 2, 2, 512], scope=sA2)
        psA = sb("psA", [64, NK], scope=sA2)
        ptsA = sb("ptsA", [P, 2, 64], scope=sA2)
        sstA = sb("sstA", [64, 4], scope=sA2)
        pdA = sb("pdA", [64, 64], scope=sA2)
        pnA = sb("pnA", [NS, 64], scope=sA2)
        vnA = sb("vnA", [NS, 512], scope=sA2)
        osA = sb("osA", [P, 4, NS], scope=sA2)
        owA = sb("owA", [P, 4, 2, NS], scope=sA2)
        sbA = sb("sbA", [33, 64 + NK], scope=sA2)
        sA2.close()
        sA3 = ExitStack()
        zt = sb("zt", [P, 2, NT], scope=sA3)
        zn = sb("zn", [P, 2, NT], scope=sA3)
        cum = sb("cum", [P, 2, SEQ], scope=sA3)
        decay = sb("decay", [P, 2, 2, NCH], scope=sA3)
        kbt = sb("kbt", [GC, 2, NCH, P], scope=sA3)
        vb = sb("vb", [GC, NCH, 4, P], scope=sA3)
        att = sb("att", [GC, 2, SEQ], scope=sA3)
        st = sb("st", [P, 2, P], scope=sA3)
        stm = sb("stm", [P, 2, NCH, P], scope=sA3)
        upd = sb("upd", [P, 2, P], scope=sA3)
        sA3.close()
        sA4 = ExitStack()
        eg = sb("eg", [P, 2, NS], scope=sA4)
        kt8 = sb("kt8", [NS, 256], scope=sA4)
        vt8 = sb("vt8", [NS, 512], scope=sA4)
        kz8 = sb("kz8", [NS, NS, 256], scope=sA4)
        s0 = sb("s0", [P, NS, 2, P], scope=sA4)
        qz8 = sb("qz8", [P, 2, NS, 2], scope=sA4)
        sA4.close()
        sA.close()

        sC = ExitStack()
        yC = sb("yC", [P, C_BLOCKS, NT], scope=sC)
        vtokC = sb("vtokC", [P, QB, 256], scope=sC)
        iwt = sb("iwt", [P, QB, NS], scope=sC)
        score = sb("score", [P, QB, SEQ], scope=sC)
        biasC = sb("biasC", [P, 2, 2, SEQ], scope=sC)
        bmC = sb("bmC", [P, 2, SEQ], scope=sC)
        qstC = sb("qstC", [P, 2, SEQ], scope=sC)
        xC = sb("xC", [P, 2, SEQ], scope=sC)
        pC = sb("pC", [P, 2, SEQ], scope=sC)
        ptC = sb("ptC", [P, 2, SEQ], scope=sC)
        statC = sb("statC", [P, 2, 4], scope=sC)
        ptab = sb("ptab", [1, 16], I32, scope=sC)
        ikc = sb("ikc", [P, NS, NK], scope=sC)
        iqz = sb("iqz", [P, NS, NS], scope=sC)
        iwz = sb("iwz", [NS, NS, NS], scope=sC)
        rel8 = sb("rel8", [NS, 2, NK], scope=sC)
        sc8 = sb("sc8", [NS, NK], scope=sC)
        wk8 = sb("wk8", [NS, NK], scope=sC)
        mx8 = sb("mx8", [NS, 8], scope=sC)
        qzC = sb("qzC", [P, 16, P], scope=sC)
        kcC = sb("kcC", [P, 2, 2, NK], scope=sC)
        vcC = sb("vcC", [P, 2, 2, 256], scope=sC)
        sbC = sb("sbC", [33, P + NK], scope=sC)
        sC0 = ExitStack()
        work = sb("work", [P, SEQ], scope=sC0)
        top8 = sb("top8", [P, 8], scope=sC0)
        reluC = sb("reluC", [P, 2, SEQ], scope=sC0)
        sC0.close()
        psC = sb("psC", [P, NK], scope=sC)
        ptsC = sb("ptsC", [P, 2, P], scope=sC)
        sstC = sb("sstC", [P, 4], scope=sC)
        pdC = sb("pdC", [P, P], scope=sC)
        pnC = sb("pnC", [NS, P], scope=sC)
        vnC = sb("vnC", [NS, 256], scope=sC)
        osC = sb("osC", [P, 8, NS], scope=sC)
        owC = sb("owC", [P, 8, NS], scope=sC)
        sC.close()

        sP = ExitStack()
        pp = sb("pp", [P, KC, NT], scope=sP)
        sP.close()
        h_hi = sb("h_hi", [P, FC, NT], F32R)
        h_lo = sb("h_lo", [P, FC, NT], F32R)
        p_raw = sb("p_raw", [P, 2, NT])
        p_hi = sb("p_hi", [P, 2, NT], F32R)
        p_lo = sb("p_lo", [P, 2, NT], F32R)
        PS = ctx.enter_context(nc.psum_tensor("PS", [P, 8, 512], F32))

        def halves(t):
            return t.rearrange("p (h n) -> p h n", h=2)

        def slot(s):
            return PS[:, 2 * s:2 * s + 2, 0:HALF]

        UNITS = [(pl, par, qb) for pl in range(2) for par in range(2) for qb in range(QB)]
        NU = len(UNITS)
        LAYERS = (
            dict(out=B_OUT0, ff=B_FF0, down=B_D0, proj=B_PR0, gate=B_G0),
            dict(out=B_OUT1, ff=B_FF1, down=B_D1, proj=B_PR1, gate=B_G1),
        )
        FREE_V = 8 + 2 * FC + 8 + 8 + 8

        IN = (
            dict(b0=B_AB, y=yA, n=AB_BLOCKS, normed=((0, 8, 0),),
                 order=((0,), (1, 7), (7,), (8,), (9, 23), (23,), (24,))),
            dict(b0=B_C, y=yC, n=C_BLOCKS, normed=((4, 5, 8), (6, 8, 9), (10, 18, 11)),
                 order=((0, 4), (4,), (5,), (6,), (7,), (8,), (9,), (10,), (11, 17), (17,))),
        )

        def walk(eng, l, body, midway=None):
            for part in IN[l]["order"]:
                if l == 1 and part[0] == 10 and midway:
                    midway()
                if len(part) == 1:
                    body(part[0], part[0])
                else:
                    with eng.Fori(part[0], part[1] - 1, 2) as j:
                        for u in range(2):
                            body(j + u, part[0] + u)

        def normed(l, n, like):
            for first, past, q in IN[l]["normed"]:
                if first <= like < past:
                    return n + (q - first)
            return None

        block = ctx.enter_context(nc.Block())

        @block.sync
        def _(sp):
            sp.dma_start(x[:], a["xT"]).then_inc(S("x_in"), 16)
            sp.dma_start(const[:], a["consts"]).then_inc(S("tables_in"), 16)
            sp.dma_start(vecs[:], a["vecs"]).then_inc(S("tables_in"), 16)
            sp.dma_start(colsel[:], a["colsel"]).then_inc(S("tables_in"), 16)
            sp.dma_start(gw2[:], a["gate_w2"]).then_inc(S("tables_in"), 16)
            sp.dma_start(brow[:], a["bias_rows"]).then_inc(S("tables_in"), 16)
            sp.dma_start(orow[:], a["onehots"]).then_inc(S("tables_in"), 16)
            for b in range(2):
                sp.dma_start(w_raw[:, b, :], a["w"][b]).then_inc(S(f"w_raw{b}"), 16)

            def weights(b0, b1):
                def one(b, s):
                    sp.wait_ge(S("w_lo"), b - 1)
                    sp.dma_start(w_raw[:, s, :], a["w"][b]).then_inc(S(f"w_raw{s}"), 16)
                n = (b1 - b0) // 2
                with sp.Fori(0, n) as j:
                    for u in range(2):
                        one(j * 2 + (b0 + u), (b0 + u) % 2)
                if 2 * n < b1 - b0:
                    one(b1 - 1, (b1 - 1) % 2)

            def pair_biases(pair0, pairs, dst, rows):
                for p in range(pairs):
                    sp.wait_ge(S("t_o"), pair0 + p + 1)
                    for par in range(2):
                        h = rows(p, par)
                        src = bass.AP(tensor=a["rows"].tensor, offset=2 * h * RW + P - 1,
                                      ap=[[RW - P // 2, 2], [-1, P // 2], [1, SEQ]])
                        sp.dma_start(dst[:, p % 2, par, :], src).then_inc(S(f"bias{p % 2}"), 16)

            weights(2, 8)
            sp.wait_ge(S("rrow_ok"), 4)
            for copy in range(2):
                sp.dma_start(a["rows"][0:8, copy, :], rrow[0:8, 0, :]).then_inc(S("rows_out"), 16)
                sp.dma_start(a["rows"][8:24, copy, :], rrow[0:16, 1, :]).then_inc(S("rows_out"), 16)
            weights(8, B_OUT0 + 1)
            sp.wait_ge(S("rows_out"), 64)
            pair_biases(0, 4, biasA, lambda p, par: 2 * p + par)
            weights(B_OUT0 + 1, B_OUT1 + 1)
            pair_biases(4, 8, biasC, lambda p, par: 8 + 4 * (2 * (p // 4) + par) + p % 4)
            weights(B_OUT1 + 1, N_BLOCKS + 1)
            for m in range(KC):
                sp.wait_ge(S("x_new"), KC + m + 1)
                sp.dma_start(a["y"][:, m, :], x[:, m, :]).then_inc(S("y_out"), 16)
            sp.wait_ge(S("y_out"), 16 * KC)

        @block.gpsimd
        def _(pool):
            def low(b, s):
                pool.wait_ge(S("w_hi"), b + 1)
                pool.tensor_tensor(w_lo[:, s, :], w_raw[:, s, :], w_hi[:, s, :].bitcast(F32),
                                   ALU.subtract).then_inc(S("w_lo"), 1)

            def blocks(b0, n):
                with pool.Fori(0, n - 1, 2) as j:
                    for u in range(2):
                        low(j + (b0 + u + 1), (b0 + u + 1) % 2)

            def norm_mul(l, q, s, n):
                y = IN[l]["y"]
                pool.wait_ge(S("hn_rs"), q + 1)
                pool.tensor_tensor(y[:, bass.ds(n, 1), :], y[:, bass.ds(n, 1), :], rs[:, s:s + 1, :],
                                   ALU.mult).then_inc(S("hn_ok"), 1)

            def products_in(l):
                b0 = IN[l]["b0"]

                def body(n, like):
                    low(n + (b0 + 1), (b0 + like + 1) % 2)
                    q = normed(l, n - 1, like - 1)
                    if q is not None:
                        norm_mul(l, q, normed(l, like - 1, like - 1) % 2, n - 1)
                walk(pool, l, body)
                last = IN[l]["n"] - 1
                q = normed(l, last, last)
                if q is not None:
                    norm_mul(l, q, q % 2, last)

            def norm_lo(k):
                for c in range(KC):
                    pool.wait_ge(S("n_hi"), KC * k + c + 1)
                    pool.tensor_tensor(act_lo[:, c, :], tmp[:, c % 2, :], act_hi[:, c, :].bitcast(F32),
                                       ALU.subtract).then_inc(S("n_lo"), 1)

            def ffn(l):
                L = LAYERS[l]
                blocks(L["out"], KC)
                norm_lo(3 * l + 1)
                pool.wait_ge(S("p_hi"), l + 1)
                pool.tensor_tensor(p_lo[:], p_raw[:], p_hi[:].bitcast(F32), ALU.subtract).then_inc(S("p_lo"), 1)
                with pool.Fori(0, FC) as f:
                    for u in range(2):
                        low(f * 2 + (L["ff"] + u + 1), (L["ff"] + u + 1) % 2)
                    pool.wait_ge(S("h_hi"), f + (FC * l + 1))
                    pool.tensor_tensor(h_lo[:, bass.ds(f, 1), :], tmp[:, 0:1, :],
                                       h_hi[:, bass.ds(f, 1), :].bitcast(F32), ALU.subtract).then_inc(S("h_lo"), 1)
                blocks(L["down"], 3 * KC)
                norm_lo(3 * l + 2)
                blocks(L["proj"], 2)
                blocks(L["gate"], KC)

            pool.sem_inc(S("hn_ok"), 2)
            low(0, 0)
            norm_lo(0)
            products_in(0)
            pool.wait_ge(S("A_v"), 4)
            with pool.Fori(0, 2) as it:
                for pl in range(2):
                    pair = it * 2 + pl
                    pool.wait_ge(S("t_o"), pair + 1)
                    pool.tensor_copy(qstA[:, pl:pl + 1, :],
                                     yA[:, bass.ds(pair, 1), 0:SEQ]).then_inc(S("A_st"), 1)
                    pool.tensor_copy(kstA[:, pl:pl + 1, :],
                                     yA[:, bass.ds(pair + 4, 1), 0:SEQ]).then_inc(S("A_st"), 1)
                    pool.tensor_copy(vstA[:, pl, :, :], vtokA[:, :, bass.ds(pair * P, P)]).then_inc(S("A_st"), 1)
            ffn(0)
            norm_lo(3)
            products_in(1)
            for T in range(2):
                with pool.Fori(0, 2) as it:
                    for pl in range(2):
                        pair = it * 2 + (4 * T + pl)
                        pool.wait_ge(S("t_o"), pair + 5)
                        pool.tensor_copy(qstC[:, pl:pl + 1, :],
                                         yC[:, bass.ds(pair + 10, 1), 0:SEQ]).then_inc(S("C_st"), 1)
                    for i, (pl, par, qb) in enumerate(UNITS):
                        if par == 0 and qb == 0:
                            pool.wait_ge(S(f"bias{pl}"), it * 32 + (64 * (T + 1) + 32))
                        if T == 0 and i == 0:
                            pool.wait_ge(S("topk"), QB)
                        pool.wait_ge(S("t_x"), it * NU + (32 * (T + 1) + i + 1))
                        W = P * (qb + 1)
                        pool.tensor_tensor(bmC[:, i % 2, 0:W], biasC[:, pl, par, SEQ - W:SEQ],
                                           score[:, qb, 0:W], ALU.add).then_inc(S("C_bm"), 1)
            ffn(1)

        @block.tensor
        def _(pe):
            def block_products(b, s, place, chunks, hi, lo, first=True, last=True, arrived=None, inc=None):
                if b is not None:
                    pe.wait_ge(S("w_lo"), b + 1)
                for half in range(2):
                    cols = slice(HALF * half, HALF * half + HALF)
                    for n, (j, c) in enumerate(chunks):
                        if arrived is not None and half == 0:
                            arrived(c)
                        for i, (w, r) in enumerate(((w_hi, hi), (w_hi, lo), (w_lo, hi))):
                            mm = pe.matmul(PS[:, 2 * place + half, 0:HALF], w[:, s, j * P:(j + 1) * P],
                                           r[:, c, cols], start=first and n == 0 and i == 0,
                                           stop=last and n == len(chunks) - 1 and i == 2)
                mm.then_inc(S(inc or "w_used"), 1)

            EVERY = [(c, c) for c in range(KC)]

            def act_chunk(k):
                return lambda c: pe.wait_ge(S("n_lo"), KC * k + c + 1)

            def broadcast_sum(t, weights, inc):
                for half in range(2):
                    mm = pe.matmul(PS[:, 4 + half, 0:HALF], weights, t[:, HALF * half:HALF * half + HALF],
                                   start=True, stop=True)
                mm.then_inc(S(inc), 1)

            def norm_sum(k):
                pe.wait_ge(S("ssum"), KC * (k + 1))
                broadcast_sum(sqsum, ones, "n_ss")

            def products_in(l, k, midway=None):
                b0 = IN[l]["b0"]

                def head_sum(q, s):
                    pe.wait_ge(S("hn_ln"), q + 1)
                    broadcast_sum(sq[:, s, :], ones2, "hn_ss")

                def body(n, like):
                    pe.wait_ge(S("free_a"), n + (l * AB_BLOCKS + 1))
                    block_products(n + b0, (b0 + like) % 2, like % 2, EVERY, act_hi, act_lo,
                                   arrived=act_chunk(k) if like == 0 else None)
                    q = normed(l, n - 1, like - 1)
                    if q is not None:
                        pe.wait_ge(S("free_a"), n + (l * AB_BLOCKS + 2))
                        head_sum(q, normed(l, like - 1, like - 1) % 2)
                walk(pe, l, body, midway)
                last = IN[l]["n"] - 1
                q = normed(l, last, last)
                if q is not None:
                    pe.wait_ge(S("free_a"), last + l * AB_BLOCKS + 3)
                    head_sum(q, q % 2)

            def attention(kind, its, base, q_of, k_of, v_of, staged):
                with pe.Fori(0, its) as it:
                    u0 = it * NU

                    def scores(i):
                        pl, par, qb = UNITS[i]
                        if par == 0 and qb == 0:
                            staged(pe, it, pl)
                        W, rows = P * (qb + 1), slice(HD * par, HD * par + HD)
                        pe.wait_ge(S("t_x"), u0 + (base + i + 1))
                        pe.matmul(PS[:, i % 2, 0:W], q_of(pl)[rows, qb * P:(qb + 1) * P],
                                  k_of(pl)[rows, 0:W], start=True, stop=True).then_inc(S("t_s"), 1)

                    def turn(i):
                        qb = UNITS[i][2]
                        pe.wait_ge(S("t_n"), u0 + (base + i + 1))
                        pe.wait_ge(S("t_c"), u0 + (base + i + 1))
                        for kb in range(qb + 1):
                            src = (pA if kind == "A" else pC)[:, i % 2, kb * P:(kb + 1) * P]
                            mm = pe.transpose(PS[:, 2 + i % 2, kb * P:(kb + 1) * P], src, ident)
                        mm.then_inc(S("t_t"), 1)

                    def out(i):
                        pl, par, qb = UNITS[i]
                        if par == 0 and qb == 0:
                            pe.wait_ge(S("t_o"), it * 2 + (base // 8 + pl + 1))
                        pe.wait_ge(S("t_c"), u0 + (base + i + 3))
                        for kb in range(qb + 1):
                            pt = (ptA if kind == "A" else ptC)[:, i % 2, kb * P:(kb + 1) * P]
                            mm = pe.matmul(PS[HD * par:HD * par + HD, 4 + pl, qb * P:(qb + 1) * P],
                                           v_of(pl, kb, par), pt, start=kb == 0, stop=kb == qb)
                        mm.then_inc(S("t_v"), 1)

                    for i in range(NU + 2):
                        if i < NU:
                            scores(i)
                        if 1 <= i <= NU:
                            turn(i - 1)
                        if i >= 2:
                            out(i - 2)

            def ffn(l):
                L = LAYERS[l]
                f0 = FREE_V * l + 1
                with pe.Fori(0, KC - 1, 2) as j:
                    for u in range(2):
                        pe.wait_ge(S("free_v"), j + (f0 + u))
                        block_products(j + (L["out"] + u), (L["out"] + u) % 2, u, EVERY, act_hi, act_lo)
                norm_sum(3 * l + 1)

                def up(f, arrived):
                    for u in range(2):
                        pe.wait_ge(S("free_v"), f * 2 + (f0 + 8 + u))
                        block_products(f * 2 + (L["ff"] + u), (L["ff"] + u) % 2, u, EVERY, act_hi, act_lo,
                                       arrived=arrived if u == 0 else None)
                up(0, act_chunk(3 * l + 1))
                with pe.Fori(1, FC) as f:
                    up(f, None)
                pe.wait_ge(S("h_lo"), FC * (l + 1) + 1)
                with pe.Fori(0, KC - 1, 2) as j:
                    for u in range(2):
                        pe.wait_ge(S("free_v"), j + (f0 + 8 + 2 * FC + u))
                        for i in range(3):
                            chunks = [(c - 8 * i, c) for c in range(8 * i, min(8 * i + 8, FC))]
                            b = L["down"] + 3 * u + i
                            block_products(j * 3 + b, b % 2, u, chunks, h_hi, h_lo, i == 0, i == 2)
                pe.wait_ge(S("p_lo"), l + 1)
                for o in range(KC):
                    b = L["proj"] + o // 4
                    pe.wait_ge(S("free_v"), f0 + 16 + 2 * FC + o)
                    block_products(b if o % 4 == 0 else None, b % 2, o % 2,
                                   [(o % 4 * 2 + c, c) for c in range(2)], p_hi, p_lo,
                                   inc="w_used" if o % 4 == 3 else "proj")
                    if o == 3:
                        norm_sum(3 * l + 2)
                for m in range(KC):
                    pe.wait_ge(S("free_v"), f0 + 24 + 2 * FC + m)
                    b = L["gate"] + m
                    block_products(b, b % 2, m % 2, EVERY, act_hi, act_lo,
                                   arrived=act_chunk(3 * l + 2) if m == 0 else None)

            pe.sem_inc(S("t_t"), 2)
            pe.sem_inc(S("t_v"), 2)
            pe.wait_ge(S("tables_in"), 16 * 6)
            for n, (r, rows, o) in enumerate(((R_A, 8, O_A), (R_C, 16, O_C))):
                for half, w in enumerate((512, RW - 512)):
                    pe.matmul(PS[0:rows, 2 * n + half, 0:w], brow[:, r:r + rows],
                              orow[:, o + 512 * half:o + 512 * half + w], start=True,
                              stop=True).then_inc(S("rrow_ps"), 1)
            norm_sum(0)
            pe.wait_ge(S("rrow_ok"), 4)
            products_in(0, 0)

            pe.wait_ge(S("free_a"), AB_BLOCKS + 2)
            pe.wait_ge(S("hn_ln"), 8 + 1)
            for kb in range(QB):
                for i in range(4):
                    mm = pe.transpose(PS[:, 4 + kb, i * P:(i + 1) * P], yA[:, 8 + i, kb * P:(kb + 1) * P], ident)
                mm.then_inc(S("A_vt"), 1)
            pe.wait_ge(S("A_v"), QB)
            attention("A", 2, 0, lambda pl: qstA[:, pl, :], lambda pl: kstA[:, pl, :],
                      lambda pl, kb, par: vstA[:, pl, kb, HD * par:HD * par + HD],
                      lambda pe, it, pl: pe.wait_ge(S("A_st"), it * 6 + (3 * pl + 3)))

            pe.wait_ge(S("a2_bias"), 32)
            pe.wait_ge(S("a2_qz"), 2)
            pe.matmul(PS[0:64, 6, 0:NK], sbA[:, 0:64], sbA[:, 64:64 + NK], start=True, stop=False)
            for b in range(NS):
                pe.wait_ge(S(f"keys{b % 2}"), 16 * (b // 2 + 1))
                pe.wait_ge(S("s_kn"), b + 1)
                for t in range(4):
                    mm = pe.matmul(PS[0:64, 6, 0:NK], qzA[:, t * NS + b, :], kcA[:, b % 2, t, :],
                                   start=False, stop=b == NS - 1 and t == 3)
                mm.then_inc(S("s_ks"), 1)
            for t in range(4):
                mm = pe.transpose(PS[0:NS, 4, t * P:(t + 1) * P], yA[:, 8 + t, SEQ:NT], ident)
            mm.then_inc(S("a2_vt"), 1)
            pe.wait_ge(S("s_p"), 1)
            for kb in range(2):
                mm = pe.transpose(PS[:, 7, kb * 64:(kb + 1) * 64], psA[:, kb * P:(kb + 1) * P], ident[0:64, 0:64])
            mm.then_inc(S("a2_pt"), 1)
            pe.wait_ge(S("a2_pd"), 1)
            pe.matmul(PS[0:NS, 5, 0:64], rowsel[0:64, :], pdA[:], start=True, stop=True).then_inc(S("a2_pn"), 1)
            pe.wait_ge(S("a2_ptc"), 1)
            pe.wait_ge(S("a2_pnc"), 2)
            for b in range(NS):
                pe.wait_ge(S(f"values{b % 2}"), 16 * (b // 2 + 1))
                for t in range(4):
                    for kb in range(2):
                        c = t * NS + b
                        mm = pe.matmul(PS[:, 5, 2 * c:2 * c + 2], vcA[:, b % 2, kb, t * P:(t + 1) * P],
                                       ptsA[:, kb, c:c + 33:32], start=kb == 0, stop=kb == 1)
                mm.then_inc(S("s_vs"), 1)
            pn = pnA[:].rearrange("k (r t b) -> k r t b", r=2, t=4)
            for t in range(4):
                mm = pe.matmul(PS[:, 6, 16 * t:16 * t + 16], vnA[:, t * P:(t + 1) * P], pn[:, :, t, :],
                               start=True, stop=True)
            mm.then_inc(S("a2_o"), 1)

            for c in range(NCH):
                if c >= 4:
                    pe.wait_ge(S("g_vc"), c - 3)
                for h in range(4):
                    mm = pe.transpose(PS[0:GC, c % 4, h * P:(h + 1) * P], yA[:, 16 + h, c * GC:(c + 1) * GC], ident)
                mm.then_inc(S("g_vt"), 1)
            pe.wait_ge(S("g_vc"), NCH)
            for i in range(2):
                for half in range(2):
                    mm = pe.matmul(PS[:, 2 * i + half, 0:HALF], gw2[:, i * P:(i + 1) * P],
                                   blr[:, half * HALF:(half + 1) * HALF], start=True, stop=True)
                mm.then_inc(S("g_z"), 1)
            pe.wait_ge(S("a2_done"), 1)
            for i in range(2):
                pe.wait_ge(S("g_qk"), i + 1)
                for c in range(NCH):
                    mm = pe.transpose(PS[0:GC, 4 + 2 * i + c // 4, c % 4 * P:(c % 4 + 1) * P],
                                      yA[:, 14 + i, c * GC:(c + 1) * GC], ident)
                mm.then_inc(S("g_kt"), 1)

            def scores_g(h):
                i, rows = h // 2, slice(HD * (h % 2), HD * (h % 2) + HD)
                if h >= 2:
                    pe.wait_ge(S("g_am"), h - 1)
                for c in range(NCH):
                    cols = slice(c * GC, (c + 1) * GC)
                    mm = pe.matmul(PS[0:GC, h % 2, cols], yA[rows, 14 + i, cols], yA[rows, 12 + i, cols],
                                   start=True, stop=True)
                mm.then_inc(S("g_a"), 1)

            def out_g(h):
                i, rows = h // 2, slice(HD * (h % 2), HD * (h % 2) + HD)
                pe.wait_ge(S("g_am"), h + 1)
                pe.wait_ge(S("g_s"), NCH * (i + 1))
                if h >= 1:
                    pe.wait_ge(S("g_oc"), h)
                for c in range(NCH):
                    cols = slice(c * GC, (c + 1) * GC)
                    pe.matmul(PS[:, 2, cols], vb[:, c, h, :], att[:, h % 2, cols], start=True, stop=True)
                for c in range(NCH):
                    cols = slice(c * GC, (c + 1) * GC)
                    mm = pe.matmul(PS[:, 3, cols], stm[rows, i, c, :], yA[rows, 12 + i, cols], start=True, stop=True)
                mm.then_inc(S("g_o"), 1)

            for i in range(2):
                scores_g(2 * i)
                scores_g(2 * i + 1)
                pe.wait_ge(S("g_ktc"), 4)
                for c in range(NCH):
                    n = NCH * i + c
                    if n >= 2:
                        pe.wait_ge(S("g_s"), n - 1)
                    pe.matmul(PS[:, 6 + c % 2, 0:2 * P], kbt[:, i, c, :], vb[:, c, 2 * i:2 * i + 2, :],
                              start=True, stop=True).then_inc(S("g_u"), 1)
                out_g(2 * i)
                out_g(2 * i + 1)

            pe.wait_ge(S("g_oc"), 4)
            for i in range(2):
                pe.transpose(PS[0:NS, 0, i * P:(i + 1) * P], yA[:, 14 + i, SEQ:NT], ident)
            for h in range(4):
                mm = pe.transpose(PS[0:NS, 1, h * P:(h + 1) * P], yA[:, 16 + h, SEQ:NT], ident)
            mm.then_inc(S("s_t"), 1)
            pe.wait_ge(S("s_kz"), 2)
            for k in range(8):
                i, b0 = k // 4, 2 * (k % 4)
                for b in range(2):
                    mm = pe.matmul(PS[:, k, b * 256:(b + 1) * 256], kz8[:, b0 + b, i * P:(i + 1) * P],
                                   vt8[:, i * 256:(i + 1) * 256], start=True, stop=True)
                mm.then_inc(S("s_kv"), 1)
            pe.wait_ge(S("s_new"), 16)
            pe.wait_ge(S("s_qz"), 1)
            for i in range(2):
                for b in range(NS):
                    c = 2 * (i * NS + b)
                    mm = pe.matmul(PS[:, 0, c:c + 2], s0[:, b, i, :], qz8[:, i, b, :], start=True, stop=True)
            mm.then_inc(S("s_o"), 1)
            for h in range(4):
                pe.wait_ge(S("b_sq"), h + 1)
                if h >= 1:
                    pe.wait_ge(S("b_ln"), h)
                broadcast_sum(sq[:, h % 2, :], ones, "b_ss")
            pe.wait_ge(S("mix_lo"), 4)
            ffn(0)

            def indexer():
                pe.wait_ge(S("free_a"), AB_BLOCKS + 8)
                for kb in range(QB):
                    mm = pe.transpose(PS[:, 6, kb * NS:(kb + 1) * NS], yC[0:NS, 5, kb * P:(kb + 1) * P],
                                      ident[0:NS, 0:NS])
                mm.then_inc(S("i_wt"), 1)
                pe.wait_ge(S("i_w"), 1)
                pe.wait_ge(S("hn_ok"), 9 + 2)
                k = 0
                for qb in range(1, QB):
                    for h in range(NS):
                        rows = slice(HD * (h % 2), HD * (h % 2) + HD)
                        if k >= 2:
                            pe.wait_ge(S("i_r"), k - 1)
                        pe.matmul(PS[:, 6 + k % 2, 0:P * (qb + 1)], yC[rows, h // 2, qb * P:(qb + 1) * P],
                                  yC[rows, 4, 0:P * (qb + 1)], start=True, stop=True).then_inc(S("i_s"), 1)
                        k += 1

            norm_sum(3)
            products_in(1, 3, indexer)
            pe.wait_ge(S("free_a"), AB_BLOCKS + C_BLOCKS + 2)
            pe.wait_ge(S("hn_ln"), 19 + 1)
            for kb in range(QB):
                for T in range(2):
                    mm = pe.transpose(PS[:, 4 + kb, T * P:(T + 1) * P], yC[:, 8 + T, kb * P:(kb + 1) * P], ident)
                mm.then_inc(S("C_vt"), 1)
            pe.wait_ge(S("C_vtc"), QB)
            pe.wait_ge(S("hn_ok"), 19 + 2)
            for T in range(2):
                attention("C", 2, 32 * (T + 1), lambda pl: qstC[:, pl, :], lambda pl: yC[:, 6 + T, :],
                          lambda pl, kb, par: vtokC[:, kb, T * P + HD * par:T * P + HD * par + HD],
                          lambda pe, it, pl: pe.wait_ge(S("C_st"), it * 2 + (4 * T + pl + 1)))

            pe.wait_ge(S("d_z"), 3)
            pe.wait_ge(S("d_ik"), 16 * 32)
            pe.wait_ge(S("t_o"), 12 + 2)
            for b in range(NS + 1):
                if b < NS:
                    if b >= 2:
                        pe.wait_ge(S("d_r"), b - 1)
                    pe.matmul(PS[0:NS, 6 + b % 2, 0:NK], iqz[:, b, :], ikc[:, b, :], start=True,
                              stop=True).then_inc(S("d_s"), 1)
                if b >= 1:
                    pe.wait_ge(S("d_r"), b)
                    pe.matmul(PS[0:NS, 5, 0:NK], iwz[:, b - 1, :], rel8[:, (b - 1) % 2, :], start=b == 1,
                              stop=b == NS).then_inc(S("d_a"), 1)
            pe.wait_ge(S("d_bias"), 32)
            pe.wait_ge(S("d_qz"), 4)
            pe.matmul(PS[:, 4, 0:NK], sbC[:, 0:P], sbC[:, P:P + NK], start=True, stop=False)
            pe.wait_ge(S("d_mask"), 1)
            pe.matmul(PS[:, 4, 0:NK], colsel[:], sc8[:], start=False, stop=False)
            for b in range(NS):
                pe.wait_ge(S(f"keys{b % 2}"), 64 + 32 * (b // 2 + 1))
                pe.wait_ge(S("s_kn"), NS + b + 1)
                for T in range(2):
                    mm = pe.matmul(PS[:, 4, 0:NK], qzC[:, T * NS + b, :], kcC[:, b % 2, T, :], start=False,
                                   stop=b == NS - 1 and T == 1)
                mm.then_inc(S("s_ks"), 1)
            for T in range(2):
                mm = pe.transpose(PS[0:NS, 6, T * P:(T + 1) * P], yC[:, 8 + T, SEQ:NT], ident)
            mm.then_inc(S("d_vt"), 1)
            pe.wait_ge(S("s_p"), 2)
            for kb in range(2):
                mm = pe.transpose(PS[:, 7, kb * P:(kb + 1) * P], psC[:, kb * P:(kb + 1) * P], ident)
            mm.then_inc(S("d_pt"), 1)
            pe.wait_ge(S("d_pd"), 1)
            pe.wait_ge(S("d_vtc"), 1)
            pe.matmul(PS[0:NS, 6, 256:256 + P], rowsel, pdC[:], start=True, stop=True).then_inc(S("d_pn"), 1)
            pe.wait_ge(S("d_ptc"), 1)
            pe.wait_ge(S("d_pnc"), 1)
            pt = ptsC[:].rearrange("k n (r t b) -> k n r t b", r=2, t=8)
            for b in range(NS):
                pe.wait_ge(S(f"values{b % 2}"), 64 + 32 * (b // 2 + 1))
                for T in range(2):
                    for kb in range(2):
                        c = (b * 2 + T) * 8
                        mm = pe.matmul(PS[:, 5, c:c + 8], vcC[:, b % 2, kb, T * P:(T + 1) * P],
                                       pt[:, kb, :, 4 * T:4 * T + 4, b], start=kb == 0, stop=kb == 1)
                mm.then_inc(S("s_vs"), 1)
            pn = pnC[:].rearrange("k (r t b) -> k r t b", r=2, t=8)
            for T in range(2):
                mm = pe.matmul(PS[:, 4, 64 * T:64 * T + 64], vnC[:, T * P:(T + 1) * P],
                               pn[:, :, 4 * T:4 * T + 4, :], start=True, stop=True)
            mm.then_inc(S("d_o"), 1)
            pe.wait_ge(S("mix_lo"), 5)
            ffn(1)

        @block.scalar
        def _(act):
            chain = [0]

            def then(ins):
                chain[0] += 1
                ins.then_inc(S("act_chain"), 1)
                act.wait_ge(S("act_chain"), chain[0])

            def high(b, s, slot_used=True):
                act.wait_ge(S(f"w_raw{s}"), b * 8 + (16 - 8 * s))
                if slot_used:
                    act.wait_ge(S("w_used"), b - 1)
                act.activation(w_hi[:, s, :], w_raw[:, s, :], ACT.Copy).then_inc(S("w_hi"), 1)

            def square(k, m, s):
                if not (isinstance(m, int) and k == 0 and m < 2):
                    act.wait_ge(S("ssum"), m + (KC * k - 1))
                act.activation(sq[:, s:s + 1, :], x[:, bass.ds(m, 1), :], ACT.Square).then_inc(S("sq_ok"), 1)

            def norm(k):
                act.wait_ge(S("n_ss"), k + 1)
                then(act.activation(halves(rs[:, 0, :]), slot(2), ACT.Ln, bias=vecs[:, V_EPS:V_EPS + 1],
                                    scale=1.0 / DM))
                act.activation(rs[:, 0, :], rs[:, 0, :], ACT.Exp, scale=-0.5).then_inc(S("n_rs"), 1)
                for c in range(KC):
                    act.wait_ge(S("n_t"), KC * k + c + 1)
                    act.activation(act_hi[:, c, :], tmp[:, c % 2, :], ACT.Copy).then_inc(S("n_hi"), 1)

            def products_in(l, midway=None):
                b0, y = IN[l]["b0"], IN[l]["y"]

                def head_rms(q, s):
                    act.wait_ge(S("hn_ss"), q + 1)
                    act.wait_ge(S("hn_ok"), q + 1)
                    act.activation(halves(rs[:, s, :]), slot(2), ACT.Ln, bias=vecs[:, V_EPS:V_EPS + 1],
                                   scale=1.0 / HD).then_inc(S("hn_ln"), 1)
                    act.wait_ge(S("hn_ln"), q + 2)
                    act.activation(rs[:, s, :], rs[:, s, :], ACT.Exp, scale=-0.5).then_inc(S("hn_rs"), 1)

                def body(n, like):
                    high(n + (b0 + 1), (b0 + like + 1) % 2, slot_used=b0 + like > 0)
                    act.wait_ge(S("w_used"), n + (b0 + 1))
                    place = slot(like % 2)
                    q = normed(l, n, like)
                    rank = l == 0 and like == AB_BLOCKS - 1
                    if not rank:
                        dst = y[:, bass.ds(n, 1), :].rearrange("p o (h n) -> p (o h) n", h=2)
                    if q is not None:
                        s = normed(l, like, like) % 2
                        act.activation(dst, place, ACT.Identity, scale=gains[:, bass.ds(q, 1)])
                        act.activation(halves(sq[:, s, :]), place, ACT.Square).then_inc(S("free_a"), 1)
                    elif rank:
                        act.activation(halves(blr[:]), place[0:16], ACT.Copy).then_inc(S("free_a"), 1)
                    else:
                        by = (NS * HD) ** -0.5 if l == 1 and like == 5 else 1.0
                        act.activation(dst, place, ACT.Copy, scale=by).then_inc(S("free_a"), 1)
                    q = normed(l, n - 1, like - 1)
                    if q is not None:
                        head_rms(q, normed(l, like - 1, like - 1) % 2)
                walk(act, l, body, midway)
                last = IN[l]["n"] - 1
                q = normed(l, last, last)
                if q is not None:
                    head_rms(q, q % 2)

            def attention(its, base, pair0, xs, ps, pts, stat):
                with act.Fori(0, its) as it:
                    u0 = it * NU

                    def exps(i):
                        W = P * (UNITS[i][2] + 1)
                        act.wait_ge(S("t_x"), u0 + (base + i + 3))
                        act.wait_ge(S("t_t"), u0 + (base + i + 1))
                        act.activation(ps[:, i % 2, 0:W], xs[:, i % 2, 0:W], ACT.Exp, bias=stat[:, i % 2, 0:1],
                                       scale=-1.0, accum_out=stat[:, i % 2, 1:2]).then_inc(S("t_e"), 1)

                    def copy(i):
                        W = P * (UNITS[i][2] + 1)
                        act.wait_ge(S("t_t"), u0 + (base + i + 3))
                        act.wait_ge(S("t_v"), u0 + (base + i + 1))
                        act.activation(pts[:, i % 2, 0:W], PS[:, 2 + i % 2, 0:W], ACT.Copy).then_inc(S("t_c"), 1)

                    def out(pl):
                        act.wait_ge(S("t_v"), u0 + (base + 8 * pl + 10))
                        act.activation(act_hi[:, bass.ds(it * 2 + (pair0 + pl), 1), 0:SEQ],
                                       PS[:, 4 + pl:5 + pl, :], ACT.Copy).then_inc(S("t_oh"), 1)

                    for i in range(NU + 1):
                        if i < NU:
                            exps(i)
                        if i > 0:
                            copy(i - 1)
                        if i == 11:
                            out(0)
                    act.wait_ge(S("t_v"), u0 + (base + NU + 2))
                    out(1)

            def ffn(l):
                L = LAYERS[l]
                with act.Fori(0, KC - 1, 2) as j:
                    for u in range(2):
                        high(j + (L["out"] + u + 1), (L["out"] + u + 1) % 2)
                        act.wait_ge(S("free_v"), j + (FREE_V * l + u + 3))
                        square(3 * l + 1, j + u, u)
                for name, n in ((("a_out", 32), ("s_out", 16)) if l == 0 else (("c_out", 48),)):
                    act.wait_ge(S(name), n)
                act.dma_start(p_raw[:], a["pT"][l]).then_inc(S("p_in"), 16)
                norm(3 * l + 1)
                act.wait_ge(S("p_in"), 16 * (l + 1))
                act.activation(p_hi[:], p_raw[:], ACT.Copy).then_inc(S("p_hi"), 1)
                with act.Fori(0, FC) as f:
                    high(f * 2 + (L["ff"] + 1), (L["ff"] + 1) % 2)
                    act.wait_ge(S("w_used"), f * 2 + (L["ff"] + 1))
                    act.activation(halves(sq[:, 0, :]), slot(0), ACT.Exp, scale=-1.0).then_inc(S("f_e"), 1)
                    high(f * 2 + (L["ff"] + 2), L["ff"] % 2)
                    act.wait_ge(S("free_v"), f * 2 + (FREE_V * l + 8 + 4))
                    act.activation(h_hi[:, bass.ds(f, 1), :], tmp[:, 0:1, :], ACT.Copy).then_inc(S("h_hi"), 1)
                with act.Fori(0, KC - 1, 2) as j:
                    for u in range(2):
                        for i in range(3):
                            b = L["down"] + 3 * u + i + 1
                            high(j * 3 + b, b % 2)
                        act.wait_ge(S("free_v"), j + (FREE_V * l + 8 + 2 * FC + u + 3))
                        square(3 * l + 2, j + u, u)
                for i in range(2):
                    high(L["proj"] + i + 1, (L["proj"] + i + 1) % 2)
                    if i == 0:
                        norm(3 * l + 2)
                with act.Fori(0, KC - 1, 2) as j:
                    for u in range(2):
                        high(j + (L["gate"] + u + 1), (L["gate"] + u + 1) % 2)
                        act.wait_ge(S("w_used"), j + (L["gate"] + u + 1))
                        act.activation(halves(tmp[:, u, :]), slot(u), ACT.Exp, scale=-1.0).then_inc(S("g_e"), 1)
                        act.wait_ge(S("x_new"), j + (KC * l + u + 1))
                        if l == 0:
                            square(3, j + u, u)

            act.sem_inc(S("free_a"), 2)
            act.sem_inc(S("hn_ln"), 1)
            act.sem_inc(S("t_e"), 2)
            act.sem_inc(S("t_c"), 2)
            act.wait_ge(S("x_in"), 16)
            for m in range(KC):
                square(0, m, m % 2)
            high(0, 0, slot_used=False)
            act.wait_ge(S("tables_in"), 16 * 6)
            norm(0)
            act.wait_ge(S("gains"), 3)
            products_in(0)
            act.wait_ge(S("hn_ok"), 8 + 2)
            act.wait_ge(S("free_a"), AB_BLOCKS + 2)
            act.dma_start(a["a_k"], yA[:, 4:8, :]).then_inc(S("a_out"), 16)
            act.dma_start(a["a_v"], yA[:, 8:12, :]).then_inc(S("a_out"), 16)
            attention(2, 0, 0, xA, pA, ptA, statA)

            act.wait_ge(S("t_o"), 4 + 2)
            act.dma_start(sbA[:, 0:64], a["bias_rows"][:, R_SA:R_SA + 64]).then_inc(S("a2_bias"), 16)
            act.dma_start(sbA[:, 64:64 + NK], a["onehots"][:, O_SA:O_SA + NK]).then_inc(S("a2_bias"), 16)
            for b in range(NS):
                if b >= 2:
                    act.wait_ge(S("s_ks"), b - 1)
                act.dma_start(kcA[:, b % 2, :, 0:PAST], a["cache_k"][b]).then_inc(S(f"keys{b % 2}"), 16)
                if b < 2:
                    act.dma_start(vcA[:, b, :, :], a["cache_v"][b]).then_inc(S(f"values{b}"), 16)
            act.wait_ge(S("s_m"), 1)
            act.activation(psA[:], PS[0:64, 6, 0:NK], ACT.Exp, bias=sstA[:, 0:1],
                           accum_out=sstA[:, 1:2]).then_inc(S("s_e"), 1)
            act.wait_ge(S("a2_pt"), 1)
            act.activation(ptsA[:], PS[:, 7, 0:P].rearrange("p (n c) -> p n c", n=2), ACT.Copy).then_inc(S("a2_ptc"), 1)
            for b in range(2, NS):
                act.wait_ge(S("s_vs"), b - 1)
                act.dma_start(vcA[:, b % 2, :, :], a["cache_v"][b]).then_inc(S(f"values{b % 2}"), 16)
            act.wait_ge(S("a2_os"), 2)
            act.activation(act_hi[:, 0:4, SEQ:NT], osA[:], ACT.Copy).then_inc(S("a2_oh"), 1)

            act.wait_ge(S("a2_done"), 1)
            for c in range(NCH):
                act.wait_ge(S("g_vt"), c + 1)
                act.activation(vb[:, c, :, :], PS[0:GC, c % 4, :].rearrange("p (h e) -> p h e", h=4),
                               ACT.Copy).then_inc(S("g_vc"), 1)
            for i in range(2):
                act.wait_ge(S("g_na"), i + 1)
                then(act.activation(zn[:, i, :], zn[:, i, :], ACT.Exp))
                act.activation(zn[:, i, :], zn[:, i, :], ACT.Ln, bias=vecs[:, V_ONE:V_ONE + 1]).then_inc(S("g_l"), 1)
            for i in range(2):
                act.wait_ge(S("g_d"), i + 1)
                by_chunk = cum[:, i, :].rearrange("p (c t) -> p c t", t=GC)
                act.activation(decay[:, i, 0, :], by_chunk[:, :, GC // 2 - 1], ACT.Exp)
                act.activation(decay[:, i, 1, :], by_chunk[:, :, GC - 1], ACT.Exp)
                act.activation(zt[:, i, 0:SEQ], zn[:, i, 0:SEQ], ACT.Exp).then_inc(S("g_e1"), 1)
                act.wait_ge(S("g_e1"), i + 1)
                act.activation(zn[:, i, 0:SEQ], zn[:, i, 0:SEQ], ACT.Exp, scale=-1.0).then_inc(S("g_e2"), 1)
            for i in range(2):
                act.wait_ge(S("g_kt"), i + 1)
                for n in range(2):
                    act.activation(kbt[:, i, 4 * n:4 * n + 4, :],
                                   PS[0:GC, 4 + 2 * i + n, :].rearrange("p (c d) -> p c d", c=4),
                                   ACT.Copy).then_inc(S("g_ktc"), 1)
            for h in range(4):
                act.wait_ge(S("g_o"), h + 1)
                act.activation(yA[:, 16 + h, 0:SEQ], PS[:, 2, :], ACT.Copy).then_inc(S("g_o1"), 1)

            act.wait_ge(S("g_s"), 2 * NCH)
            act.dma_start(a["b_state"], st[:]).then_inc(S("b_out"), 16)
            act.wait_ge(S("g_oc"), 4)
            act.wait_ge(S("b_out"), 16)
            act.dma_start(s0[:], a["state"]).then_inc(S("s_in"), 16)
            act.activation(eg[:], gs[:], ACT.Exp).then_inc(S("s_eg"), 1)
            for h in range(4):
                act.wait_ge(S("b_o"), 1)
                if h >= 2:
                    act.wait_ge(S("b_ss"), h - 1)
                act.activation(sq[:, h % 2, :], yA[:, 16 + h, :], ACT.Square).then_inc(S("b_sq"), 1)
                act.wait_ge(S("b_ss"), h + 1)
                if h >= 2:
                    act.wait_ge(S("b_n"), h - 1)
                act.activation(halves(rs[:, h % 2, :]), slot(2), ACT.Ln, bias=vecs[:, V_EPS:V_EPS + 1],
                               scale=1.0 / P).then_inc(S("b_ln"), 1)
                act.wait_ge(S("b_ln"), h + 1)
                act.activation(rs[:, h % 2, :], rs[:, h % 2, :], ACT.Exp, scale=-0.5).then_inc(S("b_rs"), 1)
                if h >= 2:
                    act.wait_ge(S("mix_lo"), h)
                act.activation(tmp[:, h % 2, :], yA[:, 20 + h, :], ACT.Exp, scale=-1.0).then_inc(S("b_e"), 1)
                act.wait_ge(S("b_g"), h + 1)
                act.activation(act_hi[:, 4 + h, :], yA[:, 16 + h, :], ACT.Copy).then_inc(S("b_hi"), 1)
            act.wait_ge(S("s_new"), 16)
            act.dma_start(a["s_state"], s0[:]).then_inc(S("s_out"), 16)
            ffn(0)

            act.wait_ge(S("x_new"), KC)
            act.dma_start(ptab[:], a["pages"]).then_inc(S("d_tab"), 16)
            act.dma_start(sbC[:, 0:P], a["bias_rows"][:, R_SC:R_SC + P]).then_inc(S("d_bias"), 16)
            act.dma_start(sbC[:, P:P + NK], a["onehots"][:, O_SC:O_SC + NK]).then_inc(S("d_bias"), 16)
            act.wait_ge(S("d_tab"), 16)

            def page(i):
                return act.value_load(ptab[0:1, i:i + 1], min_val=0, max_val=19)

            def index_pages():
                for b in range(NS):
                    for n in range(2):
                        pg = page(2 * b + n)
                        for r in range(2):
                            act.dma_start(ikc[HD * r:HD * r + HD, b, n * P:(n + 1) * P],
                                          a["pool_ik"][pg]).then_inc(S("d_ik"), 16)

            def pages(b, name, pool, dst):
                for n in range(2):
                    act.dma_start(dst(n), pool[page(2 * b + n)]).then_inc(
                        S(f"{name}{b % 2}"), 16)

            def indexer():
                k = 0
                for qb in range(1, QB):
                    for h in range(NS):
                        act.wait_ge(S("i_s"), k + 1)
                        if k >= 2:
                            act.wait_ge(S("i_a"), k - 1)
                        W = P * (qb + 1)
                        act.activation(reluC[:, k % 2, 0:W], PS[:, 6 + k % 2, 0:W], ACT.Relu).then_inc(S("i_r"), 1)
                        k += 1

            norm(3)
            products_in(1, indexer)
            act.wait_ge(S("hn_ok"), 19 + 2)
            act.wait_ge(S("free_a"), AB_BLOCKS + C_BLOCKS + 2)
            act.dma_start(a["c_k"], yC[:, 6:8, :]).then_inc(S("c_out"), 16)
            act.dma_start(a["c_v"], yC[:, 8:10, :]).then_inc(S("c_out"), 16)
            act.dma_start(a["c_ik"], yC[0:HD, 4, :]).then_inc(S("c_out"), 16)
            index_pages()
            for b in range(2):
                pages(b, "keys", a["pool_k"], lambda n: kcC[:, b, :, n * P:(n + 1) * P])
                pages(b, "values", a["pool_v"], lambda n: vcC[:, b, n, :])
            for T in range(2):
                attention(2, 32 * (T + 1), 4 * T, xC, pC, ptC, statC)

            for b in range(NS):
                act.wait_ge(S("d_s"), b + 1)
                if b >= 2:
                    act.wait_ge(S("d_a"), b - 1)
                act.activation(rel8[:, b % 2, :], PS[0:NS, 6 + b % 2, 0:NK], ACT.Relu).then_inc(S("d_r"), 1)
            for b in range(2, NS):
                act.wait_ge(S("s_ks"), NS + b - 1)
                pages(b, "keys", a["pool_k"], lambda n: kcC[:, b % 2, :, n * P:(n + 1) * P])
            act.wait_ge(S("s_m"), 2)
            act.activation(psC[:], PS[:, 4, 0:NK], ACT.Exp, bias=sstC[:, 0:1],
                           accum_out=sstC[:, 1:2]).then_inc(S("s_e"), 1)
            act.wait_ge(S("d_pt"), 1)
            act.activation(ptsC[:], PS[:, 7, 0:2 * P].rearrange("p (n c) -> p n c", n=2), ACT.Copy).then_inc(S("d_ptc"), 1)
            for b in range(2, NS):
                act.wait_ge(S("s_vs"), NS + b - 1)
                pages(b, "values", a["pool_v"], lambda n: vcC[:, b % 2, n, :])
            act.wait_ge(S("d_os"), 4)
            act.activation(act_hi[:, :, SEQ:NT], osC[:], ACT.Copy).then_inc(S("d_oh"), 1)
            ffn(1)

        @block.vector
        def _(dve):
            chain = [0]

            def then(ins):
                chain[0] += 1
                ins.then_inc(S("dve_chain"), 1)
                dve.wait_ge(S("dve_chain"), chain[0])

            def waits_done():
                dve.sem_inc(S("waits_done"), 1)

            def add_squares(k, m, s):
                dve.wait_ge(S("sq_ok"), m + (KC * k + 1))
                if not (isinstance(m, int) and k == m == 0):
                    dve.wait_ge(S("ssum"), m + KC * k)
                dve.tensor_tensor(sqsum[:], sqsum[:], sq[:, s, :], ALU.add).then_inc(S("ssum"), 1)

            def clear_sum():
                then(dve.memset(sqsum[:], 0.0))

            def norm(k, gain):
                dve.wait_ge(S("n_rs"), k + 1)
                for c in range(KC):
                    if KC * k + c >= 2:
                        dve.wait_ge(S("n_lo"), KC * k + c - 1)
                    dve.scalar_tensor_tensor(tmp[:, c % 2, :], x[:, c, :], vecs[:, gain + c:gain + c + 1],
                                             rs[:, 0, :], ALU.mult, ALU.mult).then_inc(S("n_t"), 1)
                clear_sum()

            def attention(its, base, pair0, xs, ps, stat, bias):
                with dve.Fori(0, its) as it:
                    u0 = it * NU

                    def add_bias(i):
                        W = P * (UNITS[i][2] + 1)
                        dve.wait_ge(S("t_s"), u0 + (base + i + 1))
                        dve.wait_ge(S("t_e"), u0 + (base + i + 1))
                        added = bias(it, i, W)
                        waits_done()
                        dve.tensor_tensor_reduce(xs[:, i % 2, 0:W], PS[:, i % 2, 0:W], added, -1.0, 1e38,
                                                 ALU.add, ALU.min, stat[:, i % 2, 0:1]).then_inc(S("t_x"), 1)

                    def scale(i):
                        W = P * (UNITS[i][2] + 1)
                        dve.wait_ge(S("t_e"), u0 + (base + i + 3))
                        dve.reciprocal(stat[:, i % 2, 2:3], stat[:, i % 2, 1:2]).then_inc(S("t_r"), 1)
                        dve.wait_ge(S("t_r"), u0 + (base + i + 1))
                        dve.tensor_scalar(ps[:, i % 2, 0:W], ps[:, i % 2, 0:W], stat[:, i % 2, 2:3], None,
                                          ALU.mult).then_inc(S("t_n"), 1)

                    def out(pl):
                        pair = it * 2 + (base // 8 + pl)
                        dve.wait_ge(S("t_oh"), pair + 1)
                        dst = bass.ds(it * 2 + (pair0 + pl), 1)
                        dve.tensor_tensor(act_lo[:, dst, 0:SEQ], PS[:, 4 + pl:5 + pl, :],
                                          act_hi[:, dst, 0:SEQ].bitcast(F32), ALU.subtract).then_inc(S("t_o"), 1)

                    for i in range(NU + 1):
                        if i < NU:
                            add_bias(i)
                        if i > 0:
                            scale(i - 1)
                        if i == 11:
                            out(0)
                    out(1)

            def ffn(l):
                L = LAYERS[l]
                f0 = FREE_V * l + 2
                with dve.Fori(0, KC - 1, 2) as j:
                    for u in range(2):
                        m = bass.ds(j + u, 1)
                        dve.wait_ge(S("w_used"), j + (L["out"] + u + 1))
                        dst = x[:, m, :].rearrange("p o (h n) -> p (o h) n", h=2)
                        dve.tensor_tensor(dst, slot(u), dst, ALU.add).then_inc(S("free_v"), 1)
                        add_squares(3 * l + 1, j + u, u)
                norm(3 * l + 1, V_FFN + KC * l)
                dve.wait_ge(S("n_lo"), KC * (3 * l + 2))
                with dve.Fori(0, FC) as f:
                    dve.wait_ge(S("f_e"), f + (FC * l + 1))
                    dve.tensor_scalar(sq[:, 1, :], sq[:, 0, :], 1.0, None, ALU.add).then_inc(S("f_c"), 1)
                    dve.wait_ge(S("f_c"), f * 2 + (2 * FC * l + 1))
                    dve.reciprocal(sq[:, 1, :], sq[:, 1, :]).then_inc(S("f_c"), 1)
                    dve.wait_ge(S("f_c"), f * 2 + (2 * FC * l + 2))
                    dve.tensor_tensor(halves(tmp[:, 1, :]), slot(0), halves(sq[:, 1, :]), ALU.mult).then_inc(S("free_v"), 1)
                    dve.wait_ge(S("w_used"), f * 2 + (L["ff"] + 2))
                    dve.wait_ge(S("free_v"), f * 2 + (f0 + 8 + 1))
                    dve.wait_ge(S("h_lo"), f + (FC * l + 1))
                    dve.tensor_tensor(halves(tmp[:, 0, :]), slot(1), halves(tmp[:, 1, :]), ALU.mult).then_inc(S("free_v"), 1)
                with dve.Fori(0, KC - 1, 2) as j:
                    for u in range(2):
                        m = bass.ds(j + u, 1)
                        dve.wait_ge(S("w_used"), j * 3 + (L["down"] + 3 * u + 3))
                        dst = x[:, m, :].rearrange("p o (h n) -> p (o h) n", h=2)
                        dve.tensor_tensor(dst, slot(u), dst, ALU.add).then_inc(S("free_v"), 1)
                        add_squares(3 * l + 2, j + u, u)
                for o in range(4):
                    project(l, o)
                norm(3 * l + 2, V_PLE + KC * l)
                for o in range(4, KC):
                    project(l, o)
                with dve.Fori(0, KC - 1, 2) as j:
                    for u in range(2):
                        m = bass.ds(j + u, 1)
                        c = j * 3 + (3 * KC * l + 3 * u)
                        dve.wait_ge(S("g_e"), j + (KC * l + u + 1))
                        dve.tensor_scalar(tmp[:, u, :], tmp[:, u, :], 1.0, None, ALU.add).then_inc(S("free_v"), 1)
                        dve.wait_ge(S("free_v"), j + (f0 + 24 + 2 * FC + u + 1))
                        dve.reciprocal(tmp[:, u, :], tmp[:, u, :]).then_inc(S("g_c"), 1)
                        dve.wait_ge(S("g_c"), j * 2 + (2 * KC * l + 2 * u + 1))
                        dve.tensor_tensor(tmp[:, u:u + 1, :], tmp[:, u:u + 1, :], pp[:, m, :], ALU.mult).then_inc(S("g_c"), 1)
                        dve.wait_ge(S("g_c"), j * 2 + (2 * KC * l + 2 * u + 2))
                        dve.tensor_tensor(x[:, m, :], x[:, m, :], tmp[:, u:u + 1, :], ALU.add).then_inc(S("x_new"), 1)
                        if l == 0:
                            add_squares(3, j + u, u)

            def project(l, o):
                L = LAYERS[l]
                if o % 4 == 3:
                    dve.wait_ge(S("w_used"), L["proj"] + o // 4 + 1)
                else:
                    dve.wait_ge(S("proj"), 6 * l + o - o // 4 + 1)
                dve.tensor_copy(halves(pp[:, o, :]), slot(o % 2)).then_inc(S("free_v"), 1)

            def softmax(n, scores, probs, stat):
                dve.tensor_reduce(stat[:, 0:1], scores, AX.X, ALU.max, negate=True).then_inc(S("s_m"), 1)
                dve.wait_ge(S("s_e"), n + 1)
                then(dve.reciprocal(stat[:, 2:3], stat[:, 1:2]))
                dve.tensor_scalar(probs[:], probs[:], stat[:, 2:3], None, ALU.mult).then_inc(S("s_p"), 1)
                dve.wait_ge(S("s_p"), n + 1)

            dve.sem_inc(S("free_v"), 2)
            dve.sem_inc(S("h_lo"), 1)
            dve.sem_inc(S("t_x"), 2)
            dve.sem_inc(S("t_o"), 2)
            clear_sum()
            for n, rows in enumerate((8, 16)):
                dve.wait_ge(S("rrow_ps"), 2 * n + 2)
                for half, w in enumerate((512, RW - 512)):
                    dve.tensor_copy(rrow[0:rows, n, 512 * half:512 * half + w],
                                    PS[0:rows, 2 * n + half, 0:w]).then_inc(S("rrow_ok"), 1)
            dve.wait_ge(S("tables_in"), 16 * 6)
            dve.tensor_scalar(gains[:, 0:4], vecs[:, V_NG:V_NG + 4], HD ** -0.5, None, ALU.mult).then_inc(S("gains"), 1)
            dve.tensor_copy(gains[:, 4:11], vecs[:, V_NG + 4:V_NG + 11]).then_inc(S("gains"), 1)
            dve.tensor_scalar(gains[:, 11:19], vecs[:, V_NG + 11:V_NG + 19], HD ** -0.5, None,
                              ALU.mult).then_inc(S("gains"), 1)
            for m in range(KC):
                add_squares(0, m, m % 2)
            norm(0, V_MIX)

            dve.wait_ge(S("rows_out"), 64)
            for kb in range(QB):
                dve.wait_ge(S("A_vt"), kb + 1)
                dve.tensor_copy(vtokA[:, kb, :], PS[:, 4 + kb, :]).then_inc(S("A_v"), 1)

            def bias_a(it, i, W):
                pl, par, qb = UNITS[i]
                if par == 0 and qb == 0:
                    dve.wait_ge(S(f"bias{pl}"), it * 32 + 32)
                return biasA[:, pl, par, SEQ - W:SEQ]
            attention(2, 0, 0, xA, pA, statA, bias_a)

            qz = qzA[:].rearrange("p m c -> p (m c)")
            then(dve.memset(qzA[:], 0.0))
            for r in range(2):
                rows = slice(HD * r, HD * r + HD)
                dst = qz[rows, 32 * r:32 * r + 31 * 65 + 1:65].rearrange("p (t b) -> p t b", t=4)
                dve.tensor_copy(dst, yA[rows, 0:4, SEQ:NT]).then_inc(S("a2_qz"), 1)
            for b in range(NS):
                if b >= 2:
                    dve.wait_ge(S("s_ks"), b - 1)
                dve.tensor_copy(kcA[:, b % 2, :, PAST], yA[:, 4:8, SEQ + b]).then_inc(S("s_kn"), 1)
            dve.wait_ge(S("a2_vt"), 1)
            dve.tensor_copy(vnA[:], PS[0:NS, 4, :]).then_inc(S("a2_pnc"), 1)
            dve.wait_ge(S("s_ks"), NS)
            softmax(0, PS[0:64, 6, 0:NK], psA, sstA)
            dve.tensor_scalar(pdA[:], ident[0:64, 0:64], psA[:, PAST:NK], None, ALU.mult).then_inc(S("a2_pd"), 1)
            dve.wait_ge(S("a2_pn"), 1)
            dve.tensor_copy(pnA[:], PS[0:NS, 5, 0:64]).then_inc(S("a2_pnc"), 1)
            dve.wait_ge(S("a2_o"), 1)
            then(dve.tensor_copy(owA[:], PS[:, 6, 0:64].rearrange("p (t r b) -> p t r b", t=4, r=2)))
            for r in range(2):
                rows = slice(HD * r, HD * r + HD)
                src = PS[rows, 5, 0:64].rearrange("p (t b r) -> p t b r", t=4, r=2)[:, :, :, r]
                dve.tensor_tensor(osA[rows], src, owA[rows, :, r, :], ALU.add).then_inc(S("a2_os"), 1)
            dve.wait_ge(S("a2_oh"), 1)
            dve.tensor_tensor(act_lo[:, 0:4, SEQ:NT], osA[:], act_hi[:, 0:4, SEQ:NT].bitcast(F32),
                              ALU.subtract).then_inc(S("a2_done"), 1)
            dve.wait_ge(S("a2_done"), 1)

            for i in range(2):
                dve.wait_ge(S("g_z"), i + 1)
                then(dve.tensor_scalar(halves(zt[:, i, :]), slot(i), vecs[:, V_GB + i:V_GB + i + 1], None, ALU.add))
                dve.scalar_tensor_tensor(zn[:, i, :], zt[:, i, :], -1.0, zt[:, i, :], ALU.mult,
                                         ALU.min).then_inc(S("g_na"), 1)
            for i in range(2):
                dve.wait_ge(S("g_l"), i + 1)
                then(dve.scalar_tensor_tensor(zt[:, i, :], zt[:, i, :], 0.0, zn[:, i, :], ALU.min, ALU.subtract))
                then(dve.tensor_scalar(zt[:, i, :], zt[:, i, :], 1.0 / 16.0, None, ALU.mult))
                dve.tensor_copy(gs[:, i, :], zt[:, i, SEQ:NT])
                then(dve.tensor_tensor_scan(cum[:, i, :], fresh, zt[:, i, 0:SEQ], 0.0, ALU.mult, ALU.add))
                by_chunk = cum[:, i, :].rearrange("p (c t) -> p c t", t=GC)
                middle = by_chunk[:, :, GC // 2 - 1:GC // 2].to_broadcast([P, NCH, GC])
                dve.tensor_tensor(zn[:, i, 0:SEQ].rearrange("p (c t) -> p c t", t=GC), by_chunk, middle,
                                  ALU.subtract).then_inc(S("g_d"), 1)
            for i in range(2):
                dve.wait_ge(S("g_e2"), i + 1)
                then(dve.tensor_tensor(yA[:, 14 + i, 0:SEQ], yA[:, 14 + i, 0:SEQ], zn[:, i, 0:SEQ], ALU.mult))
                dve.scalar_tensor_tensor(yA[:, 12 + i, 0:SEQ], yA[:, 12 + i, 0:SEQ], HD ** -0.5, zt[:, i, 0:SEQ],
                                         ALU.mult, ALU.mult).then_inc(S("g_qk"), 1)
            then(dve.memset(st[:], 0.0))
            last = zt[:, :, 0:SEQ].rearrange("p i (c t) -> p i c t", t=GC)[:, :, :, GC - 1:GC]
            for i in range(2):
                for h in (2 * i, 2 * i + 1):
                    dve.wait_ge(S("g_a"), h + 1)
                    if h >= 2:
                        dve.wait_ge(S("g_o"), h - 1)
                    grid = att[:, h % 2, :].rearrange("p (c t) -> p c t", t=GC)
                    dve.tensor_tensor(grid, PS[0:GC, h % 2, :].rearrange("p (c t) -> p c t", t=GC),
                                      tri.unsqueeze(1).to_broadcast([GC, NCH, GC]), ALU.mult).then_inc(S("g_am"), 1)
                for c in range(NCH):
                    dve.tensor_scalar(stm[:, i, c, :], st[:, i, :], decay[:, i, 0, c:c + 1], None, ALU.mult)
                    dve.wait_ge(S("g_u"), NCH * i + c + 1)
                    for r in range(2):
                        rows = slice(HD * r, HD * r + HD)
                        upd_r = dve.tensor_scalar(upd[rows, c % 2, :], PS[rows, 6 + c % 2, P * r:P * r + P],
                                                  last[rows, i, c, :], None, ALU.mult)
                        then(upd_r)
                    dve.scalar_tensor_tensor(st[:, i, :], st[:, i, :], decay[:, i, 1, c:c + 1], upd[:, c % 2, :],
                                             ALU.mult, ALU.add).then_inc(S("g_s"), 1)
                    dve.wait_ge(S("g_s"), NCH * i + c + 1)
                for h in (2 * i, 2 * i + 1):
                    dve.wait_ge(S("g_o1"), h + 1)
                    dve.tensor_tensor(yA[:, 16 + h, 0:SEQ], PS[:, 3, :], yA[:, 16 + h, 0:SEQ],
                                      ALU.add).then_inc(S("g_oc"), 1)
            dve.wait_ge(S("g_oc"), 4)

            dve.wait_ge(S("b_out"), 16)
            dve.wait_ge(S("s_t"), 1)
            then(dve.tensor_copy(kt8[:], PS[0:NS, 0, 0:256]))
            then(dve.tensor_copy(vt8[:], PS[0:NS, 1, :]))
            for b in range(NS):
                ins = dve.tensor_scalar(kz8[:, b, :], kt8[:], ident[0:NS, b:b + 1], None, ALU.mult)
            ins.then_inc(S("s_kz"), 2)
            then(dve.memset(qz8[:], 0.0))
            for r in range(2):
                rows = slice(HD * r, HD * r + HD)
                ins = dve.tensor_scalar(qz8[rows, :, :, r], yA[rows, 12:14, SEQ:NT], HD ** -0.5, None, ALU.mult)
                if r == 0:
                    then(ins)
            ins.then_inc(S("s_qz"), 1)
            dve.wait_ge(S("s_in"), 16)
            dve.wait_ge(S("s_eg"), 1)
            for i in range(2):
                then(dve.tensor_tensor(s0[:, :, i, :], s0[:, :, i, :],
                                       eg[:, i, :].unsqueeze(2).to_broadcast([P, NS, P]), ALU.mult))
            for k in range(8):
                i, b0 = k // 4, 2 * (k % 4)
                dve.wait_ge(S("s_kv"), k + 1)
                for r in range(2):
                    rows = slice(HD * r, HD * r + HD)
                    src = PS[rows, k, :].rearrange("p (b c) -> p b c", b=2)[:, :, P * r:P * r + P]
                    dve.tensor_tensor(s0[rows, b0:b0 + 2, i, :], src, s0[rows, b0:b0 + 2, i, :],
                                      ALU.add).then_inc(S("s_new"), 1)
            dve.wait_ge(S("s_o"), 1)
            src = PS[:, 0, 0:32].rearrange("p (i b r) -> p i b r", i=2, b=NS)
            dst = yA[:, 16:20, :].rearrange("p (i r) n -> p i r n", i=2)
            then(dve.tensor_copy(dst[:, :, 0, SEQ:NT], src[:, :, :, 0]))
            dve.tensor_copy(dst[:, :, 1, SEQ:NT], src[:, :, :, 1]).then_inc(S("b_o"), 1)
            for h in range(4):
                o, g = yA[:, 16 + h, :], yA[:, 20 + h, :]
                dve.wait_ge(S("b_rs"), h + 1)
                dve.scalar_tensor_tensor(o, o, vecs[:, V_BO:V_BO + 1], rs[:, h % 2, :], ALU.mult,
                                         ALU.mult).then_inc(S("b_n"), 1)
                dve.wait_ge(S("b_n"), h + 1)
                dve.wait_ge(S("b_e"), h + 1)
                then(dve.tensor_scalar(tmp[:, h % 2, :], tmp[:, h % 2, :], 1.0, None, ALU.add))
                then(dve.reciprocal(tmp[:, h % 2, :], tmp[:, h % 2, :]))
                then(dve.tensor_tensor(g, g, tmp[:, h % 2, :], ALU.mult))
                dve.tensor_tensor(o, o, g, ALU.mult).then_inc(S("b_g"), 1)
                dve.wait_ge(S("b_hi"), h + 1)
                dve.tensor_tensor(act_lo[:, 4 + h, :], o, act_hi[:, 4 + h, :].bitcast(F32),
                                  ALU.subtract).then_inc(S("mix_lo"), 1)
            ffn(0)

            norm(3, V_MIX + KC)
            dve.wait_ge(S("i_wt"), 1)
            dve.tensor_copy(iwt[:], PS[:, 6, 0:4 * NS].rearrange("p (k h) -> p k h", k=4)).then_inc(S("i_w"), 1)
            dve.wait_ge(S("i_w"), 1)
            k = 0
            for qb in range(1, QB):
                W = P * (qb + 1)
                for h in range(NS):
                    dve.wait_ge(S("i_r"), k + 1)
                    if k:
                        dve.wait_ge(S("i_a"), k)
                    sofar = causal[:, SEQ - W:SEQ] if h == 0 else score[:, qb, 0:W]
                    dve.scalar_tensor_tensor(score[:, qb, 0:W], reluC[:, k % 2, 0:W], iwt[:, qb, h:h + 1], sofar,
                                             ALU.mult, ALU.add).then_inc(S("i_a"), 1)
                    k += 1
            dve.wait_ge(S("i_a"), k)
            rounds = [0]

            def top(values, spare, best, n):
                def one(src, done):
                    waits_done()
                    dve.max(best, src).then_inc(S("k_c"), 1)
                    dve.wait_ge(S("k_c"), done + 1)
                    waits_done()
                    dve.match_replace(spare, best, src, GONE).then_inc(S("k_c"), 1)
                    dve.wait_ge(S("k_c"), done + 2)
                at = rounds[0]
                one(values, at)
                with dve.Fori(1, n // 8) as j:
                    one(spare, j * 2 + at)
                rounds[0] = at + n // 8 * 2
                then(dve.tensor_tensor(spare, spare, values, ALU.is_equal))

            for qb in range(1, QB):
                W = P * (qb + 1)
                top(score[:, qb, 0:W], work[:, 0:W], top8[:], TOPK_P)
                dve.tensor_scalar(score[:, qb, 0:W], work[:, 0:W], NEG, None, ALU.mult).then_inc(S("topk"), 1)
                dve.wait_ge(S("topk"), qb)
            dve.tensor_copy(score[:, 0, 0:P], causal[:, SEQ - P:SEQ]).then_inc(S("topk"), 1)

            for kb in range(QB):
                dve.wait_ge(S("C_vt"), kb + 1)
                dve.tensor_copy(vtokC[:, kb, :], PS[:, 4 + kb, 0:256]).then_inc(S("C_vtc"), 1)

            dve.wait_ge(S("hn_ok"), 19 + 2)
            dve.tensor_copy(ikc[:, :, PAST], yC[:, 4, SEQ:NT]).then_inc(S("d_z"), 1)
            then(dve.memset(iqz[:], 0.0))
            then(dve.memset(iwz[:], 0.0))
            then(dve.memset(qzC[:], 0.0))
            by_par = iqz[:].rearrange("p b (t r) -> p r t b", r=2)
            for r in range(2):
                rows = slice(HD * r, HD * r + HD)
                ins = dve.tensor_copy(by_par[rows, r], yC[rows, 0:4, SEQ:NT])
                if r == 0:
                    then(ins)
            ins.then_inc(S("d_z"), 1)
            diagonal = iwz[:].rearrange("h b c -> h (b c)")[:, 0:NS * NS:NS + 1]
            dve.tensor_copy(diagonal, yC[0:NS, 5, SEQ:NT]).then_inc(S("d_z"), 1)
            for T in range(2):
                for r in range(2):
                    rows = slice(HD * r, HD * r + HD)
                    cols = qzC[rows, T * NS:(T + 1) * NS, :].rearrange("p b c -> p (b c)")
                    for t in range(4 * T, 4 * T + 4):
                        c0 = 64 * r + NS * t
                        ins = dve.tensor_copy(cols[:, c0:c0 + 7 * 129 + 1:129], yC[rows, 10 + t, SEQ:NT])
                    ins.then_inc(S("d_qz"), 1)

            def bias_c(it, i, W):
                dve.wait_ge(S("C_bm"), it * NU + (bias_c.base + i + 1))
                return bmC[:, i % 2, 0:W]
            for T in range(2):
                bias_c.base = 32 * T
                attention(2, 32 * (T + 1), 4 * T, xC, pC, statC, bias_c)

            for b in range(2):
                dve.tensor_copy(kcC[:, b, :, PAST], yC[:, 6:8, SEQ + b]).then_inc(S("s_kn"), 1)
            dve.wait_ge(S("d_a"), NS)
            then(dve.tensor_copy(sc8[:], PS[0:NS, 5, 0:NK]))
            top(sc8[:], wk8[:], mx8[:], TOPK_S)
            dve.tensor_scalar(sc8[:], wk8[:], NEG, None, ALU.mult).then_inc(S("d_mask"), 1)
            for b in range(2, NS):
                dve.wait_ge(S("s_ks"), NS + b - 1)
                dve.tensor_copy(kcC[:, b % 2, :, PAST], yC[:, 6:8, SEQ + b]).then_inc(S("s_kn"), 1)
            dve.wait_ge(S("d_vt"), 1)
            dve.tensor_copy(vnC[:], PS[0:NS, 6, 0:256]).then_inc(S("d_vtc"), 1)
            dve.wait_ge(S("s_ks"), 2 * NS)
            softmax(1, PS[:, 4, 0:NK], psC, sstC)
            dve.tensor_scalar(pdC[:], ident, psC[:, PAST:NK], None, ALU.mult).then_inc(S("d_pd"), 1)
            dve.wait_ge(S("d_pn"), 1)
            dve.tensor_copy(pnC[:], PS[0:NS, 6, 256:256 + P]).then_inc(S("d_pnc"), 1)
            dve.wait_ge(S("d_o"), 1)
            for T in range(2):
                for r in range(2):
                    rows = slice(HD * r, HD * r + HD)
                    src = PS[rows, 4, 64 * T:64 * T + 64].rearrange("p (r t b) -> p r t b", r=2, t=4)[:, r]
                    then(dve.tensor_copy(owC[rows, 4 * T:4 * T + 4, :], src))
                    src = PS[rows, 5, 0:P].rearrange("p (b T r t) -> p T r t b", b=NS, T=2, r=2)[:, T, r]
                    dve.tensor_tensor(osC[rows, 4 * T:4 * T + 4, :], src, owC[rows, 4 * T:4 * T + 4, :],
                                      ALU.add).then_inc(S("d_os"), 1)
            dve.wait_ge(S("d_oh"), 1)
            dve.tensor_tensor(act_lo[:, :, SEQ:NT], osC[:], act_hi[:, :, SEQ:NT].bitcast(F32),
                              ALU.subtract).then_inc(S("mix_lo"), 1)
            ffn(1)


def bucket(dist):
    n = np.maximum(dist, 0)
    exact = NB // 2
    nf = np.maximum(n, exact).astype(np.float32)
    large = exact + (np.log(nf / np.float32(exact)) / np.float32(math.log(2048 / exact))
                     * np.float32(exact)).astype(np.int32)
    return np.where(n < exact, n, np.minimum(large, NB - 1))


def one_hots():
    def columns(dist, dilated):
        out = np.zeros((NB + 1, len(dist)), np.float32)
        out[bucket(dist), np.arange(len(dist))] = 1
        if dilated:
            count = sum(((dist >= 0) & (dist <= w) & (dist % d == 0)).astype(int)
                        for w, d in ((128, 1), (512, 4), (2048, 16)))
            out[NB] = np.where(count > 0, np.log(np.maximum(count, 1)), NEG)
        return out
    by_row, by_key = SEQ - 1 - np.arange(RW), PAST - np.arange(NK)
    return np.concatenate([columns(by_row, True), columns(by_row, False),
                           columns(by_key, True), columns(by_key, False)], axis=1)


def constants():
    c = np.zeros((P, NKC), np.float32)
    p = np.arange(P)
    c[:, K_ID:K_ID + P] = np.eye(P)
    c[:, K_O2:K_O2 + P] = p[:, None] // HD == p[None, :] // HD
    c[:, K_ON:K_ON + P] = 1
    c[:, K_CA:K_CA + SEQ] = np.where(np.arange(SEQ)[None, :] - (SEQ - P) <= p[:, None], 0.0, NEG)
    c[:, K_FR:K_FR + SEQ] = np.arange(SEQ) % GC != 0
    c[:GC, K_TR:K_TR + GC] = np.arange(GC)[:, None] <= np.arange(GC)[None, :]
    c[:, K_RS:K_RS + NS] = p[:, None] % NS == np.arange(NS)[None, :]
    return c


def features(t):
    return t.T.reshape(-1, P, t.shape[0]).transpose(1, 0, 2)


C_ORDER = [4 * (2 * (t // 4) + r) + t % 4 for t in range(8) for r in range(2)]


def kernel(**inputs):
    import concourse.bacc as _bacc
    from concourse.bass_utils import run_bass_kernel_spmd as _run

    i = {k: np.asarray(v) for k, v in inputs.items()}
    f32 = np.float32

    def blocks(w):
        k, m = w.shape
        pad = np.zeros((k, -m % P), f32)
        w = np.concatenate([w, pad], axis=1)
        return w.reshape(k // P, P, -1, P).transpose(2, 1, 0, 3).reshape(-1, P, k)

    w_ab, w_c = i["w_in_ab"][0], i["w_in_c"][0]
    ab = np.concatenate([w_ab[:, 0:2560], w_ab[:, 2576:3088], w_ab[:, 2560:2576]], axis=1)
    cq = w_c[:, 0:1024].reshape(DM, 16, HD)[:, C_ORDER].reshape(DM, 1024)
    ik = w_c[:, 2048:2112]
    iw = np.concatenate([w_c[:, 2112:2120], np.zeros((DM, P - NS), f32)], axis=1)
    c = np.concatenate([w_c[:, 1536:2048], ik, ik, iw, w_c[:, 1024:1536], cq], axis=1)
    out_c = i["w_out_c"][0].reshape(16, HD, DM)[C_ORDER].reshape(1024, DM)
    stream = []
    for l, parts in ((0, (ab, i["w_out_ab"][0])), (1, (c, out_c))):
        stream += [blocks(w) for w in parts]
        up = np.stack([blocks(i["w_ff1"][l]), blocks(i["w_ff3"][l])], axis=1)
        down = np.concatenate([i["w_ff2"][l], np.zeros((3 * DM - DFF, DM), f32)], axis=0)
        stream += [up.reshape(-1, P, DM),
                   blocks(down).reshape(KC, P, 3, DM).transpose(0, 2, 1, 3).reshape(-1, P, DM),
                   blocks(i["w_ple_proj"][l]).reshape(2, 4, P, 256).transpose(0, 2, 1, 3).reshape(2, P, DM),
                   blocks(i["w_ple_gate"][l])]
    stream.append(np.zeros((1, P, DM), f32))
    w = np.concatenate(stream, axis=0)

    def both(v):
        return np.concatenate([v, v])[:, None]

    by_chunk = [i[n][l].reshape(KC, P).T for n in ("g_mix", "g_ffn", "g_ple") for l in range(2)]
    norms = ([both(i["a_q_norm"][0])] * 4 + [both(i["a_k_norm"][0])] * 4 + [both(i["c_ik_norm"][0])]
             + [both(i["c_k_norm"][0])] * 2 + [both(i["c_q_norm"][0])] * 8)
    vecs = np.concatenate(by_chunk + norms + [
        i["b_out_norm"][0][:, None], i["b_gate_b"][0].reshape(2, P).T, np.full((P, 1), EPS, f32),
        np.ones((P, 1), f32)], axis=1)

    rel = i["rel_bias"]
    a_rows = [2 * (r // NS % 4) + r // 32 for r in range(64)]
    c_rows = [C_ORDER[2 * (r // NS % 8) + r // 64] for r in range(P)]
    bias = np.concatenate([rel[:, 0:8], rel, rel[:, a_rows], rel[:, c_rows]], axis=1)
    bias = np.concatenate([bias, np.ones((1, bias.shape[1]), f32)], axis=0)

    k_cache = i["cache_a_k"][0].reshape(NS, PAST, 4, P).transpose(0, 3, 2, 1)
    v_cache = i["cache_a_v"][0].reshape(NS, 2, P, 512).transpose(0, 2, 1, 3)
    state = i["state_b"][0].reshape(NS, 2, P, P).transpose(2, 0, 1, 3)
    arrays = {
        "w": w,
        "xT": features(np.concatenate([i["x_prompt"][0], i["x_sample"][:, 0]], axis=0)),
        "pT": np.stack([features(np.concatenate([i["p_prompt"][l, 0], i["p_sample"][l, :, 0]], axis=0))
                        for l in range(2)]),
        "consts": constants(),
        "colsel": constants()[:, K_RS:K_RS + NS].T,
        "vecs": vecs,
        "gate_w2": i["b_gate_w2"][0],
        "bias_rows": bias,
        "onehots": one_hots(),
        "cache_k": k_cache,
        "cache_v": v_cache,
        "state": state,
        "pool_k": i["cache_c_k"][0].reshape(-1, P, 2, P).transpose(0, 3, 2, 1),
        "pool_v": i["cache_c_v"][0].reshape(-1, P, 256),
        "pool_ik": i["cache_c_ik"][0].transpose(0, 2, 1),
        "pages": i["page_table"].reshape(1, 16),
    }
    arrays = {k: np.ascontiguousarray(v) for k, v in arrays.items()}
    outs = {"y": (P, KC, NT), "a_k": (P, 4, NT), "a_v": (P, 4, NT), "b_state": (P, 2, P),
            "s_state": (P, NS, 2, P), "c_k": (P, 2, NT), "c_v": (P, 2, NT), "c_ik": (HD, NT)}

    nc = _bacc.Bacc("TRN2", target_bir_lowering=False, num_devices=1)
    tensors = {k: nc.dram_tensor("in_" + k, v.shape, mybir.dt.from_np(v.dtype), kind="ExternalInput").ap()
               for k, v in arrays.items()}
    for k, shape in outs.items():
        tensors[k] = nc.dram_tensor("out_" + k, shape, F32, kind="ExternalOutput").ap()
    tensors["rows"] = nc.dram_tensor("scratch_rows", (24, 2, RW), F32, kind="Internal").ap()
    build(nc, tensors)
    r = _run(nc, [{"in_" + k: v for k, v in arrays.items()}], core_ids=[0]).results[0]

    def tokens(t):
        t = t.transpose(1, 0, 2).reshape(-1, t.shape[2])
        return t[:, 0:SEQ].T, t[:, SEQ:NT].T

    (yp, ys), (ak, sak), (av, sav) = tokens(r["out_y"]), tokens(r["out_a_k"]), tokens(r["out_a_v"])
    (ck, sck), (cv, scv) = tokens(r["out_c_k"]), tokens(r["out_c_v"])
    cik, scik = r["out_c_ik"][:, 0:SEQ].T, r["out_c_ik"][:, SEQ:NT].T
    return (yp[None], ys[:, None],
            ak.reshape(1, 1, SEQ, 8, HD), av.reshape(1, 1, SEQ, 8, HD),
            r["out_b_state"].transpose(1, 0, 2).reshape(1, 1, 4, HD, P),
            ck.reshape(1, 1, SEQ, 4, HD), cv.reshape(1, 1, SEQ, 4, HD), cik.reshape(1, 1, SEQ, HD),
            sak.reshape(1, NS, 1, 8, HD), sav.reshape(1, NS, 1, 8, HD),
            r["out_s_state"].transpose(1, 2, 0, 3).reshape(1, NS, 4, HD, P),
            sck.reshape(1, NS, 1, 4, HD), scv.reshape(1, NS, 1, 4, HD), scik.reshape(1, NS, 1, HD))
```

```python
import math
from contextlib import ExitStack

import numpy as np
import concourse.bass as bass
from concourse import mybir
from concourse.alu_op_type import AluOpType as ALU

F32 = mybir.dt.float32
F32R = mybir.dt.float32r
I32 = mybir.dt.int32
ACT = mybir.ActivationFunctionType
AX = mybir.AxisListType

P = 128
DM, KC = 1024, 8
SEQ, NS = 512, 8
NT = SEQ + NS
HALF = NT // 2
DFF, FC = 2816, 22
DPLE = 256
HD = 64
NB = 32
PAST = 256
NK = PAST + 1
QB = SEQ // P
NEG = -1.0e30
GONE = -3.0e38
EPS = 1e-6
GC = 64
NCH = SEQ // GC
TOPK_P, TOPK_S = 128, 64
RW = 640

AB_BLOCKS = 25
C_BLOCKS = 18
B_AB = 0
B_OUT0 = B_AB + AB_BLOCKS
B_FF0 = B_OUT0 + KC
B_D0 = B_FF0 + 2 * FC
B_PR0 = B_D0 + 3 * KC
B_G0 = B_PR0 + 2
B_C = B_G0 + KC
B_OUT1 = B_C + C_BLOCKS
B_FF1 = B_OUT1 + KC
B_D1 = B_FF1 + 2 * FC
B_PR1 = B_D1 + 3 * KC
B_G1 = B_PR1 + 2
N_BLOCKS = B_G1 + KC

Y_BQ, Y_BK, Y_BV, Y_V, Y_BG, Y_Q, Y_K = 0, 2, 4, 8, 12, 16, 20

V_MIX, V_FFN, V_PLE, V_NG = 0, 16, 32, 48
N_NG = 19
V_BO, V_GB, V_EPS, V_ONE = 67, 68, 70, 71
NV = 72
K_ID, K_O2, K_ON, K_CA, K_FR, K_TR, K_RS = 0, 128, 256, 384, 896, 1408, 1472
NKC = 1480

N_POOL = 20

R_A, R_C, R_SA, R_SC = 0, 8, 24, 88
O_A, O_C, O_SA, O_SC = 0, RW, 2 * RW, 2 * RW + NK
N_ONE = 2 * RW + 2 * NK


def build(nc, a):
    ctx = ExitStack()

    def sb(name, shape, dt=F32, scope=None):
        return (scope or ctx).enter_context(nc.sbuf_tensor(name, shape, dt))

    sems = {}

    def S(name):
        if name not in sems:
            sems[name] = ctx.enter_context(nc.semaphore(name))
        return sems[name]

    with ctx:
        x = sb("x", [P, KC, NT])
        act_hi = sb("act_hi", [P, KC, NT], F32R)
        act_lo = sb("act_lo", [P, KC, NT], F32R)
        w_raw = sb("w_raw", [P, 2, DM])
        w_hi = sb("w_hi", [P, 2, DM], F32R)
        w_lo = sb("w_lo", [P, 2, DM], F32R)
        vecs = sb("vecs", [P, NV])
        const = sb("const", [P, NKC])
        ident = const[:, K_ID:K_ID + P]
        ones2 = const[:, K_O2:K_O2 + P]
        ones = const[:, K_ON:K_ON + P]
        causal = const[:, K_CA:K_CA + SEQ]
        fresh = const[:, K_FR:K_FR + SEQ]
        tri = const[:, K_TR:K_TR + GC]
        rowsel = const[:, K_RS:K_RS + NS]
        colsel = sb("colsel", [NS, P])
        sqsum = sb("sqsum", [P, NT])
        sq = sb("sq", [P, 2, NT])
        rs = sb("rs", [P, 2, NT])
        tmp = sb("tmp", [P, 2, NT])
        bmC = sq[:, :, 0:SEQ]
        pt = tmp[:, :, 0:SEQ]
        normed_place = (tmp[:, 0, :], tmp[:, 1, :], sq[:, 0, :], sq[:, 1, :])
        gains = sb("gains", [P, N_NG])

        sA = ExitStack()
        yA = sb("yA", [P, AB_BLOCKS - 1, NT], scope=sA)
        blr = sb("blr", [16, NT], scope=sA)
        gs = sb("gs", [P, 2, NS], scope=sA)
        gw2 = sb("gw2", [16, 256], scope=sA)
        qz8 = sb("qz8", [P, 2, NS, 2], scope=sA)
        s0 = sb("s0", [P, NS, 2, P], scope=sA)
        sA0 = ExitStack()
        orow = sb("orow", [33, N_ONE], scope=sA0)
        brow = sb("brow", [33, 216], scope=sA0)
        rrow = sb("rrow", [16, 2, RW], scope=sA0)
        sA0.close()
        sAK = ExitStack()
        kcA = sb("kcA", [P, 2, 4, NK], scope=sAK)
        vcA = sb("vcA", [P, 2, 2, 512], scope=sAK)
        sbA = sb("sbA", [33, 64 + NK], scope=sAK)
        sA1 = ExitStack()
        biasA = sb("biasA", [P, 2, 2, SEQ], scope=sA1)
        q_hiA = sb("q_hiA", [P, 2, SEQ], F32R, scope=sA1)
        q_loA = sb("q_loA", [P, 2, SEQ], F32R, scope=sA1)
        vstA = sb("vstA", [P, 2, QB, P], scope=sA1)
        vtokA = sb("vtokA", [P, QB, 512], scope=sA1)
        xA = sb("xA", [P, 2, SEQ], scope=sA1)
        pA = sb("pA", [P, 2, SEQ], scope=sA1)
        statA = sb("statA", [P, 2, 4], scope=sA1)
        sA1.close()
        sA2 = ExitStack()
        kcA2 = sb("kcA2", [P, 2, 4, NK], scope=sA2)
        vcA2 = sb("vcA2", [P, 2, 2, 512], scope=sA2)
        qzA = sb("qzA", [P, 32, 64], scope=sA2)
        psA = sb("psA", [64, NK], scope=sA2)
        ptsA = sb("ptsA", [P, 2, 64], scope=sA2)
        sstA = sb("sstA", [64, 4], scope=sA2)
        pdA = sb("pdA", [64, 64], scope=sA2)
        pnA = sb("pnA", [NS, 64], scope=sA2)
        vnA = sb("vnA", [NS, 512], scope=sA2)
        osA = sb("osA", [P, 4, NS], scope=sA2)
        owA = sb("owA", [P, 4, 2, NS], scope=sA2)
        sA2.close()
        sAK.close()
        s0_flat = s0[:].rearrange("p b i e -> p (b i e)").rearrange("p (b k d) -> p b k d", b=2, k=2)

        def key_place(b):
            return (kcA, kcA2)[b % 4 // 2][:, b % 2]

        def value_place(b):
            return (vcA, s0_flat, vcA2)[b % 6 // 2][:, b % 2]

        sA3 = ExitStack()
        zt = sb("zt", [P, 2, NT], scope=sA3)
        zn = sb("zn", [P, 2, NT], scope=sA3)
        cum = sb("cum", [P, 2, SEQ], scope=sA3)
        decay = sb("decay", [P, 2, 2, NCH], scope=sA3)
        kbt = sb("kbt", [P, 2, NCH, HD], scope=sA3)
        vb = sb("vb", [P, NCH, 2, P], scope=sA3)
        att = sb("att", [P, 2, SEQ], scope=sA3)
        st = sb("st", [P, 2, P], scope=sA3)
        stm = [t[:].rearrange("p i n -> p (i n)")[:, 0:NCH * P].rearrange("p (c e) -> p c e", c=NCH)
               for t in (zn, cum)]
        upd = sb("upd", [P, 2, P], scope=sA3)
        sA4 = ExitStack()
        eg = sb("eg", [P, 2, NS], scope=sA4)
        kt8 = sb("kt8", [NS, 256], scope=sA4)
        vt8 = sb("vt8", [NS, 512], scope=sA4)
        kz8 = sb("kz8", [NS, NS, 256], scope=sA4)
        sA4.close()
        sA3.close()
        sA.close()

        sC = ExitStack()
        yC = sb("yC", [P, C_BLOCKS, NT], scope=sC)
        vtokC = sb("vtokC", [P, QB, 256], scope=sC)
        iwt = sb("iwt", [P, QB, NS], scope=sC)
        score = sb("score", [P, QB, SEQ], scope=sC)
        biasC = sb("biasC", [P, 2, 2, SEQ], scope=sC)
        q_hiC = sb("q_hiC", [P, 2, SEQ], F32R, scope=sC)
        q_loC = sb("q_loC", [P, 2, SEQ], F32R, scope=sC)
        workC = sb("workC", [P, SEQ], scope=sC)
        xC = sb("xC", [P, 2, SEQ], scope=sC)
        pC = sb("pC", [P, 2, SEQ], scope=sC)
        statC = sb("statC", [P, 2, 4], scope=sC)
        ptab = sb("ptab", [1, 16], I32, scope=sC)
        iqz = sb("iqz", [P, NS, NS], scope=sC)
        iwz = sb("iwz", [NS, NS, NS], scope=sC)
        rel8 = sb("rel8", [NS, 2, NK], scope=sC)
        sc8 = sb("sc8", [NS, NK], scope=sC)
        wk8 = sb("wk8", [NS, NK], scope=sC)
        mx8 = sb("mx8", [NS, 8], scope=sC)
        qzC = sb("qzC", [P, 16, P], scope=sC)
        kcC = sb("kcC", [P, 4, 2, NK], scope=sC)
        vcC = sb("vcC", [P, 4, 2, 256], scope=sC)
        sbC = sb("sbC", [33, P + NK], scope=sC)
        top8 = sb("top8", [P, QB, 8], scope=sC)
        work = (None, xC[:, 0, :], xC[:, 1, :], workC[:])
        reluC = pC
        sC0 = ExitStack()
        ikc = sb("ikc", [P, NS, NK], scope=sC0)
        sC0.close()
        psC = sb("psC", [P, NK], scope=sC)
        ptsC = sb("ptsC", [P, 2, P], scope=sC)
        sstC = sb("sstC", [P, 4], scope=sC)
        pdC = sb("pdC", [P, P], scope=sC)
        pnC = sb("pnC", [NS, P], scope=sC)
        vnC = sb("vnC", [NS, 256], scope=sC)
        osC = sb("osC", [P, 8, NS], scope=sC)
        owC = sb("owC", [P, 8, NS], scope=sC)
        sC.close()

        sP = ExitStack()
        pp = sb("pp", [P, KC, NT], scope=sP)
        sP.close()
        h_hi = sb("h_hi", [P, FC, NT], F32R)
        h_lo = sb("h_lo", [P, FC, NT], F32R)
        p_raw = sb("p_raw", [P, 2, NT])
        p_hi = sb("p_hi", [P, 2, NT], F32R)
        p_lo = sb("p_lo", [P, 2, NT], F32R)
        PS = ctx.enter_context(nc.psum_tensor("PS", [P, 8, 512], F32))

        def halves(t):
            return t.rearrange("p (h n) -> p h n", h=2)

        def slot(s):
            return PS[:, 2 * s:2 * s + 2, 0:HALF]

        UNITS = [(pl, par, qb) for pl in range(2) for par in range(2) for qb in range(QB)]
        NU = len(UNITS)
        LAYERS = (
            dict(out=B_OUT0, ff=B_FF0, down=B_D0, proj=B_PR0, gate=B_G0),
            dict(out=B_OUT1, ff=B_FF1, down=B_D1, proj=B_PR1, gate=B_G1),
        )
        FREE_V = 8 + 2 * FC + 8 + 8 + 8

        IN = (
            dict(b0=B_AB, y=yA, n=AB_BLOCKS, shift=-1, normed=((17, 25, 0),),
                 order=((0,), (1, 9), *((n,) for n in range(9, AB_BLOCKS)))),
            dict(b0=B_C, y=yC, n=C_BLOCKS, shift=0, normed=((4, 5, 8), (6, 8, 9), (10, 18, 11)),
                 order=((0, 4), *((n,) for n in range(4, C_BLOCKS)))),
        )

        def walk(eng, l, body, between=None):
            for part in IN[l]["order"]:
                if between:
                    between(part[0])
                if len(part) == 1:
                    body(part[0], part[0])
                else:
                    with eng.Fori(part[0], part[1] - 1, 2) as j:
                        for u in range(2):
                            body(j + u, part[0] + u)

        def normed(l, n, like):
            for first, past, q in IN[l]["normed"]:
                if first <= like < past:
                    return n + (q - first)
            return None

        block = ctx.enter_context(nc.Block())

        @block.sync
        def _(sp):
            for n in range(4):
                sp.dma_start(x[:, 2 * n:2 * n + 2, :], a["xT"][:, 2 * n:2 * n + 2, :]).then_inc(S(f"x_in{n}"), 16)
            sp.dma_start(const[:], a["consts"]).then_inc(S("tables_in"), 16)
            sp.dma_start(vecs[:], a["vecs"]).then_inc(S("tables_in"), 16)
            sp.dma_start(colsel[:], a["colsel"]).then_inc(S("tables_in"), 16)
            sp.dma_start(gw2[:], a["gate_w2"]).then_inc(S("tables_in"), 16)
            sp.dma_start(brow[:], a["bias_rows"]).then_inc(S("tables_in"), 16)
            sp.dma_start(orow[:], a["onehots"]).then_inc(S("tables_in"), 16)
            for b in range(2):
                sp.dma_start(w_raw[:, b, :], a["w"][b]).then_inc(S(f"w_raw{b}"), 16)

            def weights(b0, b1):
                def one(b, s):
                    sp.wait_ge(S("w_lo"), b - 1)
                    sp.dma_start(w_raw[:, s, :], a["w"][b]).then_inc(S(f"w_raw{s}"), 16)
                n = (b1 - b0) // 2
                if n:
                    with sp.Fori(0, n) as j:
                        for u in range(2):
                            one(j * 2 + (b0 + u), (b0 + u) % 2)
                if 2 * n < b1 - b0:
                    one(b1 - 1, (b1 - 1) % 2)

            def pair_biases(pair0, pairs, dst, rows):
                for p in pairs:
                    sp.wait_ge(S("t_o"), pair0 + p + 1)
                    for par in range(2):
                        h = rows(p, par)
                        src = bass.AP(tensor=a["rows"].tensor, offset=2 * h * RW + P - 1,
                                      ap=[[RW - P // 2, 2], [-1, P // 2], [1, SEQ]])
                        sp.dma_start(dst[:, p % 2, par, :], src).then_inc(S(f"bias{p % 2}"), 16)

            weights(2, 8)
            sp.wait_ge(S("rrow_ok"), 4)
            for copy in range(2):
                sp.dma_start(a["rows"][0:8, copy, :], rrow[0:8, 0, :]).then_inc(S("rows_out"), 16)
                sp.dma_start(a["rows"][8:24, copy, :], rrow[0:16, 1, :]).then_inc(S("rows_out"), 16)
            weights(8, B_OUT0 - 2)
            sp.wait_ge(S("rows_out"), 64)
            sp.wait_ge(S("g_oc"), 4)
            pair_biases(0, (0, 1), biasA, lambda p, par: 2 * p + par)
            sp.dma_start(sbA[:, 0:64], a["bias_rows"][:, R_SA:R_SA + 64]).then_inc(S("a2_bias"), 16)
            sp.dma_start(sbA[:, 64:64 + NK], a["onehots"][:, O_SA:O_SA + NK]).then_inc(S("a2_bias"), 16)
            weights(B_OUT0 - 2, B_OUT0 + 2)

            def keys_a(b):
                sp.dma_start(key_place(b)[:, :, 0:PAST], a["cache_k"][b]).then_inc(S(f"keys{b % 4}"), 16)

            def values_a(b):
                sp.dma_start(value_place(b), a["cache_v"][b]).then_inc(S(f"values{b % 6}"), 16)

            for b in range(2):
                keys_a(b)
                values_a(b)
            sp.wait_ge(S("b_o"), 1)
            sp.wait_ge(S("s_out"), 16)
            values_a(2)
            values_a(3)
            pair_biases(0, (2, 3), biasA, lambda p, par: 2 * p + par)
            sp.wait_ge(S("t_o"), 4 + 2)
            for b in range(2, NS):
                if b >= 4:
                    sp.wait_ge(S("s_ks"), b - 3)
                keys_a(b)
                if b in (4, 5):
                    values_a(b)
            for b in (6, 7):
                sp.wait_ge(S("s_vs"), b - 5)
                values_a(b)
            weights(B_OUT0 + 2, B_C + 2)

            sp.wait_ge(S("x_new"), KC)
            sp.dma_start(ptab[:], a["pages"]).then_inc(S("d_tab"), 16)
            sp.dma_start(sbC[:, 0:P], a["bias_rows"][:, R_SC:R_SC + P]).then_inc(S("d_bias"), 16)
            sp.dma_start(sbC[:, P:P + NK], a["onehots"][:, O_SC:O_SC + NK]).then_inc(S("d_bias"), 16)
            sp.wait_ge(S("d_tab"), 16)

            def page(b, n):
                return sp.value_load(ptab[0:1, 2 * b + n:2 * b + n + 1], min_val=0, max_val=N_POOL - 1)

            def index_pages(b):
                for n in range(2):
                    pg = page(b, n)
                    for r in range(2):
                        sp.dma_start(ikc[HD * r:HD * r + HD, b, n * P:(n + 1) * P],
                                     a["pool_ik"][pg]).then_inc(S("d_ik"), 16)

            def key_pages(b):
                for n in range(2):
                    sp.dma_start(kcC[:, b % 4, :, n * P:(n + 1) * P],
                                 a["pool_k"][page(b, n)]).then_inc(S(f"keys{b % 4}"), 16)

            def value_pages(b):
                for n in range(2):
                    sp.dma_start(vcC[:, b % 4, n, :], a["pool_v"][page(b, n)]).then_inc(S(f"values{b % 4}"), 16)

            for b in range(NS):
                weights(B_C + 2 + b, B_C + 3 + b)
                index_pages(b)
            for b in range(4):
                weights(B_C + 2 + NS + b, B_C + 3 + NS + b)
                key_pages(b)
                value_pages(b)
            weights(B_C + 2 + NS + 4, B_OUT1 + 2)
            rows_c = lambda p, par: 8 + 4 * (2 * (p // 4) + par) + p % 4
            pair_biases(4, range(2), biasC, rows_c)
            for b in range(4, NS):
                sp.wait_ge(S("s_ks"), NS + b - 3)
                key_pages(b)
            pair_biases(4, range(2, 8), biasC, rows_c)
            for b in range(4, NS):
                sp.wait_ge(S("s_vs"), NS + b - 3)
                value_pages(b)
            weights(B_OUT1 + 2, N_BLOCKS + 2)
            for m in range(KC):
                sp.wait_ge(S("x_new"), KC + m + 1)
                sp.dma_start(a["y"][:, m, :], x[:, m, :]).then_inc(S("y_out"), 16)
            sp.wait_ge(S("y_out"), 16 * KC)

        @block.gpsimd
        def _(pool):
            def low(b, s):
                pool.wait_ge(S("w_hi"), b + 1)
                pool.tensor_tensor(w_lo[:, s, :], w_raw[:, s, :], w_hi[:, s, :].bitcast(F32),
                                   ALU.subtract).then_inc(S("w_lo"), 1)

            def blocks(b0, n):
                with pool.Fori(0, n - 1, 2) as j:
                    for u in range(2):
                        low(j + (b0 + u + 2), (b0 + u) % 2)

            def norm_mul(l, q, s, n):
                y, n = IN[l]["y"], n + IN[l]["shift"]
                pool.wait_ge(S("hn_rs"), q + 1)
                pool.tensor_tensor(y[:, bass.ds(n, 1), :], y[:, bass.ds(n, 1), :], rs[:, s:s + 1, :],
                                   ALU.mult).then_inc(S("hn_ok"), 1)

            def products_in(l):
                b0 = IN[l]["b0"]

                def body(n, like):
                    low(n + (b0 + 2), (b0 + like) % 2)
                    q = normed(l, n - 1, like - 1)
                    if q is not None:
                        norm_mul(l, q, normed(l, like - 1, like - 1) % 2, n - 1)
                walk(pool, l, body)
                last = IN[l]["n"] - 1
                q = normed(l, last, last)
                if q is not None:
                    norm_mul(l, q, q % 2, last)

            def norm_lo(k):
                for c in range(0, KC, 2):
                    pool.wait_ge(S("n_hi"), KC * k + c + 1)
                    pool.tensor_tensor(act_lo[:, c, :], normed_place[c % 4], act_hi[:, c, :].bitcast(F32),
                                       ALU.subtract).then_inc(S("n_lo_even"), 1)

            def ffn(l):
                L = LAYERS[l]
                blocks(L["out"], KC)
                norm_lo(3 * l + 1)
                pool.wait_ge(S("p_hi"), l + 1)
                pool.tensor_tensor(p_lo[:], p_raw[:], p_hi[:].bitcast(F32), ALU.subtract).then_inc(S("p_lo"), 1)
                blocks(L["ff"], 2 * FC)
                blocks(L["down"], 3 * KC)
                low(L["proj"] + 2, L["proj"] % 2)
                norm_lo(3 * l + 2)
                low(L["proj"] + 3, (L["proj"] + 1) % 2)
                blocks(L["gate"], KC)

            pool.sem_inc(S("hn_ok"), 2)
            low(0, 0)
            low(1, 1)
            norm_lo(0)
            products_in(0)
            pool.wait_ge(S("s_new"), 4)
            pool.wait_ge(S("b_out"), 16)

            def split(hi, lo, t, signal, k):
                pool.tensor_copy(hi, t).then_inc(S("A_hi"), 1)
                pool.wait_ge(S("A_hi"), k)
                pool.tensor_tensor(lo, t, hi.bitcast(F32), ALU.subtract).then_inc(S(signal), 1)

            for pair in range(4):
                pl = pair % 2
                pool.wait_ge(S("t_o"), pair + 1)
                if pair >= 2:
                    split(act_hi[:, 4 + pl, 0:SEQ], act_lo[:, 4 + pl, 0:SEQ], yA[:, Y_K + pair, 0:SEQ],
                          "k_split", 2 * pair - 1)
                split(q_hiA[:, pl, :], q_loA[:, pl, :], yA[:, Y_Q + pair, 0:SEQ], "A_st", (1, 2, 4, 6)[pair])
                pool.wait_ge(S("A_v"), 4)
                pool.tensor_copy(vstA[:, pl, :, :], vtokA[:, :, pair * P:(pair + 1) * P]).then_inc(S("A_st"), 1)
            ffn(0)
            norm_lo(3)
            products_in(1)
            pool.wait_ge(S("t_o"), 6)
            for T in range(2):
                with pool.Fori(0, 2) as it:
                    def place_q(pl):
                        pool.wait_ge(S("t_s"), it * NU + (32 * T + 8 * pl + 24))
                        q = yC[:, bass.ds(it * 2 + (4 * T + pl + 10), 1), 0:SEQ]
                        pool.tensor_copy(q_hiC[:, pl:pl + 1, :], q).then_inc(S("C_st"), 1)
                        pool.wait_ge(S("C_st"), it * 4 + (8 * T + 2 * pl + 1))
                        pool.sem_inc(S("waits_done"), 1)
                        pool.tensor_tensor(q_loC[:, pl:pl + 1, :], q, q_hiC[:, pl:pl + 1, :].bitcast(F32),
                                           ALU.subtract).then_inc(S("C_st"), 1)

                    for i, (pl, par, qb) in enumerate(UNITS):
                        if i in (0, 2):
                            place_q(i // 2)
                        if par == 0 and qb == 0:
                            pool.wait_ge(S(f"bias{pl}"), it * 32 + (64 * (T + 1) + 32))
                        if T == 0 and i == 0:
                            pool.wait_ge(S("topk"), QB)
                        pool.wait_ge(S("t_x"), it * NU + (32 * (T + 1) + i + 1))
                        W = P * (qb + 1)
                        pool.tensor_tensor(bmC[:, i % 2, 0:W], biasC[:, pl, par, SEQ - W:SEQ],
                                           score[:, qb, 0:W], ALU.add).then_inc(S("C_bm"), 1)
            ffn(1)

        @block.tensor
        def _(pe):
            def block_products(b, s, place, chunks, hi, lo, first=True, last=True, arrived=None, inc=None):
                if b is not None:
                    pe.wait_ge(S("w_lo"), b + 1)
                for half in range(2):
                    cols = slice(HALF * half, HALF * half + HALF)
                    for n, (j, c) in enumerate(chunks):
                        if arrived is not None and half == 0:
                            arrived(c)
                        for i, (w, r) in enumerate(((w_hi, hi), (w_hi, lo), (w_lo, hi))):
                            mm = pe.matmul(PS[:, 2 * place + half, 0:HALF], w[:, s, j * P:(j + 1) * P],
                                           r[:, c, cols], start=first and n == 0 and i == 0,
                                           stop=last and n == len(chunks) - 1 and i == 2)
                mm.then_inc(S(inc or "w_used"), 1)

            EVERY = [(c, c) for c in range(KC)]

            def act_chunk(k):
                def wait(c):
                    pe.wait_ge(S("n_lo_odd" if c % 2 else "n_lo_even"), KC // 2 * k + c // 2 + 1)
                return wait

            def broadcast_sum(t, weights, inc, bank=4):
                for half in range(2):
                    mm = pe.matmul(PS[:, bank + half, 0:HALF], weights, t[:, HALF * half:HALF * half + HALF],
                                   start=True, stop=True)
                mm.then_inc(S(inc), 1)

            def norm_sum(k):
                pe.wait_ge(S("ssum"), KC * (k + 1))
                broadcast_sum(sqsum, ones, "n_ss")

            def products_in(l, k, between=None):
                b0 = IN[l]["b0"]

                def head_sum(q, s):
                    pe.wait_ge(S("hn_ln"), q + 1)
                    broadcast_sum(sq[:, s, :], ones2, "hn_ss")

                def body(n, like):
                    pe.wait_ge(S("free_a"), n + (l * AB_BLOCKS + 1))
                    block_products(n + b0, (b0 + like) % 2, like % 2, EVERY, act_hi, act_lo,
                                   arrived=act_chunk(k) if like == 0 else None)
                    q = normed(l, n - 1, like - 1)
                    if q is not None:
                        pe.wait_ge(S("free_a"), n + (l * AB_BLOCKS + 2))
                        head_sum(q, normed(l, like - 1, like - 1) % 2)
                walk(pe, l, body, between)
                if between:
                    between(IN[l]["n"])
                last = IN[l]["n"] - 1
                q = normed(l, last, last)
                if q is not None:
                    pe.wait_ge(S("free_a"), last + l * AB_BLOCKS + 3)
                    head_sum(q, q % 2)

            def attention(its, base, q_hi, q_lo, k_chunk, v_of, staged, between=None):
                with pe.Fori(0, its) as it:
                    u0 = it * NU

                    def scores(i):
                        pl, par, qb = UNITS[i]
                        if par == 0 and qb == 0:
                            staged(pe, it, pl)
                        W, rows = P * (qb + 1), slice(HD * par, HD * par + HD)
                        pe.wait_ge(S("t_x"), u0 + (base + i + 1))
                        chunk = k_chunk(it, pl)
                        for n, (q, k) in enumerate(((q_hi, act_hi), (q_hi, act_lo), (q_lo, act_hi))):
                            mm = pe.matmul(PS[:, i % 2, 0:W], q[rows, pl, qb * P:(qb + 1) * P],
                                           k[rows, chunk, 0:W], start=n == 0, stop=n == 2)
                        mm.then_inc(S("t_s"), 1)

                    def turn(i):
                        qb = UNITS[i][2]
                        pe.wait_ge(S("t_n"), u0 + (base + i + 1))
                        pe.wait_ge(S("t_c"), u0 + (base + i + 1))
                        for kb in range(qb + 1):
                            src = (pA if base == 0 else pC)[:, i % 2, kb * P:(kb + 1) * P]
                            mm = pe.transpose(PS[:, 2 + i % 2, kb * P:(kb + 1) * P], src, ident)
                        mm.then_inc(S("t_t"), 1)

                    def out(i):
                        pl, par, qb = UNITS[i]
                        if par == 0 and qb == 0:
                            pe.wait_ge(S("t_o"), it * 2 + (base // 8 + pl + 1))
                        pe.wait_ge(S("t_c"), u0 + (base + i + 3))
                        for kb in range(qb + 1):
                            pt_kb = pt[:, i % 2, kb * P:(kb + 1) * P]
                            mm = pe.matmul(PS[HD * par:HD * par + HD, 4 + pl, qb * P:(qb + 1) * P],
                                           v_of(pl, kb, par), pt_kb, start=kb == 0, stop=kb == qb)
                        mm.then_inc(S("t_v"), 1)

                    for i in range(NU + 3):
                        if i < NU:
                            scores(i)
                        if 2 <= i <= NU + 1:
                            turn(i - 2)
                        if i >= 3:
                            out(i - 3)
                        if between is not None and i % 8 == 7:
                            between(it, i // 8)

            def ffn(l):
                L = LAYERS[l]
                f0 = FREE_V * l + 1
                with pe.Fori(0, KC - 1, 2) as j:
                    for u in range(2):
                        pe.wait_ge(S("free_v"), j + (f0 + u))
                        block_products(j + (L["out"] + u), (L["out"] + u) % 2, u, EVERY, act_hi, act_lo)
                norm_sum(3 * l + 1)

                def up(f, arrived):
                    for u in range(2):
                        pe.wait_ge(S("free_v"), f * 2 + (f0 + 8 + u))
                        block_products(f * 2 + (L["ff"] + u), (L["ff"] + u) % 2, u, EVERY, act_hi, act_lo,
                                       arrived=arrived if u == 0 else None)
                up(0, act_chunk(3 * l + 1))
                with pe.Fori(1, FC) as f:
                    up(f, None)
                pe.wait_ge(S("h_lo"), FC * (l + 1) + 1)
                with pe.Fori(0, KC - 1, 2) as j:
                    for u in range(2):
                        pe.wait_ge(S("free_v"), j + (f0 + 8 + 2 * FC + u))
                        for i in range(3):
                            chunks = [(c - 8 * i, c) for c in range(8 * i, min(8 * i + 8, FC))]
                            b = L["down"] + 3 * u + i
                            block_products(j * 3 + b, b % 2, u, chunks, h_hi, h_lo, i == 0, i == 2)
                pe.wait_ge(S("p_lo"), l + 1)
                for o in range(KC):
                    b = L["proj"] + o // 4
                    pe.wait_ge(S("free_v"), f0 + 16 + 2 * FC + o)
                    block_products(b if o % 4 == 0 else None, b % 2, o % 2,
                                   [(o % 4 * 2 + c, c) for c in range(2)], p_hi, p_lo,
                                   inc="w_used" if o % 4 == 3 else "proj")
                    if o == 2:
                        norm_sum(3 * l + 2)
                for m in range(KC):
                    pe.wait_ge(S("free_v"), f0 + 24 + 2 * FC + m)
                    b = L["gate"] + m
                    block_products(b, b % 2, m % 2, EVERY, act_hi, act_lo,
                                   arrived=act_chunk(3 * l + 2) if m == 0 else None)

            pe.sem_inc(S("t_t"), 2)
            pe.sem_inc(S("t_v"), 2)
            pe.wait_ge(S("tables_in"), 16 * 6)
            for n, (r, rows, o) in enumerate(((R_A, 8, O_A), (R_C, 16, O_C))):
                for half, w in enumerate((512, RW - 512)):
                    pe.matmul(PS[0:rows, 2 * n + half, 0:w], brow[:, r:r + rows],
                              orow[:, o + 512 * half:o + 512 * half + w], start=True,
                              stop=True).then_inc(S("rrow_ps"), 1)
            norm_sum(0)
            pe.wait_ge(S("rrow_ok"), 4)
            def gate_logits():
                pe.wait_ge(S("free_a"), 9 + 2)
                for i in range(2):
                    for half in range(2):
                        mm = pe.matmul(PS[:, 4 + 2 * i + half, 0:HALF], gw2[:, i * P:(i + 1) * P],
                                       blr[:, half * HALF:(half + 1) * HALF], start=True, stop=True)
                    mm.then_inc(S("g_z"), 1)

            def values_by_token(banks):
                for n in banks:
                    pe.wait_ge(S("g_na"), 2)
                    for c in (2 * n, 2 * n + 1):
                        for h in range(4):
                            rows = slice(HD * (h % 2), HD * (h % 2) + HD)
                            column = P * (2 * (c % 2) + h // 2)
                            mm = pe.matmul(PS[rows, 4 + n, column:column + P],
                                           yA[:, Y_BV + h, c * GC:(c + 1) * GC], ident, start=True, stop=True)
                    mm.then_inc(S("g_vt"), 1)

            def keys_by_token():
                for i in range(2):
                    pe.wait_ge(S("g_vc"), i + 1)
                    pe.wait_ge(S("g_qk"), i + 1)
                    for r in range(2):
                        rows = slice(HD * r, HD * r + HD)
                        for c in range(NCH):
                            mm = pe.matmul(PS[rows, 4 + i, c * HD:(c + 1) * HD],
                                           yA[rows, Y_BK + i, c * GC:(c + 1) * GC], ident[rows, rows],
                                           start=True, stop=True)
                    mm.then_inc(S("g_kt"), 1)

            def scores_g(i):
                pe.wait_ge(S("g_ktc"), i + 1)
                for r in range(2):
                    rows = slice(HD * r, HD * r + HD)
                    for c in range(NCH):
                        cols = slice(c * GC, (c + 1) * GC)
                        mm = pe.matmul(PS[rows, 4 + i, cols], yA[rows, Y_BK + i, cols], yA[rows, Y_BQ + i, cols],
                                       start=True, stop=True)
                mm.then_inc(S("g_a"), 1)

            def updates(g):
                for i in range(2):
                    if g == 0:
                        pe.wait_ge(S("g_vc"), 4)
                    else:
                        pe.wait_ge(S("g_am"), i + 1)
                    for r in range(2):
                        rows = slice(HD * r, HD * r + HD)
                        for c in range(4 * g, 4 * g + 4):
                            mm = pe.matmul(PS[rows, 6 - 2 * g + i, c % 4 * P:(c % 4 + 1) * P], kbt[rows, i, c, :],
                                           vb[rows, c, i, :], start=True, stop=True)
                    mm.then_inc(S("g_u"), 1)

            def out_g(h):
                i, rows = h // 2, slice(HD * (h % 2), HD * (h % 2) + HD)
                pe.wait_ge(S("g_s"), 2 * NCH)
                if h >= 2:
                    pe.wait_ge(S("g_oc"), h - 1)
                for c in range(NCH):
                    cols = slice(c * GC, (c + 1) * GC)
                    pe.matmul(PS[:, 6 + h % 2, cols], vb[rows, c, i, :], att[rows, i, cols], start=True, stop=False)
                    mm = pe.matmul(PS[:, 6 + h % 2, cols], stm[i][rows, c, :], yA[rows, Y_BQ + i, cols],
                                   start=False, stop=True)
                mm.then_inc(S("g_o"), 1)

            def sample_by_token():
                pe.wait_ge(S("g_oc"), 4)
                for i in range(2):
                    pe.transpose(PS[0:NS, 6, i * P:(i + 1) * P], yA[:, Y_BK + i, SEQ:NT], ident)
                for h in range(4):
                    mm = pe.transpose(PS[0:NS, 7, h * P:(h + 1) * P], yA[:, Y_BV + h, SEQ:NT], ident)
                mm.then_inc(S("s_t"), 1)

            def sample_updates(k):
                pe.wait_ge(S("s_kz"), 2)
                if k >= 2:
                    pe.wait_ge(S("s_new"), k - 1)
                i, b0 = k // 2, 4 * (k % 2)
                for r in range(2):
                    for b in range(4):
                        c = i * P + HD * r
                        mm = pe.matmul(PS[HD * r:HD * r + HD, 6 + k % 2, b * P:(b + 1) * P], kz8[:, b0 + b, c:c + HD],
                                       vt8[:, (2 * i + r) * P:(2 * i + r + 1) * P], start=True, stop=True)
                mm.then_inc(S("s_kv"), 1)

            def gla(n):
                if n == 10:
                    gate_logits()
                elif n in (11, 12):
                    values_by_token((2 * (n - 11), 2 * (n - 11) + 1))
                elif n == 14:
                    keys_by_token()
                elif n == 15:
                    scores_g(0)
                    scores_g(1)
                    updates(0)
                elif n == 16:
                    updates(1)
                elif n in (18, 19):
                    out_g(2 * (n - 18))
                    out_g(2 * (n - 18) + 1)
                elif n == 20:
                    sample_by_token()
                elif 21 <= n < AB_BLOCKS:
                    sample_updates(n - 21)
                elif n == AB_BLOCKS:
                    pe.wait_ge(S("s_new"), 4)
                    attention_v(2)
                    attention_v(3)

            def attention_v(kb):
                for i in range(4):
                    mm = pe.transpose(PS[:, 4 + kb, i * P:(i + 1) * P], yA[:, Y_V + i, kb * P:(kb + 1) * P], ident)
                mm.then_inc(S("A_vt"), 1)

            def norm_b(h):
                pe.wait_ge(S("b_sq"), h + 1)
                if h >= 2:
                    pe.wait_ge(S("b_ln"), h - 1)
                broadcast_sum(sq[:, h % 2, :], ones, "b_ss", 2 * (h % 2))

            products_in(0, 0, gla)
            pe.wait_ge(S("free_a"), AB_BLOCKS + 2)
            pe.wait_ge(S("hn_ln"), 8 + 1)
            attention_v(0)
            attention_v(1)
            pe.wait_ge(S("s_qz"), 1)
            for i in range(2):
                for b in range(NS):
                    c = 2 * (i * NS + b)
                    mm = pe.matmul(PS[:, 2, c:c + 2], s0[:, b, i, :], qz8[:, i, b, :], start=True, stop=True)
            mm.then_inc(S("s_o"), 1)

            pe.wait_ge(S("A_v"), QB)
            pe.wait_ge(S("b_o"), 1)
            def staged_a(pe, it, pl):
                pe.wait_ge(S("A_st"), it * 4 + (2 * pl + 2))
                pe.wait_ge(S("k_split"), it * (1 + pl) + 1)

            attention(2, 0, q_hiA, q_loA, lambda it, pl: 4 + pl,
                      lambda pl, kb, par: vstA[:, pl, kb, HD * par:HD * par + HD],
                      staged_a)

            pe.wait_ge(S("a2_bias"), 32)
            pe.wait_ge(S("a2_qz"), 2)
            pe.matmul(PS[0:64, 6, 0:NK], sbA[:, 0:64], sbA[:, 64:64 + NK], start=True, stop=False)
            for b in range(NS):
                pe.wait_ge(S(f"keys{b % 4}"), 16 * (b // 4 + 1))
                pe.wait_ge(S("s_kn"), b + 1)
                for t in range(4):
                    mm = pe.matmul(PS[0:64, 6, 0:NK], qzA[:, t * NS + b, :], key_place(b)[:, t, :],
                                   start=False, stop=b == NS - 1 and t == 3)
                mm.then_inc(S("s_ks"), 1)
                if b in (3, 5):
                    norm_b(b - 3)
                    norm_b(b - 2)
            for t in range(4):
                mm = pe.transpose(PS[0:NS, 4, t * P:(t + 1) * P], yA[:, Y_V + t, SEQ:NT], ident)
            mm.then_inc(S("a2_vt"), 1)
            pe.wait_ge(S("s_p"), 1)
            for kb in range(2):
                mm = pe.transpose(PS[:, 7, kb * 64:(kb + 1) * 64], psA[:, kb * P:(kb + 1) * P], ident[0:64, 0:64])
            mm.then_inc(S("a2_pt"), 1)
            pe.wait_ge(S("a2_pd"), 1)
            pe.matmul(PS[0:NS, 5, 0:64], rowsel[0:64, :], pdA[:], start=True, stop=True).then_inc(S("a2_pn"), 1)
            pe.wait_ge(S("a2_ptc"), 1)
            pe.wait_ge(S("a2_pnc"), 2)
            for b in range(NS):
                pe.wait_ge(S(f"values{b % 6}"), 16 * (b // 6 + 1))
                for t in range(4):
                    for kb in range(2):
                        c = t * NS + b
                        mm = pe.matmul(PS[:, 5, 2 * c:2 * c + 2], value_place(b)[:, kb, t * P:(t + 1) * P],
                                       ptsA[:, kb, c:c + 33:32], start=kb == 0, stop=kb == 1)
                mm.then_inc(S("s_vs"), 1)
            pn = pnA[:].rearrange("k (r t b) -> k r t b", r=2, t=4)
            for t in range(4):
                mm = pe.matmul(PS[:, 6, 16 * t:16 * t + 16], vnA[:, t * P:(t + 1) * P], pn[:, :, t, :],
                               start=True, stop=True)
            mm.then_inc(S("a2_o"), 1)

            pe.wait_ge(S("a2_done"), 1)
            pe.wait_ge(S("mix_lo"), 4)
            ffn(0)

            def indexer(n):
                if n > 10:
                    sample_index(n - 11)
                if n != 10:
                    return
                pe.wait_ge(S("free_a"), AB_BLOCKS + 8)
                for kb in range(QB):
                    mm = pe.transpose(PS[:, 6, kb * NS:(kb + 1) * NS], yC[0:NS, 5, kb * P:(kb + 1) * P],
                                      ident[0:NS, 0:NS])
                mm.then_inc(S("i_wt"), 1)
                pe.wait_ge(S("i_w"), 1)
                pe.wait_ge(S("hn_ok"), 9 + 2)
                k = 0
                for qb in range(1, QB):
                    for h in range(NS):
                        rows = slice(HD * (h % 2), HD * (h % 2) + HD)
                        if k >= 2:
                            pe.wait_ge(S("i_r"), k - 1)
                        pe.matmul(PS[:, 6 + k % 2, 0:P * (qb + 1)], yC[rows, h // 2, qb * P:(qb + 1) * P],
                                  yC[rows, 4, 0:P * (qb + 1)], start=True, stop=True).then_inc(S("i_s"), 1)
                        k += 1

            def sample_index(b):
                if b == 0:
                    pe.wait_ge(S("i_r"), 24)
                    pe.wait_ge(S("d_z"), 3)
                    pe.wait_ge(S("d_ik"), 16 * 32)
                else:
                    pe.wait_ge(S("d_r"), b)
                    pe.matmul(PS[0:NS, 7, 0:NK], iwz[:, b - 1, :], rel8[:, (b - 1) % 2, :], start=b == 1,
                              stop=b == NS).then_inc(S("d_a"), 1)
                if b < NS:
                    pe.matmul(PS[0:NS, 6, 0:NK], iqz[:, b, :], ikc[:, b, :], start=True,
                              stop=True).then_inc(S("d_s"), 1)

            norm_sum(3)
            products_in(1, 3, indexer)
            pe.wait_ge(S("free_a"), AB_BLOCKS + C_BLOCKS + 2)
            pe.wait_ge(S("hn_ln"), 19 + 1)
            for kb in range(QB):
                for T in range(2):
                    column = P * (2 * (kb % 2) + T)
                    mm = pe.transpose(PS[:, 4 + kb // 2, column:column + P], yC[:, 8 + T, kb * P:(kb + 1) * P], ident)
                if kb % 2:
                    mm.then_inc(S("C_vt"), 1)
            sample_index(8)
            pe.wait_ge(S("hn_ok"), 19 + 2)

            def sample_keys(tokens):
                for b in tokens:
                    pe.wait_ge(S(f"keys{b % 4}"), 32 * (b // 4 + 1) + 32)
                    pe.wait_ge(S("s_kn"), NS + b + 1)
                    for T in range(2):
                        mm = pe.matmul(PS[:, 6, 0:NK], qzC[:, T * NS + b, :], kcC[:, b % 4, T, :], start=False,
                                       stop=b == NS - 1 and T == 1)
                    mm.then_inc(S("s_ks"), 1)

            pe.wait_ge(S("d_bias"), 32)
            pe.wait_ge(S("d_qz"), 4)
            pe.matmul(PS[:, 6, 0:NK], sbC[:, 0:P], sbC[:, P:P + NK], start=True, stop=False)
            sample_keys(range(4))
            pe.wait_ge(S("k_split"), 4)
            pe.wait_ge(S("C_vtc"), 2)
            pts = ptsC[:].rearrange("k n (r t b) -> k n r t b", r=2, t=8)
            sums = PS[:, 7, 2 * P:3 * P].rearrange("p (b T c) -> p b T c", b=NS, T=2)

            def sample_values(it, pl):
                for place in range(2 * pl, 2 * pl + 2):
                    pe.wait_ge(S(f"values{place}"), it * 32 + (64 if place < 2 else 48))
                    pe.sem_inc(S("waits_done"), 1)
                    b = bass.ds(it * 4 + place, 1)
                    for T in range(2):
                        for kb in range(2):
                            mm = pe.matmul(sums[:, b, T, :], vcC[:, place, kb, T * P:(T + 1) * P],
                                           pts[:, kb, :, 4 * T:4 * T + 4, b], start=kb == 0, stop=kb == 1)
                    mm.then_inc(S("s_vs"), 1)

            for T in range(2):
                attention(2, 32 * (T + 1), q_hiC, q_loC, lambda it, pl: 4 * T + 3,
                          lambda pl, kb, par: vtokC[:, kb, T * P + HD * par:T * P + HD * par + HD],
                          lambda pe, it, pl: pe.wait_ge(S("C_st"), it * 4 + (8 * T + 2 * pl + 2)),
                          sample_values if T == 1 else None)
                if T == 0:
                    pe.wait_ge(S("d_mask"), 1)
                    pe.matmul(PS[:, 6, 0:NK], colsel[:], sc8[:], start=False, stop=False)
                    sample_keys(range(4, NS))
                    pe.wait_ge(S("s_p"), 2)
                    for kb in range(2):
                        mm = pe.transpose(PS[:, 7, kb * P:(kb + 1) * P], psC[:, kb * P:(kb + 1) * P], ident)
                    mm.then_inc(S("d_pt"), 1)
                    for v in range(2):
                        mm = pe.transpose(PS[0:NS, 6, v * P:(v + 1) * P], yC[:, 8 + v, SEQ:NT], ident)
                    mm.then_inc(S("d_vt"), 1)
                    pe.wait_ge(S("d_ptc"), 1)

            pe.wait_ge(S("d_pd"), 1)
            pe.wait_ge(S("d_vtc"), 1)
            pe.matmul(PS[0:NS, 6, 256:256 + P], rowsel, pdC[:], start=True, stop=True).then_inc(S("d_pn"), 1)
            pe.wait_ge(S("t_o"), 12 + 2)
            pe.wait_ge(S("d_pnc"), 1)
            pn = pnC[:].rearrange("k (r t b) -> k r t b", r=2, t=8)
            for T in range(2):
                mm = pe.matmul(PS[:, 4, 64 * T:64 * T + 64], vnC[:, T * P:(T + 1) * P],
                               pn[:, :, 4 * T:4 * T + 4, :], start=True, stop=True)
            mm.then_inc(S("d_o"), 1)
            pe.wait_ge(S("mix_lo"), 5)
            ffn(1)

        @block.scalar
        def _(act):
            chain = [0]

            def then(ins):
                chain[0] += 1
                ins.then_inc(S("act_chain"), 1)
                act.wait_ge(S("act_chain"), chain[0])

            def sigmoid(dst, src, signal, so_far):
                act.activation(dst, src, ACT.Exp, scale=-1.0).then_inc(S(signal), 1)
                act.wait_ge(S(signal), so_far + 1)
                act.activation(dst, dst, ACT.Ln, bias=vecs[:, V_ONE:V_ONE + 1]).then_inc(S(signal), 1)
                act.wait_ge(S(signal), so_far + 2)
                act.activation(dst, dst, ACT.Exp, scale=-1.0).then_inc(S(signal), 1)

            def high(b, s, slot_used=True):
                act.wait_ge(S(f"w_raw{s}"), b * 8 + (16 - 8 * s))
                if slot_used:
                    act.wait_ge(S("w_used"), b - 1)
                act.activation(w_hi[:, s, :], w_raw[:, s, :], ACT.Copy).then_inc(S("w_hi"), 1)

            def square(k, m, s):
                if not (isinstance(m, int) and k == 0 and m < 2):
                    act.wait_ge(S("ssum"), m + (KC * k - 1))
                act.activation(sq[:, s:s + 1, :], x[:, bass.ds(m, 1), :], ACT.Square).then_inc(S("sq_ok"), 1)

            def norm(k, midway=None):
                act.wait_ge(S("n_ss"), k + 1)
                then(act.activation(halves(rs[:, 0, :]), slot(2), ACT.Ln, bias=vecs[:, V_EPS:V_EPS + 1],
                                    scale=1.0 / DM))
                act.activation(rs[:, 0, :], rs[:, 0, :], ACT.Exp, scale=-0.5).then_inc(S("n_rs"), 1)
                if midway:
                    midway()
                for c in range(KC):
                    act.wait_ge(S("n_t"), KC * k + c + 1)
                    act.activation(act_hi[:, c, :], normed_place[c % 4], ACT.Copy).then_inc(S("n_hi"), 1)

            def products_in(l, between=None):
                b0, y = IN[l]["b0"], IN[l]["y"]

                def head_rms(q, s):
                    act.wait_ge(S("hn_ss"), q + 1)
                    act.wait_ge(S("hn_ok"), q + 1)
                    act.activation(halves(rs[:, s, :]), slot(2), ACT.Ln, bias=vecs[:, V_EPS:V_EPS + 1],
                                   scale=1.0 / HD).then_inc(S("hn_ln"), 1)
                    act.wait_ge(S("hn_ln"), q + 2)
                    act.activation(rs[:, s, :], rs[:, s, :], ACT.Exp, scale=-0.5).then_inc(S("hn_rs"), 1)

                def body(n, like):
                    high(n + (b0 + 2), (b0 + like) % 2)
                    act.wait_ge(S("w_used"), n + (b0 + 1))
                    place = slot(like % 2)
                    q = normed(l, n, like)
                    rank = l == 0 and like == 0
                    if not rank:
                        dst = y[:, bass.ds(n + IN[l]["shift"], 1), :].rearrange("p o (h n) -> p (o h) n", h=2)
                    if q is not None:
                        s = normed(l, like, like) % 2
                        act.activation(dst, place, ACT.Identity, scale=gains[:, bass.ds(q, 1)])
                        act.activation(halves(sq[:, s, :]), place, ACT.Square).then_inc(S("free_a"), 1)
                    elif rank:
                        act.activation(halves(blr[:]), place[0:16], ACT.Copy).then_inc(S("free_a"), 1)
                    else:
                        by = (NS * HD) ** -0.5 if l == 1 and like == 5 else 1.0
                        act.activation(dst, place, ACT.Copy, scale=by).then_inc(S("free_a"), 1)
                    q = normed(l, n - 1, like - 1)
                    if q is not None:
                        head_rms(q, normed(l, like - 1, like - 1) % 2)
                walk(act, l, body, between)
                last = IN[l]["n"] - 1
                q = normed(l, last, last)
                if q is not None:
                    head_rms(q, q % 2)

            def attention(its, base, pair0, xs, ps, stat):
                with act.Fori(0, its) as it:
                    u0 = it * NU

                    def exps(i):
                        W = P * (UNITS[i][2] + 1)
                        act.wait_ge(S("t_x"), u0 + (base + i + 3))
                        act.wait_ge(S("t_t"), u0 + (base + i + 1))
                        act.activation(ps[:, i % 2, 0:W], xs[:, i % 2, 0:W], ACT.Exp, bias=stat[:, i % 2, 0:1],
                                       scale=-1.0, accum_out=stat[:, i % 2, 1:2]).then_inc(S("t_e"), 1)

                    def copy(i):
                        W = P * (UNITS[i][2] + 1)
                        act.wait_ge(S("t_t"), u0 + (base + i + 3))
                        act.wait_ge(S("t_v"), u0 + (base + i + 1))
                        act.activation(pt[:, i % 2, 0:W], PS[:, 2 + i % 2, 0:W], ACT.Copy).then_inc(S("t_c"), 1)

                    def out(pl):
                        act.wait_ge(S("t_v"), u0 + (base + 8 * pl + 10))
                        act.activation(act_hi[:, bass.ds(it * 2 + (pair0 + pl), 1), 0:SEQ],
                                       PS[:, 4 + pl:5 + pl, :], ACT.Copy).then_inc(S("t_oh"), 1)

                    for i in range(NU + 2):
                        if i >= 2:
                            copy(i - 2)
                        if i < NU:
                            exps(i)
                        if i == 12:
                            out(0)
                    act.wait_ge(S("t_v"), u0 + (base + NU + 2))
                    out(1)

            def ffn(l):
                L = LAYERS[l]
                with act.Fori(0, KC - 1, 2) as j:
                    for u in range(2):
                        high(j + (L["out"] + u + 2), (L["out"] + u) % 2)
                        act.wait_ge(S("free_v"), j + (FREE_V * l + u + 3))
                        square(3 * l + 1, j + u, u)
                for name, n in ((("a_out", 32), ("s_out", 16)) if l == 0 else (("c_out", 48),)):
                    act.wait_ge(S(name), n)
                act.dma_start(p_raw[:], a["pT"][l]).then_inc(S("p_in"), 16)
                norm(3 * l + 1)
                act.wait_ge(S("p_in"), 16 * (l + 1))
                act.activation(p_hi[:], p_raw[:], ACT.Copy).then_inc(S("p_hi"), 1)
                with act.Fori(0, FC) as f:
                    high(f * 2 + (L["ff"] + 2), L["ff"] % 2)
                    act.wait_ge(S("w_used"), f * 2 + (L["ff"] + 1))
                    sigmoid(halves(sq[:, 0, :]), slot(0), "f_e", f * 3 + 3 * FC * l)
                    high(f * 2 + (L["ff"] + 3), (L["ff"] + 1) % 2)
                    act.wait_ge(S("free_v"), f * 2 + (FREE_V * l + 8 + 4))
                    act.activation(h_hi[:, bass.ds(f, 1), :], tmp[:, 0:1, :], ACT.Copy).then_inc(S("h_hi"), 1)
                with act.Fori(0, KC - 1, 2) as j:
                    for u in range(2):
                        for i in range(3):
                            b = L["down"] + 3 * u + i + 2
                            high(j * 3 + b, b % 2)
                        act.wait_ge(S("free_v"), j + (FREE_V * l + 8 + 2 * FC + u + 3))
                        square(3 * l + 2, j + u, u)
                norm(3 * l + 2, lambda: high(L["proj"] + 2, L["proj"] % 2))
                high(L["proj"] + 3, (L["proj"] + 1) % 2)
                with act.Fori(0, KC - 1, 2) as j:
                    for u in range(2):
                        high(j + (L["gate"] + u + 2), (L["gate"] + u) % 2)
                        act.wait_ge(S("w_used"), j + (L["gate"] + u + 1))
                        sigmoid(halves(tmp[:, u, :]), slot(u), "g_e", j * 3 + (3 * KC * l + 3 * u))
                        act.wait_ge(S("x_new"), j + (KC * l + u + 1))
                        if l == 0:
                            square(3, j + u, u)

            act.preload_act_table_set("natural_log_exp_and_others")
            act.sem_inc(S("free_a"), 2)
            act.sem_inc(S("hn_ln"), 1)
            act.sem_inc(S("t_e"), 2)
            act.sem_inc(S("t_c"), 2)
            for m in range(KC):
                act.wait_ge(S(f"x_in{m // 2}"), 16)
                square(0, m, m % 2)
            for b in range(2):
                high(b, b, slot_used=False)
            act.wait_ge(S("tables_in"), 16 * 6)
            norm(0)
            act.wait_ge(S("gains"), 3)

            def gla(n):
                if n == 11:
                    for i in range(2):
                        act.wait_ge(S("g_na"), i + 1)
                        then(act.activation(zn[:, i, :], zn[:, i, :], ACT.Exp))
                        act.activation(zn[:, i, :], zn[:, i, :], ACT.Ln,
                                       bias=vecs[:, V_ONE:V_ONE + 1]).then_inc(S("g_l"), 1)
                    act.dma_start(s0[:], a["state"]).then_inc(S("s_in"), 16)
                if n in (11, 12):
                    for m in (2 * (n - 11), 2 * (n - 11) + 1):
                        act.wait_ge(S("g_vt"), m + 1)
                        act.activation(vb[:, 2 * m:2 * m + 2, :, :],
                                       PS[:, 4 + m, :].rearrange("p (c i e) -> p c i e", c=2, i=2),
                                       ACT.Copy).then_inc(S("g_vc"), 1)
                if n == 13:
                    for i in range(2):
                        act.wait_ge(S("g_d"), i + 1)
                        by_chunk = cum[:, i, :].rearrange("p (c t) -> p c t", t=GC)
                        act.activation(decay[:, i, 0, :], by_chunk[:, :, GC // 2 - 1], ACT.Exp)
                        act.activation(decay[:, i, 1, :], by_chunk[:, :, GC - 1], ACT.Exp)
                        act.activation(zt[:, i, 0:SEQ], zn[:, i, 0:SEQ], ACT.Exp).then_inc(S("g_e1"), 1)
                        act.wait_ge(S("g_e1"), i + 1)
                        act.activation(zn[:, i, 0:SEQ], zn[:, i, 0:SEQ], ACT.Exp, scale=-1.0).then_inc(S("g_e2"), 1)
                    act.activation(eg[:], gs[:], ACT.Exp).then_inc(S("s_eg"), 1)
                if n == 14:
                    for i in range(2):
                        act.wait_ge(S("g_kt"), i + 1)
                        act.activation(kbt[:, i, :, :], PS[:, 4 + i, :].rearrange("p (c d) -> p c d", c=NCH),
                                       ACT.Copy).then_inc(S("g_ktc"), 1)
                if n in (18, 19):
                    for h in range(2 * (n - 18), 2 * (n - 17)):
                        act.wait_ge(S("g_o"), h + 1)
                        act.activation(yA[:, Y_BV + h, 0:SEQ], PS[:, 6 + h % 2, :], ACT.Copy).then_inc(S("g_oc"), 1)
                if n == 19:
                    act.dma_start(a["b_state"], st[:]).then_inc(S("b_out"), 16)
                if n >= 21:
                    h = n - 21
                    if h >= 2:
                        act.wait_ge(S("b_gt"), h - 1)
                    sigmoid(tmp[:, h % 2, :], yA[:, Y_BG + h, :], "b_e", 3 * h)

            products_in(0, gla)
            act.wait_ge(S("s_new"), 4)
            act.dma_start(a["s_state"], s0[:]).then_inc(S("s_out"), 16)
            act.wait_ge(S("hn_ok"), 8 + 2)
            act.wait_ge(S("w_used"), AB_BLOCKS)
            act.activation(act_hi[:, 4:6, 0:SEQ], yA[:, Y_K:Y_K + 2, 0:SEQ], ACT.Copy).then_inc(S("k_hi"), 1)
            act.dma_start(a["a_k"], yA[:, Y_K:Y_K + 4, :]).then_inc(S("a_out"), 16)
            act.dma_start(a["a_v"], yA[:, Y_V:Y_V + 4, :]).then_inc(S("a_out"), 16)

            attention(2, 0, 0, xA, pA, statA)

            def square_b(h):
                act.activation(sq[:, h % 2, :], yA[:, Y_BV + h, :], ACT.Square).then_inc(S("b_sq"), 1)

            def high_b(h):
                act.wait_ge(S("b_g"), h + 1)
                act.activation(act_hi[:, 4 + h, :], yA[:, Y_BV + h, :], ACT.Copy).then_inc(S("b_hi"), 1)

            act.wait_ge(S("b_o"), 1)
            square_b(0)
            square_b(1)
            for h in range(4):
                act.wait_ge(S("b_ss"), h + 1)
                if h >= 2:
                    act.wait_ge(S("b_n"), h - 1)
                act.activation(halves(rs[:, h % 2, :]), slot(h % 2), ACT.Ln, bias=vecs[:, V_EPS:V_EPS + 1],
                               scale=1.0 / P).then_inc(S("b_ln"), 1)
                if h < 2:
                    square_b(h + 2)
                act.wait_ge(S("b_ln"), h + 1)
                act.activation(rs[:, h % 2, :], rs[:, h % 2, :], ACT.Exp, scale=-0.5).then_inc(S("b_rs"), 1)
                if h >= 1:
                    high_b(h - 1)
            high_b(3)

            act.wait_ge(S("s_m"), 1)
            act.activation(psA[:], PS[0:64, 6, 0:NK], ACT.Exp, bias=sstA[:, 0:1],
                           accum_out=sstA[:, 1:2]).then_inc(S("s_e"), 1)
            act.wait_ge(S("a2_pt"), 1)
            act.activation(ptsA[:], PS[:, 7, 0:P].rearrange("p (n c) -> p n c", n=2), ACT.Copy).then_inc(S("a2_ptc"), 1)
            act.wait_ge(S("a2_os"), 2)
            act.activation(act_hi[:, 0:4, SEQ:NT], osA[:], ACT.Copy).then_inc(S("a2_oh"), 1)
            ffn(0)

            def sample_index(b):
                act.wait_ge(S("d_s"), b + 1)
                if b >= 2:
                    act.wait_ge(S("d_a"), b - 1)
                act.activation(rel8[:, b % 2, :], PS[0:NS, 6, 0:NK], ACT.Relu).then_inc(S("d_r"), 1)

            def indexer(n):
                if n > 10:
                    sample_index(n - 11)
                if n != 10:
                    return
                k = 0
                for qb in range(1, QB):
                    for h in range(NS):
                        act.wait_ge(S("i_s"), k + 1)
                        if k >= 2:
                            act.wait_ge(S("i_a"), k - 1)
                        W = P * (qb + 1)
                        act.activation(reluC[:, k % 2, 0:W], PS[:, 6 + k % 2, 0:W], ACT.Relu).then_inc(S("i_r"), 1)
                        k += 1

            norm(3)
            products_in(1, indexer)
            act.wait_ge(S("hn_ok"), 19 + 2)
            act.wait_ge(S("free_a"), AB_BLOCKS + C_BLOCKS + 2)
            act.activation(act_hi[:, 3:8:4, 0:SEQ], yC[:, 6:8, 0:SEQ], ACT.Copy).then_inc(S("k_hi"), 1)
            act.dma_start(a["c_k"], yC[:, 6:8, :]).then_inc(S("c_out"), 16)
            act.dma_start(a["c_v"], yC[:, 8:10, :]).then_inc(S("c_out"), 16)
            act.dma_start(a["c_ik"], yC[0:HD, 4, :]).then_inc(S("c_out"), 16)
            sample_index(7)
            for T in range(2):
                attention(2, 32 * (T + 1), 4 * T, xC, pC, statC)
                if T == 0:
                    act.wait_ge(S("s_m"), 2)
                    act.activation(psC[:], PS[:, 6, 0:NK], ACT.Exp, bias=sstC[:, 0:1],
                                   accum_out=sstC[:, 1:2]).then_inc(S("s_e"), 1)
                    act.wait_ge(S("d_pt"), 1)
                    act.activation(ptsC[:], PS[:, 7, 0:2 * P].rearrange("p (n c) -> p n c", n=2),
                                   ACT.Copy).then_inc(S("d_ptc"), 1)

            act.wait_ge(S("d_os"), 4)
            act.activation(act_hi[:, :, SEQ:NT], osC[:], ACT.Copy).then_inc(S("d_oh"), 1)
            ffn(1)

        @block.vector
        def _(dve):
            chain = [0]

            def then(ins):
                step(ins)
                dve.wait_ge(S("dve_chain"), chain[0])

            def step(ins):
                chain[0] += 1
                ins.then_inc(S("dve_chain"), 1)

            def waits_done():
                dve.sem_inc(S("waits_done"), 1)

            def add_squares(k, m, s):
                dve.wait_ge(S("sq_ok"), m + (KC * k + 1))
                if not (isinstance(m, int) and k == m == 0):
                    dve.wait_ge(S("ssum"), m + KC * k)
                dve.tensor_tensor(sqsum[:], sqsum[:], sq[:, s, :], ALU.add).then_inc(S("ssum"), 1)

            def clear_sum():
                then(dve.memset(sqsum[:], 0.0))

            def norm(k, gain, between=None):
                def low(c):
                    dve.wait_ge(S("n_hi"), KC * k + c + 1)
                    dve.tensor_tensor(act_lo[:, c, :], normed_place[c % 4], act_hi[:, c, :].bitcast(F32),
                                      ALU.subtract).then_inc(S("n_lo_odd"), 1)

                dve.wait_ge(S("n_rs"), k + 1)
                for c in range(KC):
                    if c >= 4:
                        dve.wait_ge(S("n_lo_odd" if c % 2 else "n_lo_even"), KC // 2 * k + (c - 4) // 2 + 1)
                    dve.scalar_tensor_tensor(normed_place[c % 4], x[:, c, :], vecs[:, gain + c:gain + c + 1],
                                             rs[:, 0, :], ALU.mult, ALU.mult).then_inc(S("n_t"), 1)
                    if c >= 2 and c % 2 == 0:
                        low(c - 1)
                        if between:
                            between(c // 2 - 1)
                low(KC - 1)
                clear_sum()

            def attention(its, base, pair0, xs, ps, stat, bias):
                with dve.Fori(0, its) as it:
                    u0 = it * NU

                    def add_bias(i):
                        W = P * (UNITS[i][2] + 1)
                        dve.wait_ge(S("t_s"), u0 + (base + i + 1))
                        dve.wait_ge(S("t_e"), u0 + (base + i + 1))
                        added = bias(it, i, W)
                        waits_done()
                        dve.tensor_tensor_reduce(xs[:, i % 2, 0:W], PS[:, i % 2, 0:W], added, -1.0, 1e38,
                                                 ALU.add, ALU.min, stat[:, i % 2, 0:1]).then_inc(S("t_x"), 1)

                    def scale(i):
                        W = P * (UNITS[i][2] + 1)
                        dve.wait_ge(S("t_e"), u0 + (base + i + 3))
                        dve.reciprocal(stat[:, i % 2, 2:3], stat[:, i % 2, 1:2]).then_inc(S("t_r"), 1)
                        dve.wait_ge(S("t_r"), u0 + (base + i + 1))
                        dve.tensor_scalar(ps[:, i % 2, 0:W], ps[:, i % 2, 0:W], stat[:, i % 2, 2:3], None,
                                          ALU.mult).then_inc(S("t_n"), 1)

                    def out(pl):
                        pair = it * 2 + (base // 8 + pl)
                        dve.wait_ge(S("t_oh"), pair + 1)
                        dst = bass.ds(it * 2 + (pair0 + pl), 1)
                        dve.tensor_tensor(act_lo[:, dst, 0:SEQ], PS[:, 4 + pl:5 + pl, :],
                                          act_hi[:, dst, 0:SEQ].bitcast(F32), ALU.subtract).then_inc(S("t_o"), 1)

                    for i in range(NU + 1):
                        if i < NU:
                            add_bias(i)
                        if i > 0:
                            scale(i - 1)
                        if i == 12:
                            out(0)
                    out(1)

            def ffn(l):
                L = LAYERS[l]
                f0 = FREE_V * l + 2
                with dve.Fori(0, KC - 1, 2) as j:
                    for u in range(2):
                        m = bass.ds(j + u, 1)
                        dve.wait_ge(S("w_used"), j + (L["out"] + u + 1))
                        dst = x[:, m, :].rearrange("p o (h n) -> p (o h) n", h=2)
                        dve.tensor_tensor(dst, slot(u), dst, ALU.add).then_inc(S("free_v"), 1)
                        add_squares(3 * l + 1, j + u, u)
                norm(3 * l + 1, V_FFN + KC * l)
                dve.wait_ge(S("n_lo_even"), KC // 2 * (3 * l + 2))
                with dve.Fori(0, FC) as f:
                    dve.wait_ge(S("f_e"), f * 3 + (3 * FC * l + 3))
                    dve.tensor_tensor(halves(tmp[:, 1, :]), slot(0), halves(sq[:, 0, :]),
                                      ALU.mult).then_inc(S("free_v"), 1)
                    dve.wait_ge(S("w_used"), f * 2 + (L["ff"] + 2))
                    dve.wait_ge(S("free_v"), f * 2 + (f0 + 8 + 1))
                    dve.wait_ge(S("h_lo"), f + (FC * l + 1))
                    dve.tensor_tensor(halves(tmp[:, 0, :]), slot(1), halves(tmp[:, 1, :]),
                                      ALU.mult).then_inc(S("free_v"), 1)
                    dve.wait_ge(S("h_hi"), f + (FC * l + 1))
                    dve.tensor_tensor(h_lo[:, bass.ds(f, 1), :], tmp[:, 0:1, :],
                                      h_hi[:, bass.ds(f, 1), :].bitcast(F32), ALU.subtract).then_inc(S("h_lo"), 1)
                with dve.Fori(0, KC - 1, 2) as j:
                    for u in range(2):
                        m = bass.ds(j + u, 1)
                        dve.wait_ge(S("w_used"), j * 3 + (L["down"] + 3 * u + 3))
                        dst = x[:, m, :].rearrange("p o (h n) -> p (o h) n", h=2)
                        dve.tensor_tensor(dst, slot(u), dst, ALU.add).then_inc(S("free_v"), 1)
                        add_squares(3 * l + 2, j + u, u)
                for o in range(5):
                    project(l, o)
                norm(3 * l + 2, V_PLE + KC * l, lambda n: project(l, 5 + n))
                with dve.Fori(0, KC - 1, 2) as j:
                    for u in range(2):
                        m = bass.ds(j + u, 1)
                        dve.wait_ge(S("g_e"), j * 3 + (3 * KC * l + 3 * u + 3))
                        dve.tensor_tensor(tmp[:, u:u + 1, :], tmp[:, u:u + 1, :], pp[:, m, :],
                                          ALU.mult).then_inc(S("free_v"), 1)
                        dve.wait_ge(S("free_v"), j + (f0 + 24 + 2 * FC + u + 1))
                        dve.tensor_tensor(x[:, m, :], x[:, m, :], tmp[:, u:u + 1, :], ALU.add).then_inc(S("x_new"), 1)
                        if l == 0:
                            add_squares(3, j + u, u)

            def project(l, o):
                L = LAYERS[l]
                if o % 4 == 3:
                    dve.wait_ge(S("w_used"), L["proj"] + o // 4 + 1)
                else:
                    dve.wait_ge(S("proj"), 6 * l + o - o // 4 + 1)
                dve.tensor_copy(halves(pp[:, o, :]), slot(o % 2)).then_inc(S("free_v"), 1)

            def softmax(n, scores, probs, stat):
                dve.tensor_reduce(stat[:, 0:1], scores, AX.X, ALU.max, negate=True).then_inc(S("s_m"), 1)
                dve.wait_ge(S("s_e"), n + 1)
                then(dve.reciprocal(stat[:, 2:3], stat[:, 1:2]))
                dve.tensor_scalar(probs[:], probs[:], stat[:, 2:3], None, ALU.mult).then_inc(S("s_p"), 1)
                dve.wait_ge(S("s_p"), n + 1)

            dve.sem_inc(S("free_v"), 2)
            dve.sem_inc(S("h_lo"), 1)
            dve.sem_inc(S("t_x"), 2)
            dve.sem_inc(S("t_o"), 2)
            clear_sum()
            for n, rows in enumerate((8, 16)):
                dve.wait_ge(S("rrow_ps"), 2 * n + 2)
                for half, w in enumerate((512, RW - 512)):
                    dve.tensor_copy(rrow[0:rows, n, 512 * half:512 * half + w],
                                    PS[0:rows, 2 * n + half, 0:w]).then_inc(S("rrow_ok"), 1)
            dve.wait_ge(S("tables_in"), 16 * 6)
            dve.tensor_scalar(gains[:, 0:4], vecs[:, V_NG:V_NG + 4], HD ** -0.5, None, ALU.mult).then_inc(S("gains"), 1)
            dve.tensor_copy(gains[:, 4:11], vecs[:, V_NG + 4:V_NG + 11]).then_inc(S("gains"), 1)
            dve.tensor_scalar(gains[:, 11:19], vecs[:, V_NG + 11:V_NG + 19], HD ** -0.5, None,
                              ALU.mult).then_inc(S("gains"), 1)
            for m in range(KC):
                add_squares(0, m, m % 2)
            norm(0, V_MIX)

            dve.wait_ge(S("rows_out"), 64)
            for i in range(2):
                dve.wait_ge(S("g_z"), i + 1)
                then(dve.tensor_scalar(halves(zt[:, i, :]), slot(2 + i), vecs[:, V_GB + i:V_GB + i + 1], None, ALU.add))
                dve.scalar_tensor_tensor(zn[:, i, :], zt[:, i, :], -1.0, zt[:, i, :], ALU.mult,
                                         ALU.min).then_inc(S("g_na"), 1)
            for i in range(2):
                dve.wait_ge(S("g_l"), i + 1)
                then(dve.scalar_tensor_tensor(zt[:, i, :], zt[:, i, :], 0.0, zn[:, i, :], ALU.min, ALU.subtract))
                then(dve.tensor_scalar(zt[:, i, :], zt[:, i, :], 1.0 / 16.0, None, ALU.mult))
                dve.tensor_copy(gs[:, i, :], zt[:, i, SEQ:NT])
                then(dve.tensor_tensor_scan(cum[:, i, :], fresh, zt[:, i, 0:SEQ], 0.0, ALU.mult, ALU.add))
                by_chunk = cum[:, i, :].rearrange("p (c t) -> p c t", t=GC)
                middle = by_chunk[:, :, GC // 2 - 1:GC // 2].to_broadcast([P, NCH, GC])
                dve.tensor_tensor(zn[:, i, 0:SEQ].rearrange("p (c t) -> p c t", t=GC), by_chunk, middle,
                                  ALU.subtract).then_inc(S("g_d"), 1)
            for i in range(2):
                dve.wait_ge(S("g_e2"), i + 1)
                then(dve.tensor_tensor(yA[:, Y_BK + i, 0:SEQ], yA[:, Y_BK + i, 0:SEQ], zn[:, i, 0:SEQ], ALU.mult))
                dve.scalar_tensor_tensor(yA[:, Y_BQ + i, 0:SEQ], yA[:, Y_BQ + i, 0:SEQ], HD ** -0.5, zt[:, i, 0:SEQ],
                                         ALU.mult, ALU.mult).then_inc(S("g_qk"), 1)
            then(dve.memset(st[:], 0.0))
            last = zt[:, :, 0:SEQ].rearrange("p i (c t) -> p i c t", t=GC)[:, :, :, GC - 1:GC]
            for i in range(2):
                dve.wait_ge(S("g_a"), i + 1)
                grid = att[:, i, :].rearrange("p (c t) -> p c t", t=GC)
                dve.tensor_tensor(grid, PS[:, 4 + i, :].rearrange("p (c t) -> p c t", t=GC),
                                  tri.unsqueeze(1).to_broadcast([P, NCH, GC]), ALU.mult).then_inc(S("g_am"), 1)
            for g in range(2):
                for i in range(2):
                    dve.wait_ge(S("g_u"), 2 * g + i + 1)
                    for c in range(4 * g, 4 * g + 4):
                        dve.tensor_scalar(stm[i][:, c, :], st[:, i, :], decay[:, i, 0, c:c + 1], None, ALU.mult)
                        then(dve.tensor_scalar(upd[:, c % 2, :], PS[:, 6 - 2 * g + i, c % 4 * P:(c % 4 + 1) * P],
                                               last[:, i, c, :], None, ALU.mult))
                        dve.scalar_tensor_tensor(st[:, i, :], st[:, i, :], decay[:, i, 1, c:c + 1], upd[:, c % 2, :],
                                                 ALU.mult, ALU.add).then_inc(S("g_s"), 1)
                        dve.wait_ge(S("g_s"), 8 * g + 4 * i + c % 4 + 1)

            dve.wait_ge(S("s_t"), 1)
            then(dve.tensor_copy(kt8[:], PS[0:NS, 6, 0:256]))
            then(dve.tensor_copy(vt8[:], PS[0:NS, 7, :]))
            for b in range(NS):
                ins = dve.tensor_scalar(kz8[:, b, :], kt8[:], ident[0:NS, b:b + 1], None, ALU.mult)
            ins.then_inc(S("s_kz"), 2)
            then(dve.memset(qz8[:], 0.0))
            for r in range(2):
                rows = slice(HD * r, HD * r + HD)
                ins = dve.tensor_scalar(qz8[rows, :, :, r], yA[rows, Y_BQ:Y_BQ + 2, SEQ:NT], HD ** -0.5, None, ALU.mult)
                if r == 0:
                    then(ins)
            ins.then_inc(S("s_qz"), 1)
            dve.wait_ge(S("s_in"), 16)
            dve.wait_ge(S("s_eg"), 1)
            for i in range(2):
                then(dve.tensor_tensor(s0[:, :, i, :], s0[:, :, i, :],
                                       eg[:, i, :].unsqueeze(2).to_broadcast([P, NS, P]), ALU.mult))
            for k in range(4):
                gate = yA[:, Y_BG + k, :]
                dve.wait_ge(S("b_e"), 3 * k + 3)
                dve.tensor_tensor(gate, gate, tmp[:, k % 2, :], ALU.mult).then_inc(S("b_gt"), 1)
                i, b0 = k // 2, 4 * (k % 2)
                dve.wait_ge(S("s_kv"), k + 1)
                dve.tensor_tensor(s0[:, b0:b0 + 4, i, :], PS[:, 6 + k % 2, :].rearrange("p (b c) -> p b c", b=4),
                                  s0[:, b0:b0 + 4, i, :], ALU.add).then_inc(S("s_new"), 1)
            dve.wait_ge(S("b_out"), 16)
            dve.wait_ge(S("k_hi"), 1)
            dve.tensor_tensor(act_lo[:, 4:6, 0:SEQ], yA[:, Y_K:Y_K + 2, 0:SEQ], act_hi[:, 4:6, 0:SEQ].bitcast(F32),
                              ALU.subtract).then_inc(S("k_split"), 1)
            for n, kb in enumerate((2, 3, 0, 1)):
                dve.wait_ge(S("A_vt"), n + 1)
                dve.tensor_copy(vtokA[:, kb, :], PS[:, 4 + kb, :]).then_inc(S("A_v"), 1)
            dve.wait_ge(S("s_o"), 1)
            src = PS[:, 2, 0:32].rearrange("p (i b r) -> p i b r", i=2, b=NS)
            dst = yA[:, Y_BV:Y_BV + 4, :].rearrange("p (i r) n -> p i r n", i=2)
            then(dve.tensor_copy(dst[:, :, 0, SEQ:NT], src[:, :, :, 0]))
            dve.tensor_copy(dst[:, :, 1, SEQ:NT], src[:, :, :, 1]).then_inc(S("b_o"), 1)

            def low_b(h):
                dve.wait_ge(S("b_hi"), h + 1)
                dve.tensor_tensor(act_lo[:, 4 + h, :], yA[:, Y_BV + h, :], act_hi[:, 4 + h, :].bitcast(F32),
                                  ALU.subtract).then_inc(S("mix_lo"), 1)

            def norm_b(h):
                o = yA[:, Y_BV + h, :]
                dve.wait_ge(S("b_rs"), h + 1)
                dve.scalar_tensor_tensor(o, o, vecs[:, V_BO:V_BO + 1], rs[:, h % 2, :], ALU.mult,
                                         ALU.mult).then_inc(S("b_n"), 1)
                dve.wait_ge(S("b_n"), h + 1)
                dve.tensor_tensor(o, o, yA[:, Y_BG + h, :], ALU.mult).then_inc(S("b_g"), 1)
                if h >= 1:
                    low_b(h - 1)

            dve.wait_ge(S("b_gt"), 4)
            def bias_a(it, i, W):
                pl, par, qb = UNITS[i]
                if par == 0 and qb == 0:
                    dve.wait_ge(S(f"bias{pl}"), it * 32 + 32)
                return biasA[:, pl, par, SEQ - W:SEQ]
            attention(2, 0, 0, xA, pA, statA, bias_a)

            qz = qzA[:].rearrange("p m c -> p (m c)")
            then(dve.memset(qzA[:], 0.0))
            for r in range(2):
                rows = slice(HD * r, HD * r + HD)
                dst = qz[rows, 32 * r:32 * r + 31 * 65 + 1:65].rearrange("p (t b) -> p t b", t=4)
                dve.tensor_copy(dst, yA[rows, Y_Q:Y_Q + 4, SEQ:NT]).then_inc(S("a2_qz"), 1)
            for b in range(NS):
                if b >= 4:
                    dve.wait_ge(S("s_ks"), b - 3)
                dve.tensor_copy(key_place(b)[:, :, PAST], yA[:, Y_K:Y_K + 4, SEQ + b]).then_inc(S("s_kn"), 1)
                if b in (3, 5):
                    norm_b(b - 3)
                    norm_b(b - 2)
                if b == 5:
                    low_b(3)
            dve.wait_ge(S("a2_vt"), 1)
            dve.tensor_copy(vnA[:], PS[0:NS, 4, :]).then_inc(S("a2_pnc"), 1)
            dve.wait_ge(S("s_ks"), NS)
            softmax(0, PS[0:64, 6, 0:NK], psA, sstA)
            dve.tensor_scalar(pdA[:], ident[0:64, 0:64], psA[:, PAST:NK], None, ALU.mult).then_inc(S("a2_pd"), 1)
            dve.wait_ge(S("a2_pn"), 1)
            dve.tensor_copy(pnA[:], PS[0:NS, 5, 0:64]).then_inc(S("a2_pnc"), 1)
            dve.wait_ge(S("a2_o"), 1)
            then(dve.tensor_copy(owA[:], PS[:, 6, 0:64].rearrange("p (t r b) -> p t r b", t=4, r=2)))
            for r in range(2):
                rows = slice(HD * r, HD * r + HD)
                src = PS[rows, 5, 0:64].rearrange("p (t b r) -> p t b r", t=4, r=2)[:, :, :, r]
                dve.tensor_tensor(osA[rows], src, owA[rows, :, r, :], ALU.add).then_inc(S("a2_os"), 1)
            dve.wait_ge(S("a2_oh"), 1)
            dve.tensor_tensor(act_lo[:, 0:4, SEQ:NT], osA[:], act_hi[:, 0:4, SEQ:NT].bitcast(F32),
                              ALU.subtract).then_inc(S("a2_done"), 1)
            dve.wait_ge(S("a2_done"), 1)

            ffn(0)

            norm(3, V_MIX + KC)
            dve.wait_ge(S("free_a"), AB_BLOCKS + 10)
            dve.wait_ge(S("hn_ok"), 11 + 2)
            dve.tensor_copy(ikc[:, :, PAST], yC[:, 4, SEQ:NT]).then_inc(S("d_z"), 1)
            then(dve.memset(iqz[:], 0.0))
            then(dve.memset(iwz[:], 0.0))
            then(dve.memset(qzC[:], 0.0))
            by_par = iqz[:].rearrange("p b (t r) -> p r t b", r=2)
            for r in range(2):
                rows = slice(HD * r, HD * r + HD)
                ins = dve.tensor_copy(by_par[rows, r], yC[rows, 0:4, SEQ:NT])
                if r == 0:
                    then(ins)
            ins.then_inc(S("d_z"), 1)
            diagonal = iwz[:].rearrange("h b c -> h (b c)")[:, 0:NS * NS:NS + 1]
            dve.tensor_copy(diagonal, yC[0:NS, 5, SEQ:NT]).then_inc(S("d_z"), 1)
            for b in range(4):
                dve.tensor_copy(kcC[:, b, :, PAST], yC[:, 6:8, SEQ + b]).then_inc(S("s_kn"), 1)
            dve.wait_ge(S("i_wt"), 1)
            dve.tensor_copy(iwt[:], PS[:, 6, 0:4 * NS].rearrange("p (k h) -> p k h", k=4)).then_inc(S("i_w"), 1)
            dve.wait_ge(S("i_w"), 1)
            k = 0
            for qb in range(1, QB):
                W = P * (qb + 1)
                for h in range(NS):
                    dve.wait_ge(S("i_r"), k + 1)
                    if k:
                        dve.wait_ge(S("i_a"), k)
                    sofar = causal[:, SEQ - W:SEQ] if h == 0 else score[:, qb, 0:W]
                    dve.scalar_tensor_tensor(score[:, qb, 0:W], reluC[:, k % 2, 0:W], iwt[:, qb, h:h + 1], sofar,
                                             ALU.mult, ALU.add).then_inc(S("i_a"), 1)
                    k += 1
            dve.wait_ge(S("i_a"), k)

            def top(searches, n):
                for j in range(n // 8):
                    first = chain[0]
                    for m, (values, spare, best) in enumerate(searches):
                        if j:
                            dve.wait_ge(S("dve_chain"), first - len(searches) + m + 1)
                        step(dve.max(best, spare if j else values))
                    for m, (values, spare, best) in enumerate(searches):
                        dve.wait_ge(S("dve_chain"), first + m + 1)
                        step(dve.match_replace(spare, best, spare if j else values, GONE))
                first = chain[0] - len(searches)
                for m, (values, spare, best) in enumerate(searches):
                    dve.wait_ge(S("dve_chain"), first + m + 1)
                    step(dve.tensor_tensor(spare, spare, values, ALU.is_equal))
                dve.wait_ge(S("dve_chain"), chain[0])

            top([(score[:, qb, 0:P * (qb + 1)], work[qb][:, 0:P * (qb + 1)], top8[:, qb, :])
                 for qb in range(1, QB)], TOPK_P)
            for qb in range(1, QB):
                W = P * (qb + 1)
                dve.tensor_scalar(score[:, qb, 0:W], work[qb][:, 0:W], NEG, None, ALU.mult).then_inc(S("topk"), 1)
            dve.tensor_copy(score[:, 0, 0:P], causal[:, SEQ - P:SEQ]).then_inc(S("topk"), 1)

            dve.wait_ge(S("k_hi"), 2)
            dve.tensor_tensor(act_lo[:, 3:8:4, 0:SEQ], yC[:, 6:8, 0:SEQ], act_hi[:, 3:8:4, 0:SEQ].bitcast(F32),
                              ALU.subtract).then_inc(S("k_split"), 1)
            for n in range(2):
                dve.wait_ge(S("C_vt"), n + 1)
                dve.tensor_copy(vtokC[:, 2 * n:2 * n + 2, :],
                                PS[:, 4 + n, :].rearrange("p (k d) -> p k d", k=2)).then_inc(S("C_vtc"), 1)
            dve.wait_ge(S("hn_ok"), 19 + 2)
            for T in range(2):
                for r in range(2):
                    rows = slice(HD * r, HD * r + HD)
                    cols = qzC[rows, T * NS:(T + 1) * NS, :].rearrange("p b c -> p (b c)")
                    for t in range(4 * T, 4 * T + 4):
                        c0 = 64 * r + NS * t
                        ins = dve.tensor_copy(cols[:, c0:c0 + 7 * 129 + 1:129], yC[rows, 10 + t, SEQ:NT])
                    ins.then_inc(S("d_qz"), 1)

            dve.wait_ge(S("d_a"), NS)
            then(dve.tensor_copy(sc8[:], PS[0:NS, 7, 0:NK]))
            top([(sc8[:], wk8[:], mx8[:])], TOPK_S)
            dve.tensor_scalar(sc8[:], wk8[:], NEG, None, ALU.mult).then_inc(S("d_mask"), 1)

            def bias_c(it, i, W):
                dve.wait_ge(S("C_bm"), it * NU + (bias_c.base + i + 1))
                return bmC[:, i % 2, 0:W]
            for T in range(2):
                bias_c.base = 32 * T
                attention(2, 32 * (T + 1), 4 * T, xC, pC, statC, bias_c)
                if T == 0:
                    for b in range(4, NS):
                        dve.wait_ge(S("s_ks"), NS + b - 3)
                        dve.tensor_copy(kcC[:, b % 4, :, PAST], yC[:, 6:8, SEQ + b]).then_inc(S("s_kn"), 1)
                    dve.wait_ge(S("s_ks"), 2 * NS)
                    softmax(1, PS[:, 6, 0:NK], psC, sstC)
                    dve.tensor_scalar(pdC[:], ident, psC[:, PAST:NK], None, ALU.mult).then_inc(S("d_pd"), 1)

            dve.wait_ge(S("d_vt"), 1)
            dve.tensor_copy(vnC[:], PS[0:NS, 6, 0:256]).then_inc(S("d_vtc"), 1)
            dve.wait_ge(S("d_pn"), 1)
            dve.tensor_copy(pnC[:], PS[0:NS, 6, 256:256 + P]).then_inc(S("d_pnc"), 1)
            dve.wait_ge(S("d_o"), 1)
            for T in range(2):
                for r in range(2):
                    rows = slice(HD * r, HD * r + HD)
                    src = PS[rows, 4, 64 * T:64 * T + 64].rearrange("p (r t b) -> p r t b", r=2, t=4)[:, r]
                    then(dve.tensor_copy(owC[rows, 4 * T:4 * T + 4, :], src))
                    src = PS[rows, 7, 2 * P:3 * P].rearrange("p (b T r t) -> p T r t b", b=NS, T=2, r=2)[:, T, r]
                    dve.tensor_tensor(osC[rows, 4 * T:4 * T + 4, :], src, owC[rows, 4 * T:4 * T + 4, :],
                                      ALU.add).then_inc(S("d_os"), 1)
            dve.wait_ge(S("d_oh"), 1)
            dve.tensor_tensor(act_lo[:, :, SEQ:NT], osC[:], act_hi[:, :, SEQ:NT].bitcast(F32),
                              ALU.subtract).then_inc(S("mix_lo"), 1)
            ffn(1)


def bucket(dist):
    n = np.maximum(dist, 0)
    exact = NB // 2
    nf = np.maximum(n, exact).astype(np.float32)
    large = exact + (np.log(nf / np.float32(exact)) / np.float32(math.log(2048 / exact))
                     * np.float32(exact)).astype(np.int32)
    return np.where(n < exact, n, np.minimum(large, NB - 1))


def one_hots():
    def columns(dist, dilated):
        out = np.zeros((NB + 1, len(dist)), np.float32)
        out[bucket(dist), np.arange(len(dist))] = 1
        if dilated:
            count = sum(((dist >= 0) & (dist <= w) & (dist % d == 0)).astype(int)
                        for w, d in ((128, 1), (512, 4), (2048, 16)))
            out[NB] = np.where(count > 0, np.log(np.maximum(count, 1)), NEG)
        return out
    by_row, by_key = SEQ - 1 - np.arange(RW), PAST - np.arange(NK)
    return np.concatenate([columns(by_row, True), columns(by_row, False),
                           columns(by_key, True), columns(by_key, False)], axis=1)


def constants():
    c = np.zeros((P, NKC), np.float32)
    p = np.arange(P)
    c[:, K_ID:K_ID + P] = np.eye(P)
    c[:, K_O2:K_O2 + P] = p[:, None] // HD == p[None, :] // HD
    c[:, K_ON:K_ON + P] = 1
    c[:, K_CA:K_CA + SEQ] = np.where(np.arange(SEQ)[None, :] - (SEQ - P) <= p[:, None], 0.0, NEG)
    c[:, K_FR:K_FR + SEQ] = np.arange(SEQ) % GC != 0
    c[:, K_TR:K_TR + GC] = p[:, None] % GC <= np.arange(GC)[None, :]
    c[:, K_RS:K_RS + NS] = p[:, None] % NS == np.arange(NS)[None, :]
    return c


def features(t):
    return t.T.reshape(-1, P, t.shape[0]).transpose(1, 0, 2)


C_ORDER = [4 * (2 * (t // 4) + r) + t % 4 for t in range(8) for r in range(2)]


def kernel(**inputs):
    import concourse.bacc as _bacc
    from concourse.bass_utils import run_bass_kernel_spmd as _run

    i = {k: np.asarray(v) for k, v in inputs.items()}
    f32 = np.float32

    def blocks(w):
        k, m = w.shape
        pad = np.zeros((k, -m % P), f32)
        w = np.concatenate([w, pad], axis=1)
        return w.reshape(k // P, P, -1, P).transpose(2, 1, 0, 3).reshape(-1, P, k)

    w_ab, w_c = i["w_in_ab"][0], i["w_in_c"][0]
    rank = np.concatenate([w_ab[:, 2560:2576], np.zeros((DM, P - 16), f32)], axis=1)
    ab = np.concatenate([rank, w_ab[:, 1536:2560], w_ab[:, 1024:1536], w_ab[:, 2576:3088],
                         w_ab[:, 0:1024]], axis=1)
    cq = w_c[:, 0:1024].reshape(DM, 16, HD)[:, C_ORDER].reshape(DM, 1024)
    ik = w_c[:, 2048:2112]
    iw = np.concatenate([w_c[:, 2112:2120], np.zeros((DM, P - NS), f32)], axis=1)
    c = np.concatenate([w_c[:, 1536:2048], ik, ik, iw, w_c[:, 1024:1536], cq], axis=1)
    out_c = i["w_out_c"][0].reshape(16, HD, DM)[C_ORDER].reshape(1024, DM)
    stream = []
    for l, parts in ((0, (ab, i["w_out_ab"][0])), (1, (c, out_c))):
        stream += [blocks(w) for w in parts]
        up = np.stack([blocks(i["w_ff1"][l]), blocks(i["w_ff3"][l])], axis=1)
        down = np.concatenate([i["w_ff2"][l], np.zeros((3 * DM - DFF, DM), f32)], axis=0)
        stream += [up.reshape(-1, P, DM),
                   blocks(down).reshape(KC, P, 3, DM).transpose(0, 2, 1, 3).reshape(-1, P, DM),
                   blocks(i["w_ple_proj"][l]).reshape(2, 4, P, 256).transpose(0, 2, 1, 3).reshape(2, P, DM),
                   blocks(i["w_ple_gate"][l])]
    stream.append(np.zeros((2, P, DM), f32))
    w = np.concatenate(stream, axis=0)

    def both(v):
        return np.concatenate([v, v])[:, None]

    by_chunk = [i[n][l].reshape(KC, P).T for n in ("g_mix", "g_ffn", "g_ple") for l in range(2)]
    norms = ([both(i["a_q_norm"][0])] * 4 + [both(i["a_k_norm"][0])] * 4 + [both(i["c_ik_norm"][0])]
             + [both(i["c_k_norm"][0])] * 2 + [both(i["c_q_norm"][0])] * 8)
    vecs = np.concatenate(by_chunk + norms + [
        i["b_out_norm"][0][:, None], i["b_gate_b"][0].reshape(2, P).T, np.full((P, 1), EPS, f32),
        np.ones((P, 1), f32)], axis=1)

    rel = i["rel_bias"]
    a_rows = [2 * (r // NS % 4) + r // 32 for r in range(64)]
    c_rows = [C_ORDER[2 * (r // NS % 8) + r // 64] for r in range(P)]
    bias = np.concatenate([rel[:, 0:8], rel, rel[:, a_rows], rel[:, c_rows]], axis=1)
    bias = np.concatenate([bias, np.ones((1, bias.shape[1]), f32)], axis=0)

    k_cache = i["cache_a_k"][0].reshape(NS, PAST, 4, P).transpose(0, 3, 2, 1)
    v_cache = i["cache_a_v"][0].reshape(NS, 2, P, 512).transpose(0, 2, 1, 3)
    state = i["state_b"][0].reshape(NS, 2, P, P).transpose(2, 0, 1, 3)
    arrays = {
        "w": w,
        "xT": features(np.concatenate([i["x_prompt"][0], i["x_sample"][:, 0]], axis=0)),
        "pT": np.stack([features(np.concatenate([i["p_prompt"][l, 0], i["p_sample"][l, :, 0]], axis=0))
                        for l in range(2)]),
        "consts": constants(),
        "colsel": constants()[:, K_RS:K_RS + NS].T,
        "vecs": vecs,
        "gate_w2": i["b_gate_w2"][0],
        "bias_rows": bias,
        "onehots": one_hots(),
        "cache_k": k_cache,
        "cache_v": v_cache,
        "state": state,
        "pool_k": i["cache_c_k"][0].reshape(-1, P, 2, P).transpose(0, 3, 2, 1),
        "pool_v": i["cache_c_v"][0].reshape(-1, P, 256),
        "pool_ik": i["cache_c_ik"][0].transpose(0, 2, 1),
        "pages": i["page_table"].reshape(1, 16),
    }
    arrays = {k: np.ascontiguousarray(v) for k, v in arrays.items()}
    outs = {"y": (P, KC, NT), "a_k": (P, 4, NT), "a_v": (P, 4, NT), "b_state": (P, 2, P),
            "s_state": (P, NS, 2, P), "c_k": (P, 2, NT), "c_v": (P, 2, NT), "c_ik": (HD, NT)}

    nc = _bacc.Bacc("TRN2", target_bir_lowering=False, num_devices=1)
    tensors = {k: nc.dram_tensor("in_" + k, v.shape, mybir.dt.from_np(v.dtype), kind="ExternalInput").ap()
               for k, v in arrays.items()}
    for k, shape in outs.items():
        tensors[k] = nc.dram_tensor("out_" + k, shape, F32, kind="ExternalOutput").ap()
    tensors["rows"] = nc.dram_tensor("scratch_rows", (24, 2, RW), F32, kind="Internal").ap()
    build(nc, tensors)
    r = _run(nc, [{"in_" + k: v for k, v in arrays.items()}], core_ids=[0]).results[0]

    def tokens(t):
        t = t.transpose(1, 0, 2).reshape(-1, t.shape[2])
        return t[:, 0:SEQ].T, t[:, SEQ:NT].T

    (yp, ys), (ak, sak), (av, sav) = tokens(r["out_y"]), tokens(r["out_a_k"]), tokens(r["out_a_v"])
    (ck, sck), (cv, scv) = tokens(r["out_c_k"]), tokens(r["out_c_v"])
    cik, scik = r["out_c_ik"][:, 0:SEQ].T, r["out_c_ik"][:, SEQ:NT].T
    return (yp[None], ys[:, None],
            ak.reshape(1, 1, SEQ, 8, HD), av.reshape(1, 1, SEQ, 8, HD),
            r["out_b_state"].transpose(1, 0, 2).reshape(1, 1, 4, HD, P),
            ck.reshape(1, 1, SEQ, 4, HD), cv.reshape(1, 1, SEQ, 4, HD), cik.reshape(1, 1, SEQ, HD),
            sak.reshape(1, NS, 1, 8, HD), sav.reshape(1, NS, 1, 8, HD),
            r["out_s_state"].transpose(1, 2, 0, 3).reshape(1, NS, 4, HD, P),
            sck.reshape(1, NS, 1, 4, HD), scv.reshape(1, NS, 1, 4, HD), scik.reshape(1, NS, 1, HD))
```
